# Optimizing a Trainium2 kernel written in Bass

```python
import numpy as np
import jax
import jax.numpy as jnp
from jax import lax
import math

D_MODEL = 1024
BATCH = 1
SEQ = 256
DEPTH = 2

PLE_DIM = 256
N_HEADS = 16
HEAD_DIM = 64
ATT_DIM = N_HEADS * HEAD_DIM
NSA_KV_HEADS = 4
NSA_KV_DIM = NSA_KV_HEADS * HEAD_DIM
CMP_BLOCK = 32
CMP_STRIDE = 16
CMP_HIDDEN = 256
SEL_BLOCK = 64
SEL_TOPN = 16
WINDOW = 512
NSA_Q_BLOCK = 64
NSA_PROJ = ATT_DIM + 6 * NSA_KV_DIM + 3 * N_HEADS
MOBA_KV_HEADS = 4
MOBA_KV_DIM = MOBA_KV_HEADS * HEAD_DIM
MOBA_BLOCK = 256
MOBA_TOPK = 3
MOBA_Q_BLOCK = 16
N_GROUPS = 4
EXPERTS_PER_GROUP = 8
N_EXPERTS = N_GROUPS * EXPERTS_PER_GROUP
TOPK_IN_GROUP = 2
D_EXPERT = 128
NORM_EPS = 1e-6
FORCED_SCORE = 1e9


def rms_norm(x, g):
    xf = x.astype(jnp.float32)
    y = xf * lax.rsqrt(jnp.mean(xf * xf, axis=-1, keepdims=True) + NORM_EPS)
    return (y * g.astype(jnp.float32)).astype(x.dtype)

def to_heads(t, n_heads):
    b, s = t.shape[0], t.shape[1]
    return t.reshape(b, s, n_heads, HEAD_DIM).transpose(0, 2, 1, 3)

def alibi_slopes(n_heads):
    return jnp.asarray(2.0 ** (-8.0 * np.arange(1, n_heads + 1) / n_heads), dtype=jnp.float32)

def masked_softmax(s, mask, axis=-1):
    s = jnp.where(mask, s, -jnp.inf)
    m = jnp.max(s, axis=axis, keepdims=True)
    m = jnp.where(jnp.isfinite(m), m, 0.0)
    e = jnp.exp(s - m)
    return e / jnp.maximum(jnp.sum(e, axis=axis, keepdims=True), 1e-30)

def compress_blocks(k, pos, w1, w2):
    b, g, s, d = k.shape
    n_cmp = (s - CMP_BLOCK) // CMP_STRIDE + 1
    idx = np.arange(n_cmp)[:, None] * CMP_STRIDE + np.arange(CMP_BLOCK)[None, :]
    blk = (k[:, :, idx] + pos).reshape(b, g, n_cmp, CMP_BLOCK * d)
    return jax.nn.gelu(blk @ w1) @ w2

def cmp_sel_overlap(n_cmp, n_sel):
    c0 = np.arange(n_cmp)[:, None] * CMP_STRIDE
    s0 = np.arange(n_sel)[None, :] * SEL_BLOCK
    ov = np.clip(np.minimum(c0 + CMP_BLOCK, s0 + SEL_BLOCK) - np.maximum(c0, s0), 0, None)
    return jnp.asarray(ov / CMP_BLOCK, dtype=jnp.float32)

def nsa_attention(xn, w_in, q_gain, k_gain, ck_pos, ck_w1, ck_w2, cv_pos, cv_w1, cv_w2, w_out):
    b, s, _ = xn.shape
    g, r = NSA_KV_HEADS, N_HEADS // NSA_KV_HEADS
    splits = np.cumsum([ATT_DIM] + [NSA_KV_DIM] * 6).tolist()
    q, kc, vc, ks, vs, kw, vw, gl = jnp.split(xn @ w_in, splits, axis=-1)
    q = (rms_norm(to_heads(q, N_HEADS), q_gain) * HEAD_DIM ** -0.5).reshape(b, g, r, s, HEAD_DIM)
    kc = rms_norm(compress_blocks(to_heads(kc, g), ck_pos, ck_w1, ck_w2), k_gain[0])
    vc = compress_blocks(to_heads(vc, g), cv_pos, cv_w1, cv_w2)
    n_cmp = kc.shape[2]
    n_sel = s // SEL_BLOCK
    n_top = min(SEL_TOPN, n_sel)
    ks = rms_norm(to_heads(ks, g), k_gain[1]).reshape(b, g, n_sel, SEL_BLOCK, HEAD_DIM)
    vs = to_heads(vs, g).reshape(b, g, n_sel, SEL_BLOCK, HEAD_DIM)
    pad = ((0, 0), (0, 0), (WINDOW, 0), (0, 0))
    kw = jnp.pad(rms_norm(to_heads(kw, g), k_gain[2]), pad)
    vw = jnp.pad(to_heads(vw, g), pad)
    gates = jax.nn.sigmoid(gl).reshape(b, s, N_HEADS, 3).transpose(0, 2, 1, 3).reshape(b, g, r, s, 3)
    slopes = alibi_slopes(N_HEADS).reshape(1, g, r, 1, 1)
    cmp_end = jnp.arange(n_cmp) * CMP_STRIDE + (CMP_BLOCK - 1)
    overlap = cmp_sel_overlap(n_cmp, n_sel)
    blk_ids = jnp.arange(n_sel)
    bi = jnp.arange(b)[:, None, None, None]
    gi = jnp.arange(g)[None, :, None, None]

    def query_block(c):
        start = c * NSA_Q_BLOCK
        t = start + jnp.arange(NSA_Q_BLOCK)
        qc = lax.dynamic_slice_in_dim(q, start, NSA_Q_BLOCK, axis=3)
        gc = lax.dynamic_slice_in_dim(gates, start, NSA_Q_BLOCK, axis=3)
        dist_c = (t[:, None] - cmp_end[None, :]).astype(jnp.float32)
        s_c = jnp.einsum('bgrqd,bgnd->bgrqn', qc, kc).astype(jnp.float32) - slopes * dist_c
        p_c = masked_softmax(s_c, dist_c >= 0)
        o_c = jnp.einsum('bgrqn,bgnd->bgrqd', p_c.astype(vc.dtype), vc)
        imp = jnp.einsum('bgrqn,nj->bgqj', p_c, overlap)
        cur = (t // SEL_BLOCK)[:, None]
        forced = (blk_ids == 0) | (blk_ids == cur) | (blk_ids == cur - 1)
        imp = jnp.where(blk_ids <= cur, jnp.where(forced, FORCED_SCORE, imp), -jnp.inf)
        _, sel = lax.top_k(imp, n_top)
        k_g = ks[bi, gi, sel]
        v_g = vs[bi, gi, sel]
        pos = sel[..., None] * SEL_BLOCK + jnp.arange(SEL_BLOCK)
        dist_s = (t[:, None, None] - pos)[:, :, None].astype(jnp.float32)
        s_s = jnp.einsum('bgrqd,bgqnld->bgrqnl', qc, k_g).astype(jnp.float32) - slopes[..., None] * dist_s
        p_s = masked_softmax(s_s, dist_s >= 0, axis=(-2, -1))
        o_s = jnp.einsum('bgrqnl,bgqnld->bgrqd', p_s.astype(v_g.dtype), v_g)
        kwc = lax.dynamic_slice_in_dim(kw, start, NSA_Q_BLOCK + WINDOW, axis=2)
        vwc = lax.dynamic_slice_in_dim(vw, start, NSA_Q_BLOCK + WINDOW, axis=2)
        kp = start - WINDOW + jnp.arange(NSA_Q_BLOCK + WINDOW)
        dist_w = t[:, None] - kp[None, :]
        s_w = jnp.einsum('bgrqd,bgkd->bgrqk', qc, kwc).astype(jnp.float32) - slopes * dist_w.astype(jnp.float32)
        p_w = masked_softmax(s_w, (dist_w >= 0) & (dist_w < WINDOW) & (kp[None, :] >= 0))
        o_w = jnp.einsum('bgrqk,bgkd->bgrqd', p_w.astype(vwc.dtype), vwc)
        o = gc[..., 0:1] * o_c + gc[..., 1:2] * o_s + gc[..., 2:3] * o_w
        return o.transpose(0, 3, 1, 2, 4).reshape(b, NSA_Q_BLOCK, ATT_DIM)

    o = lax.map(query_block, jnp.arange(s // NSA_Q_BLOCK))
    o = o.transpose(1, 0, 2, 3).reshape(b, s, ATT_DIM)
    return o @ w_out

def shared_kv(h, kv_norm, w_kv, k_gain):
    b, s, _ = h.shape
    k, v = jnp.split(rms_norm(h, kv_norm) @ w_kv, 2, axis=-1)
    k = rms_norm(to_heads(k, MOBA_KV_HEADS), k_gain)
    v = to_heads(v, MOBA_KV_HEADS)
    nb = -(-s // MOBA_BLOCK)
    pad = ((0, 0), (0, 0), (0, nb * MOBA_BLOCK - s), (0, 0))
    kb = jnp.pad(k, pad).reshape(b, MOBA_KV_HEADS, nb, MOBA_BLOCK, HEAD_DIM)
    vb = jnp.pad(v, pad).reshape(b, MOBA_KV_HEADS, nb, MOBA_BLOCK, HEAD_DIM)
    km = jnp.mean(kb.astype(jnp.float32), axis=3).astype(kb.dtype)
    return kb, vb, km

def moba_attention(xn, kb, vb, km, w_q, q_gain, w_out):
    b, s, _ = xn.shape
    g, r = MOBA_KV_HEADS, N_HEADS // MOBA_KV_HEADS
    q = (rms_norm(to_heads(xn @ w_q, N_HEADS), q_gain) * HEAD_DIM ** -0.5).reshape(b, g, r, s, HEAD_DIM)
    nb = kb.shape[2]
    ktop = min(MOBA_TOPK, nb)
    slopes = alibi_slopes(N_HEADS).reshape(1, g, r, 1, 1)
    bi = jnp.arange(b)[:, None, None, None, None]
    gi = jnp.arange(g)[None, :, None, None, None]
    blk_ids = jnp.arange(nb)
    offs = jnp.arange(MOBA_BLOCK)

    def query_block(c):
        start = c * MOBA_Q_BLOCK
        t = start + jnp.arange(MOBA_Q_BLOCK)
        cb = start // MOBA_BLOCK
        qc = lax.dynamic_slice_in_dim(q, start, MOBA_Q_BLOCK, axis=3)
        sg = jnp.einsum('bgrqd,bgnd->bgrqn', qc, km).astype(jnp.float32)
        sg = jnp.where(blk_ids < cb, sg, -jnp.inf)
        _, idx = lax.top_k(sg, ktop)
        k_g = kb[bi, gi, idx]
        v_g = vb[bi, gi, idx]
        pos = idx[..., None] * MOBA_BLOCK + offs
        dist = (t[:, None, None] - pos).astype(jnp.float32)
        s_sel = jnp.einsum('bgrqd,bgrqkld->bgrqkl', qc, k_g).astype(jnp.float32)
        s_sel = jnp.where((idx < cb)[..., None], s_sel - slopes[..., None] * dist, -jnp.inf)
        ko = lax.dynamic_index_in_dim(kb, cb, axis=2, keepdims=False)
        vo = lax.dynamic_index_in_dim(vb, cb, axis=2, keepdims=False)
        dist_o = t[:, None] - (cb * MOBA_BLOCK + offs)[None, :]
        s_own = jnp.einsum('bgrqd,bgld->bgrql', qc, ko).astype(jnp.float32)
        s_own = jnp.where(dist_o >= 0, s_own - slopes * dist_o.astype(jnp.float32), -jnp.inf)
        n_sel_keys = ktop * MOBA_BLOCK
        sc = jnp.concatenate([s_sel.reshape(b, g, r, MOBA_Q_BLOCK, n_sel_keys), s_own], axis=-1)
        pr = jax.nn.softmax(sc, axis=-1)
        p_sel = pr[..., :n_sel_keys].reshape(s_sel.shape).astype(vb.dtype)
        p_own = pr[..., n_sel_keys:].astype(vb.dtype)
        o = (jnp.einsum('bgrqkl,bgrqkld->bgrqd', p_sel, v_g)
             + jnp.einsum('bgrql,bgld->bgrqd', p_own, vo))
        return o.transpose(0, 3, 1, 2, 4).reshape(b, MOBA_Q_BLOCK, ATT_DIM)

    o = lax.map(query_block, jnp.arange(s // MOBA_Q_BLOCK))
    o = o.transpose(1, 0, 2, 3).reshape(b, s, ATT_DIM)
    return o @ w_out

def hier_moe(xn, w_group, b_group, w_expert, b_expert, w_gate, w_up, w_down):
    b, s, d = xn.shape
    xt = xn.reshape(b * s, d)
    g_prob = jax.nn.softmax((xt @ w_group + b_group).astype(jnp.float32), axis=-1)
    g_w, g_idx = lax.top_k(g_prob, 1)
    e_logits = (xt @ w_expert + b_expert).astype(jnp.float32).reshape(-1, N_GROUPS, EXPERTS_PER_GROUP)
    e_logits = jnp.einsum('tge,tg->te', e_logits, jax.nn.one_hot(g_idx[:, 0], N_GROUPS, dtype=jnp.float32))
    e_prob = jax.nn.softmax(e_logits, axis=-1)
    e_w, e_idx = lax.top_k(e_prob, TOPK_IN_GROUP)
    e_w = e_w / jnp.sum(e_w, axis=-1, keepdims=True)
    comb = g_w * e_w
    expert_id = g_idx * EXPERTS_PER_GROUP + e_idx
    cw = jnp.einsum('tk,tke->te', comb, jax.nn.one_hot(expert_id, N_EXPERTS, dtype=jnp.float32)).astype(xt.dtype)
    hid = jax.nn.silu(jnp.einsum('td,edf->tef', xt, w_gate)) * jnp.einsum('td,edf->tef', xt, w_up)
    y = jnp.einsum('tef,efd->td', hid * cw[:, :, None], w_down)
    return y.reshape(b, s, d)

def first_inputs(seed: int = 0) -> dict:
    key = jax.random.key(seed)
    keys = iter(jax.random.split(key, 40))

    def nrm(shape, scale):
        return jax.random.normal(next(keys), shape, jnp.float32) * scale

    def gain(shape):
        return 1.0 + 0.05 * jax.random.normal(next(keys), shape, jnp.float32)

    n_a = (DEPTH + 1) // 2
    n_b = DEPTH - n_a
    cmp_in = CMP_BLOCK * HEAD_DIM
    return {
        'x': nrm((BATCH, SEQ, D_MODEL), 1.0),
        'p': nrm((DEPTH, BATCH, SEQ, PLE_DIM), 1.0),
        'ln_mix': gain((DEPTH, D_MODEL)),
        'ln_ffn': gain((DEPTH, D_MODEL)),
        'ln_ple': gain((DEPTH, D_MODEL)),
        'a_w_in': nrm((n_a, D_MODEL, NSA_PROJ), D_MODEL ** -0.5),
        'a_q_norm': gain((n_a, HEAD_DIM)),
        'a_k_norm': gain((n_a, 3, HEAD_DIM)),
        'a_ck_pos': nrm((n_a, CMP_BLOCK, HEAD_DIM), 0.1),
        'a_ck_w1': nrm((n_a, cmp_in, CMP_HIDDEN), cmp_in ** -0.5),
        'a_ck_w2': nrm((n_a, CMP_HIDDEN, HEAD_DIM), CMP_HIDDEN ** -0.5),
        'a_cv_pos': nrm((n_a, CMP_BLOCK, HEAD_DIM), 0.1),
        'a_cv_w1': nrm((n_a, cmp_in, CMP_HIDDEN), cmp_in ** -0.5),
        'a_cv_w2': nrm((n_a, CMP_HIDDEN, HEAD_DIM), CMP_HIDDEN ** -0.5),
        'a_w_out': nrm((n_a, ATT_DIM, D_MODEL), ATT_DIM ** -0.5),
        'kv_norm': gain((D_MODEL,)),
        'w_kv_shared': nrm((D_MODEL, 2 * MOBA_KV_DIM), D_MODEL ** -0.5),
        'k_norm_shared': gain((HEAD_DIM,)),
        'b_w_q': nrm((n_b, D_MODEL, ATT_DIM), D_MODEL ** -0.5),
        'b_q_norm': gain((n_b, HEAD_DIM)),
        'b_w_out': nrm((n_b, ATT_DIM, D_MODEL), ATT_DIM ** -0.5),
        'moe_w_group': nrm((DEPTH, D_MODEL, N_GROUPS), D_MODEL ** -0.5),
        'moe_b_group': nrm((DEPTH, N_GROUPS), 0.01),
        'moe_w_expert': nrm((DEPTH, D_MODEL, N_EXPERTS), D_MODEL ** -0.5),
        'moe_b_expert': nrm((DEPTH, N_EXPERTS), 0.01),
        'moe_w_gate': nrm((DEPTH, N_EXPERTS, D_MODEL, D_EXPERT), D_MODEL ** -0.5),
        'moe_w_up': nrm((DEPTH, N_EXPERTS, D_MODEL, D_EXPERT), D_MODEL ** -0.5),
        'moe_w_down': nrm((DEPTH, N_EXPERTS, D_EXPERT, D_MODEL), D_EXPERT ** -0.5),
        'ple_w_proj': nrm((DEPTH, PLE_DIM, D_MODEL), PLE_DIM ** -0.5),
        'ple_w_gate': nrm((DEPTH, D_MODEL, D_MODEL), D_MODEL ** -0.5),
    }

def first_block(x, p, ln_mix, ln_ffn, ln_ple, a_w_in, a_q_norm, a_k_norm, a_ck_pos, a_ck_w1, a_ck_w2,
              a_cv_pos, a_cv_w1, a_cv_w2, a_w_out, kv_norm, w_kv_shared, k_norm_shared, b_w_q, b_q_norm,
              b_w_out, moe_w_group, moe_b_group, moe_w_expert, moe_b_expert, moe_w_gate, moe_w_up,
              moe_w_down, ple_w_proj, ple_w_gate):
    n_a = (DEPTH + 1) // 2
    h = x
    kb = vb = km = None
    for i in range(DEPTH):
        xn = rms_norm(h, ln_mix[i])
        if i < n_a:
            mix = nsa_attention(xn, a_w_in[i], a_q_norm[i], a_k_norm[i], a_ck_pos[i], a_ck_w1[i], a_ck_w2[i],
                                a_cv_pos[i], a_cv_w1[i], a_cv_w2[i], a_w_out[i])
        else:
            if i == n_a:
                kb, vb, km = shared_kv(h, kv_norm, w_kv_shared, k_norm_shared)
            j = i - n_a
            mix = moba_attention(xn, kb, vb, km, b_w_q[j], b_q_norm[j], b_w_out[j])
        h = h + mix.astype(h.dtype)
        h = h + hier_moe(rms_norm(h, ln_ffn[i]), moe_w_group[i], moe_b_group[i], moe_w_expert[i],
                         moe_b_expert[i], moe_w_gate[i], moe_w_up[i], moe_w_down[i]).astype(h.dtype)
        gate = jax.nn.sigmoid(rms_norm(h, ln_ple[i]) @ ple_w_gate[i])
        h = h + (gate * (p[i] @ ple_w_proj[i])).astype(h.dtype)
    return h


DEPTH_2 = 4

N_MIXERS = 3
N_SUB = 3
D_FF = 2816
MACARON_W = 0.5
N_A = (DEPTH_2 + 2) // 3
N_B = (DEPTH_2 + 1) // 3
N_C = DEPTH_2 // 3
N_A_VRES = max(N_A - 1, 0)

RW_HEAD = 64
RW_HEADS = D_MODEL // RW_HEAD
RW_DECAY_LORA = max(32, int(round(1.8 * D_MODEL ** 0.5 / 32)) * 32)
RW_AAA_LORA = max(32, int(round(1.8 * D_MODEL ** 0.5 / 32)) * 32)
RW_MV_LORA = max(32, int(round(1.3 * D_MODEL ** 0.5 / 32)) * 32)
RW_GATE_LORA = max(32, int(round(0.6 * D_MODEL ** 0.8 / 32)) * 32)
RW_GN_EPS = 64e-5

MB_D_INNER = 2 * D_MODEL
MB_HEADDIM = 64
MB_HEADS = MB_D_INNER // MB_HEADDIM
MB_GROUPS = 8
MB_STATE = 128
MB_CONV = 4
MB_CHUNK = 128
MB_CONV_DIM = MB_D_INNER + 2 * MB_GROUPS * MB_STATE
MB_IN_DIM = MB_D_INNER + MB_CONV_DIM + MB_HEADS

SW_HEAD_DIM = 64
SW_Q_HEADS = D_MODEL // SW_HEAD_DIM
SW_KV_HEADS = 4
SW_WINDOW = 128
SW_BLOCK = 128
NEG_INF = -1e30


def rms_norm_2(x, g, eps=NORM_EPS):
    xf = x.astype(jnp.float32)
    y = xf * lax.rsqrt(jnp.mean(xf * xf, axis=-1, keepdims=True) + eps)
    return (y * g.astype(jnp.float32)).astype(x.dtype)

def adaln(x, g, shift, scale):
    return rms_norm_2(x, g) * (1 + scale[:, None, :]) + shift[:, None, :]

def swiglu(h, w_in, w_out):
    a, b = jnp.split(h @ w_in, 2, axis=-1)
    return (jax.nn.silu(a) * b) @ w_out

def token_shift(h):
    return jnp.pad(h, ((0, 0), (1, 0), (0, 0)))[:, :-1]

def rwkv7_time_mix(h, mu, w_rkv, w_o, w0, w1, w2, a0, a1, a2, g1, g2,
                   k_k, k_a, r_k, ln_w, ln_b, v_first, vres):
    f32 = jnp.float32
    bsz, seq, d = h.shape
    H, N = RW_HEADS, RW_HEAD
    dx = token_shift(h) - h
    xr, xw, xk, xv, xa, xg = [h + dx * mu[j] for j in range(6)]
    r = xr @ w_rkv[0]
    k = xk @ w_rkv[1]
    v = xv @ w_rkv[2]
    w = -jax.nn.softplus(-(w0 + jnp.tanh(xw @ w1) @ w2)) - 0.5
    decay = jnp.exp(-jnp.exp(w.astype(f32)))
    a = jax.nn.sigmoid(a0 + (xa @ a1) @ a2)
    if vres is None:
        v_first = v
    else:
        v0, v1, v2 = vres
        v = v + (v_first - v) * jax.nn.sigmoid(v0 + (xv @ v1) @ v2)
    g = jax.nn.sigmoid(xg @ g1) @ g2

    def heads(t):
        return t.reshape(bsz, seq, H, N).astype(f32)

    kk = heads(k * k_k)
    kk = kk / jnp.maximum(jnp.sqrt(jnp.sum(kk * kk, axis=-1, keepdims=True)), 1e-12)
    k = k * (1 + (a - 1) * k_a)
    rh, kh, vh, wh, ah = heads(r), heads(k), heads(v), heads(decay), heads(a)

    def step(state, inp):
        r_t, w_t, k_t, v_t, kk_t, a_t = inp
        sa = jnp.einsum('bhvk,bhk->bhv', state, -kk_t)
        state = (state * w_t[:, :, None, :]
                 + sa[..., None] * (kk_t * a_t)[:, :, None, :]
                 + v_t[..., None] * k_t[:, :, None, :])
        return state, jnp.einsum('bhvk,bhk->bhv', state, r_t)

    def tm(t):
        return jnp.swapaxes(t, 0, 1)

    state0 = jnp.zeros((bsz, H, N, N), f32)
    _, y = lax.scan(step, state0, (tm(rh), tm(wh), tm(kh), tm(vh), tm(kk), tm(ah)))
    y = tm(y)
    mean = jnp.mean(y, axis=-1, keepdims=True)
    var = jnp.mean(jnp.square(y - mean), axis=-1, keepdims=True)
    y = ((y - mean) * lax.rsqrt(var + RW_GN_EPS)).reshape(bsz, seq, d) * ln_w + ln_b
    bonus = jnp.sum(rh * kh * r_k, axis=-1, keepdims=True) * vh
    out = ((y + bonus.reshape(bsz, seq, d)) * g).astype(h.dtype) @ w_o
    return out, v_first

def causal_dwconv(x, w, b):
    k_w, ch = w.shape
    out = lax.conv_general_dilated(x, w[:, None, :].astype(x.dtype), window_strides=(1,),
                                   padding=[(k_w - 1, 0)],
                                   dimension_numbers=('NWC', 'WIO', 'NWC'),
                                   feature_group_count=ch)
    return out + b

def ssd_chunked(x, dt, A, Bm, Cm):
    f32 = jnp.float32
    bsz, seq, H, P = x.shape
    G, N = Bm.shape[2], Bm.shape[3]
    hg = H // G
    L = MB_CHUNK
    nc = seq // L
    X = (x.astype(f32) * dt[..., None]).reshape(bsz, nc, L, G, hg, P)
    dA = (dt * A).reshape(bsz, nc, L, G, hg)
    Bc = Bm.astype(f32).reshape(bsz, nc, L, G, N)
    Cc = Cm.astype(f32).reshape(bsz, nc, L, G, N)
    X, dA, Bc, Cc = [jnp.moveaxis(t, 1, 0) for t in (X, dA, Bc, Cc)]
    mask = jnp.tril(jnp.ones((L, L), dtype=bool))[None, :, :, None, None]

    def step(state, inp):
        Xc, dAc, Bk, Ck = inp
        acum = jnp.cumsum(dAc, axis=1)
        seg = acum[:, :, None] - acum[:, None, :]
        lmat = jnp.exp(jnp.where(mask, seg, -jnp.inf))
        cb = jnp.einsum('blgn,bsgn->blsg', Ck, Bk)
        y_diag = jnp.einsum('blsgh,bsghp->blghp', cb[..., None] * lmat, Xc)
        y_off = jnp.einsum('blgn,bghpn->blghp', Ck, state) * jnp.exp(acum)[..., None]
        decay_end = jnp.exp(acum[:, -1:] - acum)
        new_state = (state * jnp.exp(acum[:, -1])[..., None, None]
                     + jnp.einsum('blgn,blghp->bghpn', Bk, Xc * decay_end[..., None]))
        return new_state, y_diag + y_off

    state0 = jnp.zeros((bsz, G, hg, P, N), f32)
    _, y = lax.scan(step, state0, (X, dA, Bc, Cc))
    return jnp.moveaxis(y, 0, 1).reshape(bsz, seq, H, P)

def mamba2_ssd_mix(h, w_in, conv_w, conv_b, dt_bias, A_log, D_skip, norm_g, w_out):
    f32 = jnp.float32
    bsz, seq, _ = h.shape
    zxbcdt = h @ w_in
    z, xbc, dt = jnp.split(zxbcdt, [MB_D_INNER, MB_D_INNER + MB_CONV_DIM], axis=-1)
    xbc = jax.nn.silu(causal_dwconv(xbc, conv_w, conv_b))
    xs, Bm, Cm = jnp.split(xbc, [MB_D_INNER, MB_D_INNER + MB_GROUPS * MB_STATE], axis=-1)
    dt = jax.nn.softplus((dt + dt_bias).astype(f32))
    A = -jnp.exp(A_log.astype(f32))
    xs = xs.reshape(bsz, seq, MB_HEADS, MB_HEADDIM)
    y = ssd_chunked(xs, dt, A,
                    Bm.reshape(bsz, seq, MB_GROUPS, MB_STATE),
                    Cm.reshape(bsz, seq, MB_GROUPS, MB_STATE))
    y = y + xs.astype(f32) * D_skip.astype(f32)[:, None]
    y = y.reshape(bsz, seq, MB_D_INNER) * jax.nn.silu(z.astype(f32))
    y = rms_norm_2(y.reshape(bsz, seq, MB_GROUPS, -1), norm_g.reshape(MB_GROUPS, -1))
    return y.reshape(bsz, seq, MB_D_INNER).astype(h.dtype) @ w_out

def swa_sink_attention(h, w_qkv, q_norm, k_norm, sinks, w_o):
    f32 = jnp.float32
    bsz, seq, _ = h.shape
    Hq, Hk, Dh, T = SW_Q_HEADS, SW_KV_HEADS, SW_HEAD_DIM, SW_BLOCK
    G = Hq // Hk
    nb = seq // T
    q, k, v = jnp.split(h @ w_qkv, [Hq * Dh, (Hq + Hk) * Dh], axis=-1)
    q = rms_norm_2(q.reshape(bsz, seq, Hq, Dh), q_norm).reshape(bsz, nb, T, Hk, G, Dh)
    k = rms_norm_2(k.reshape(bsz, seq, Hk, Dh), k_norm).reshape(bsz, nb, T, Hk, Dh)
    v = v.reshape(bsz, nb, T, Hk, Dh)

    def with_prev(t):
        prev = jnp.pad(t, ((0, 0), (1, 0), (0, 0), (0, 0), (0, 0)))[:, :-1]
        return jnp.concatenate([prev, t], axis=2)

    kb, vb = with_prev(k), with_prev(v)
    qi = jnp.arange(T)[:, None]
    si = jnp.arange(2 * T)[None, :]
    rel = qi + T - si
    band = (rel >= 0) & (rel < SW_WINDOW)
    mask = band[None] & ((jnp.arange(nb)[:, None, None] > 0) | (si >= T)[None])
    scale = Dh ** -0.5
    sink = sinks.astype(f32).reshape(Hk, G)[None, :, :, None, None]

    def block(args):
        qb, kbb, vbb, mb = args
        s = jnp.einsum('bqkgd,bskd->bkgqs', qb, kbb).astype(f32) * scale
        s = jnp.where(mb, s, NEG_INF)
        m = jnp.maximum(jnp.max(s, axis=-1, keepdims=True), sink)
        p = jnp.exp(s - m)
        denom = jnp.sum(p, axis=-1, keepdims=True) + jnp.exp(sink - m)
        return jnp.einsum('bkgqs,bskd->bqkgd', (p / denom).astype(vbb.dtype), vbb)

    o = lax.map(block, (jnp.moveaxis(q, 1, 0), jnp.moveaxis(kb, 1, 0),
                        jnp.moveaxis(vb, 1, 0), mask))
    o = jnp.moveaxis(o, 0, 1).reshape(bsz, seq, Hq * Dh)
    return o @ w_o

def second_inputs(seed: int = 0) -> dict:
    key = jax.random.key(seed)
    ks = iter(jax.random.split(key, 64))

    def nrm(shape, scale=1.0):
        return scale * jax.random.normal(next(ks), shape, jnp.float32)

    def unif(shape, lo, hi):
        return jax.random.uniform(next(ks), shape, jnp.float32, lo, hi)

    D = D_MODEL
    dt0 = jnp.exp(unif((N_B, MB_HEADS), math.log(1e-3), math.log(1e-1)))
    return {
        'x': nrm((BATCH, SEQ, D)),
        'c': nrm((BATCH, D)),
        'ada_w': nrm((DEPTH_2, D, N_SUB * 3 * D), 0.5 * D ** -0.5),
        'ada_b': nrm((DEPTH_2, N_SUB * 3 * D), 0.02),
        'norm_g': 1.0 + nrm((DEPTH_2, N_SUB, D), 0.05),
        'ffn_w_in': nrm((DEPTH_2, 2, D, 2 * D_FF), D ** -0.5),
        'ffn_w_out': nrm((DEPTH_2, 2, D_FF, D), D_FF ** -0.5),
        'rw_mu': unif((N_A, 6, D), 0.0, 1.0),
        'rw_w_rkv': nrm((N_A, 3, D, D), D ** -0.5),
        'rw_w_o': nrm((N_A, D, D), D ** -0.5),
        'rw_w0': unif((N_A, D), -6.5, -1.5),
        'rw_w1': nrm((N_A, D, RW_DECAY_LORA), D ** -0.5),
        'rw_w2': nrm((N_A, RW_DECAY_LORA, D), 0.1 * RW_DECAY_LORA ** -0.5),
        'rw_a0': nrm((N_A, D), 0.1),
        'rw_a1': nrm((N_A, D, RW_AAA_LORA), D ** -0.5),
        'rw_a2': nrm((N_A, RW_AAA_LORA, D), 0.5 * RW_AAA_LORA ** -0.5),
        'rw_g1': nrm((N_A, D, RW_GATE_LORA), D ** -0.5),
        'rw_g2': nrm((N_A, RW_GATE_LORA, D), RW_GATE_LORA ** -0.5),
        'rw_k_k': 0.85 + nrm((N_A, D), 0.05),
        'rw_k_a': 1.0 + nrm((N_A, D), 0.05),
        'rw_r_k': nrm((N_A, RW_HEADS, RW_HEAD), 0.1),
        'rw_ln_w': 1.0 + nrm((N_A, D), 0.05),
        'rw_ln_b': nrm((N_A, D), 0.02),
        'rw_v0': 1.0 + nrm((N_A_VRES, D), 0.1),
        'rw_v1': nrm((N_A_VRES, D, RW_MV_LORA), D ** -0.5),
        'rw_v2': nrm((N_A_VRES, RW_MV_LORA, D), 0.5 * RW_MV_LORA ** -0.5),
        'mb_w_in': nrm((N_B, D, MB_IN_DIM), D ** -0.5),
        'mb_conv_w': nrm((N_B, MB_CONV, MB_CONV_DIM), 0.5),
        'mb_conv_b': nrm((N_B, MB_CONV_DIM), 0.02),
        'mb_dt_bias': dt0 + jnp.log(-jnp.expm1(-dt0)),
        'mb_A_log': jnp.log(unif((N_B, MB_HEADS), 1.0, 16.0)),
        'mb_D': 1.0 + nrm((N_B, MB_HEADS), 0.1),
        'mb_norm_g': 1.0 + nrm((N_B, MB_D_INNER), 0.05),
        'mb_w_out': nrm((N_B, MB_D_INNER, D), MB_D_INNER ** -0.5),
        'sw_w_qkv': nrm((N_C, D, (SW_Q_HEADS + 2 * SW_KV_HEADS) * SW_HEAD_DIM), D ** -0.5),
        'sw_q_norm': 1.0 + nrm((N_C, SW_HEAD_DIM), 0.05),
        'sw_k_norm': 1.0 + nrm((N_C, SW_HEAD_DIM), 0.05),
        'sw_sinks': nrm((N_C, SW_Q_HEADS), 0.5),
        'sw_w_o': nrm((N_C, SW_Q_HEADS * SW_HEAD_DIM, D), (SW_Q_HEADS * SW_HEAD_DIM) ** -0.5),
    }

def second_block(x, c, ada_w, ada_b, norm_g, ffn_w_in, ffn_w_out,
              rw_mu, rw_w_rkv, rw_w_o, rw_w0, rw_w1, rw_w2, rw_a0, rw_a1, rw_a2,
              rw_g1, rw_g2, rw_k_k, rw_k_a, rw_r_k, rw_ln_w, rw_ln_b,
              rw_v0, rw_v1, rw_v2,
              mb_w_in, mb_conv_w, mb_conv_b, mb_dt_bias, mb_A_log, mb_D, mb_norm_g, mb_w_out,
              sw_w_qkv, sw_q_norm, sw_k_norm, sw_sinks, sw_w_o):
    bsz, _, d = x.shape
    c_act = jax.nn.silu(c)
    v_first = None
    for i in range(DEPTH_2):
        mod = (c_act @ ada_w[i] + ada_b[i]).reshape(bsz, N_SUB, 3, d)
        shift, scale, gate = mod[:, :, 0], mod[:, :, 1], mod[:, :, 2]

        h = adaln(x, norm_g[i, 0], shift[:, 0], scale[:, 0])
        x = x + MACARON_W * gate[:, 0, None] * swiglu(h, ffn_w_in[i, 0], ffn_w_out[i, 0])

        h = adaln(x, norm_g[i, 1], shift[:, 1], scale[:, 1])
        kind, j = i % N_MIXERS, i // N_MIXERS
        if kind == 0:
            vres = None if v_first is None else (rw_v0[j - 1], rw_v1[j - 1], rw_v2[j - 1])
            y, v_first = rwkv7_time_mix(h, rw_mu[j], rw_w_rkv[j], rw_w_o[j], rw_w0[j], rw_w1[j],
                                        rw_w2[j], rw_a0[j], rw_a1[j], rw_a2[j], rw_g1[j],
                                        rw_g2[j], rw_k_k[j], rw_k_a[j], rw_r_k[j],
                                        rw_ln_w[j], rw_ln_b[j], v_first, vres)
        elif kind == 1:
            y = mamba2_ssd_mix(h, mb_w_in[j], mb_conv_w[j], mb_conv_b[j], mb_dt_bias[j],
                               mb_A_log[j], mb_D[j], mb_norm_g[j], mb_w_out[j])
        else:
            y = swa_sink_attention(h, sw_w_qkv[j], sw_q_norm[j], sw_k_norm[j],
                                   sw_sinks[j], sw_w_o[j])
        x = x + gate[:, 1, None] * y

        h = adaln(x, norm_g[i, 2], shift[:, 2], scale[:, 2])
        x = x + MACARON_W * gate[:, 2, None] * swiglu(h, ffn_w_in[i, 1], ffn_w_out[i, 1])
    return x


def setup_inputs(seed=0):
    out = dict(first_inputs(seed))
    for name, value in second_inputs(seed + 1).items():
        if name != "x":
            out[name + "_2"] = value
    return out


def reference(
    x, p, ln_mix, ln_ffn, ln_ple, a_w_in, a_q_norm, a_k_norm, a_ck_pos, a_ck_w1, a_ck_w2,
    a_cv_pos, a_cv_w1, a_cv_w2, a_w_out, kv_norm, w_kv_shared, k_norm_shared, b_w_q, b_q_norm,
    b_w_out, moe_w_group, moe_b_group, moe_w_expert, moe_b_expert, moe_w_gate, moe_w_up,
    moe_w_down, ple_w_proj, ple_w_gate, c_2, ada_w_2, ada_b_2, norm_g_2, ffn_w_in_2,
    ffn_w_out_2, rw_mu_2, rw_w_rkv_2, rw_w_o_2, rw_w0_2, rw_w1_2, rw_w2_2, rw_a0_2, rw_a1_2,
    rw_a2_2, rw_g1_2, rw_g2_2, rw_k_k_2, rw_k_a_2, rw_r_k_2, rw_ln_w_2, rw_ln_b_2, rw_v0_2,
    rw_v1_2, rw_v2_2, mb_w_in_2, mb_conv_w_2, mb_conv_b_2, mb_dt_bias_2, mb_A_log_2, mb_D_2,
    mb_norm_g_2, mb_w_out_2, sw_w_qkv_2, sw_q_norm_2, sw_k_norm_2, sw_sinks_2, sw_w_o_2,
):
    x = first_block(
        x, p, ln_mix, ln_ffn, ln_ple, a_w_in, a_q_norm, a_k_norm, a_ck_pos, a_ck_w1, a_ck_w2,
        a_cv_pos, a_cv_w1, a_cv_w2, a_w_out, kv_norm, w_kv_shared, k_norm_shared, b_w_q,
        b_q_norm, b_w_out, moe_w_group, moe_b_group, moe_w_expert, moe_b_expert, moe_w_gate,
        moe_w_up, moe_w_down, ple_w_proj, ple_w_gate,
    )
    return second_block(
        x, c_2, ada_w_2, ada_b_2, norm_g_2, ffn_w_in_2, ffn_w_out_2, rw_mu_2, rw_w_rkv_2,
        rw_w_o_2, rw_w0_2, rw_w1_2, rw_w2_2, rw_a0_2, rw_a1_2, rw_a2_2, rw_g1_2, rw_g2_2,
        rw_k_k_2, rw_k_a_2, rw_r_k_2, rw_ln_w_2, rw_ln_b_2, rw_v0_2, rw_v1_2, rw_v2_2,
        mb_w_in_2, mb_conv_w_2, mb_conv_b_2, mb_dt_bias_2, mb_A_log_2, mb_D_2, mb_norm_g_2,
        mb_w_out_2, sw_w_qkv_2, sw_q_norm_2, sw_k_norm_2, sw_sinks_2, sw_w_o_2,
    )


_drawn_inputs = setup_inputs


def setup_inputs(seed=0):
    import zlib

    import numpy as np

    out = dict(_drawn_inputs(seed))
    spreads = {}
    factors = {'a_ck_pos': 3.877,
     'k_norm_shared': 2.956,
     'b_q_norm': 2.739,
     'moe_b_expert': 2.916,
     'rw_w1_2': 8.0,
     'rw_w2_2': 8.0,
     'rw_a0_2': 8.0,
     'rw_k_k_2': 4.356,
     'rw_k_a_2': 4.149,
     'rw_ln_w_2': 7.653,
     'rw_ln_b_2': 8.0,
     'rw_v0_2': 8.0,
     'rw_v1_2': 3.424,
     'rw_v2_2': 3.397,
     'mb_conv_b_2': 8.0,
     'mb_D_2': 5.038,
     'mb_norm_g_2': 5.744,
     'sw_q_norm_2': 8.0,
     'sw_k_norm_2': 8.0,
     'sw_sinks_2': 200.0}
    for name, (base, spread) in spreads.items():
        noise = np.random.default_rng([zlib.crc32(name.encode()), seed]).standard_normal(out[name].shape)
        drawn = base * np.exp(spread * noise) if base else spread * noise
        out[name] = jnp.asarray(drawn.astype(out[name].dtype))
    for name, factor in factors.items():
        out[name] = (out[name] * factor).astype(out[name].dtype)
    return out
```

```python
from contextlib import ExitStack

import numpy as np

import concourse.bass as bass
import concourse.mybir as mybir
from concourse.alu_op_type import AluOpType as ALU

F32 = mybir.dt.float32
FR = mybir.dt.float32r
I32 = mybir.dt.int32
ACT = mybir.ActivationFunctionType
AX = mybir.AxisListType

T = 256
D = 1024
KD = 8
SLOT = 3072
NSLOT = 4
PIECE = 1024
NPIECE = 8
BIG = 1e30
RSQRT_MAGIC = 1597463007.0
SLOPES = [float(2.0 ** (-8.0 * (i + 1) / 16)) for i in range(16)]


class Queue:

    def __init__(self, sem):
        self.sem, self.ops, self.n = sem, [], 0

    def __call__(self, fn, *waits, inc=True):
        self.ops.append((waits, fn, inc))
        self.n += inc
        return (self.sem, self.n)

    @property
    def last(self):
        return (self.sem, self.n)

    def emit(self, eng):
        seen = {}

        def wait(w):
            if w is None:
                return
            if isinstance(w, (list, tuple)) and not (len(w) == 2 and isinstance(w[1], int)):
                for x in w:
                    wait(x)
                return
            sem, value = w
            if value > seen.get(sem.name, 0):
                eng.wait_ge(sem, value)
                seen[sem.name] = value

        for waits, fn, inc in self.ops:
            wait(waits)
            ins = fn(eng)
            if inc:
                ins.then_inc(self.sem, 1)


def shape_constants():
    p = np.arange(128)[:, None]
    f = np.arange(128)[None, :]
    cols, at = {}, 0
    parts = []

    def add(name, a):
        nonlocal at
        a = np.asarray(a, np.float32)
        cols[name] = (at, a.shape[1])
        at += a.shape[1]
        parts.append(a)

    add("ident", p == f)
    add("blk64", (p // 64) == (f // 64))
    q = np.arange(128)[:, None]
    tri = np.where(q >= f, q - f, BIG)
    add("dist", np.concatenate([tri, q + 128 - f, tri], 1))
    add("swa", np.concatenate([np.where(q >= f, 0, -BIG), np.where(f > q, 0, -BIG), np.where(q >= f, 0, -BIG)], 1))
    slopes = np.array(SLOPES)[None, :, None]
    for qb in range(2):
        t = (np.arange(128) + 128 * qb)[:, None, None]
        end = (np.arange(15) * 16 + 31)[None, None, :]
        dist = (t - end).astype(np.float32)
        add(f"cmp{qb}", np.where(dist >= 0, -slopes * dist, -BIG).reshape(128, 240))
    same = lambda n: (p // n) == (f // n)
    add("L16", same(16) & (f < p))
    add("U16", same(16) & (f > p))
    add("Lo32", same(32) & ~same(16) & (f < p))
    add("Uo32", same(32) & ~same(16) & (f > p))
    add("Lo64", same(64) & ~same(32) & (f < p))
    add("U64", same(64) & (f > p))
    add("Ui64", same(64) & (f >= p))
    add("S384", np.concatenate([f >= p, np.ones((128, 128)), f >= p], 1))
    add("half", p == (np.arange(1024)[None, :] // 64))
    add("reset", np.broadcast_to((np.arange(256) % 64 != 0)[None, :], (128, 256)))
    return np.concatenate(parts, 1), cols


def feat(v):
    v = np.asarray(v).reshape(-1, 128)
    return v.T


def twice(v):
    v = np.asarray(v).reshape(64, 1)
    return np.concatenate([v, v], 0)


def ktiles(w):
    w = np.asarray(w)
    k = w.shape[0] // 128
    return w.reshape(k, 128, w.shape[1]).transpose(1, 0, 2).reshape(128, k * w.shape[1])


def dup_heads(w):
    w = np.asarray(w)
    w = w.reshape(w.shape[0], -1, 1, 64)
    return np.concatenate([w, w], 2).reshape(w.shape[0], -1)


class Layout:

    def __init__(self):
        self.params, self.chunks = [], []
        self.cols, self.size = 0, 0

    def param(self, rows, cols, fn):
        at = self.cols
        self.params.append((at, rows, cols, fn))
        self.cols += cols
        return at

    def chunk(self, rows, cols, fn):
        at = self.size
        self.chunks.append((at, rows, cols, fn))
        self.size += rows * cols
        return at

    def fill(self, inputs):
        small = np.zeros((128, self.cols), np.float32)
        for at, rows, cols, fn in self.params:
            a = np.asarray(fn(inputs))
            assert a.shape == (rows, cols), (a.shape, rows, cols)
            small[:rows, at:at + cols] = a
        flat = np.empty((self.size,), np.float32)
        for at, rows, cols, fn in self.chunks:
            a = np.asarray(fn(inputs))
            assert a.shape == (rows, cols), (a.shape, rows, cols)
            flat[at:at + rows * cols] = a.reshape(-1)
        return small, flat


def plan_params(L):
    c = {}

    def vec(name, n, fn):
        c[name] = L.param(128, n, fn)

    for i in range(2):
        vec(f"ln_mix{i}", 8, lambda I, i=i: feat(I["ln_mix"][i]))
        vec(f"ln_ffn{i}", 8, lambda I, i=i: feat(I["ln_ffn"][i]))
        vec(f"ln_ple{i}", 8, lambda I, i=i: feat(I["ln_ple"][i]))
        c[f"moe_b{i}"] = L.param(1, 36, lambda I, i=i: np.concatenate(
            [np.asarray(I["moe_b_group"])[i], np.asarray(I["moe_b_expert"])[i]])[None, :])
        vec(f"moe_w{i}", 288, lambda I, i=i: ktiles(np.concatenate(
            [np.asarray(I["moe_w_group"])[i], np.asarray(I["moe_w_expert"])[i]], 1)))
        vec(f"p{i}", 512, lambda I, i=i: ktiles(np.asarray(I["p"])[i, 0].T))
    vec("kv_norm", 8, lambda I: feat(I["kv_norm"]))
    vec("a_q", 1, lambda I: twice(np.asarray(I["a_q_norm"])[0]))
    for j in range(3):
        vec(f"a_k{j}", 1, lambda I, j=j: twice(np.asarray(I["a_k_norm"])[0, j]))
    vec("k_shared", 1, lambda I: twice(I["k_norm_shared"]))
    vec("b_q", 1, lambda I: twice(np.asarray(I["b_q_norm"])[0]))
    vec("sw_q", 1, lambda I: twice(np.asarray(I["sw_q_norm_2"])[0]))
    vec("sw_k", 1, lambda I: twice(np.asarray(I["sw_k_norm_2"])[0]))
    vec("sinks", 16, lambda I: np.broadcast_to(np.asarray(I["sw_sinks_2"])[0][None, :], (128, 16)))
    for n in ("ck", "cv"):
        vec(f"{n}_pos", 16, lambda I, n=n: np.asarray(I[f"a_{n}_pos"])[0].reshape(16, 128).T)
    vec("c", 8, lambda I: feat(np.asarray(I["c_2"])[0]))
    for l in range(4):
        vec(f"ada_b{l}", 72, lambda I, l=l: feat(np.asarray(I["ada_b_2"])[l]))
        for s in range(3):
            vec(f"ng{l}{s}", 8, lambda I, l=l, s=s: feat(np.asarray(I["norm_g_2"])[l, s]))
    for j in range(2):
        for m in range(6):
            vec(f"mu{j}{m}", 8, lambda I, j=j, m=m: feat(np.asarray(I["rw_mu_2"])[j, m]))
        for n in ("w0", "a0", "k_k", "k_a", "ln_w", "ln_b"):
            vec(f"{n}{j}", 8, lambda I, j=j, n=n: feat(np.asarray(I[f"rw_{n}_2"])[j]))
        vec(f"r_k{j}", 8, lambda I, j=j: feat(np.asarray(I["rw_r_k_2"])[j].reshape(-1)))
    vec("v01", 8, lambda I: feat(np.asarray(I["rw_v0_2"])[0]))
    for k in range(4):
        vec(f"conv{k}", 32, lambda I, k=k: feat(np.asarray(I["mb_conv_w_2"])[0, k]))
    vec("conv_b", 32, lambda I: feat(np.asarray(I["mb_conv_b_2"])[0]))
    vec("mb_g", 16, lambda I: feat(np.asarray(I["mb_norm_g_2"])[0]))
    vec("mb_D", 16, lambda I: feat(np.repeat(np.asarray(I["mb_D_2"])[0], 64)))
    c["dt_bias"] = L.param(32, 1, lambda I: np.asarray(I["mb_dt_bias_2"])[0][:, None])
    c["A_log"] = L.param(32, 1, lambda I: np.asarray(I["mb_A_log_2"])[0][:, None])
    return c


def build_program(nc, stop=None):
    consts, ccol = shape_constants()
    L = Layout()
    pcol = plan_params(L)
    ctx = ExitStack()
    NC = consts.shape[1]

    def sb(name, cols, dt=F32, rows=128):
        return ctx.enter_context(nc.sbuf_tensor(name, [rows, cols], dt))

    def sem(name):
        return ctx.enter_context(nc.semaphore(name))

    PE, V, A, G, SP = (Queue(sem(f"s_{n}")) for n in ("pe", "dve", "act", "pool", "sp"))

    def now():
        return (PE.last, V.last, A.last, G.last)

    xT = sb("xT", 2048)
    hT = sb("hT", 2048)
    sq = sb("sq", 2048)
    vfirst = sb("vfirst", 2048)
    prm = sb("prm", L.cols)
    cst = sb("cst", NC)
    ones = sb("ones", 256)
    mods = sb("mods", 288)
    cact = sb("cact", 8)
    rsb = sb("rsb", 256)
    nv, nm, nt = sb("nv", 256), sb("nm", 256), sb("nt", 256)
    gs = sb("gs", 16)
    ring = sb("ring", NSLOT * SLOT)
    selw, selg = sb("selw", 128), sb("selg", 64)
    hr, bsum = sb("hr", 256, rows=16), sb("bsum", 256, rows=16)
    dl = sb("dl", 32)
    WK = 23 * 1024 - 64
    with nc.sbuf_tensor("wk", [128, WK], F32) as region:
        wk = region
    with ExitStack() as other:
        def sc(name, cols, dt):
            return other.enter_context(nc.sbuf_tensor(name, [128, cols], dt))

        hx = sc("hx", 4096, FR)
        ex = sc("ex", 3 * 512, FR)
        wh, wl = sc("wh", NPIECE * PIECE, FR), sc("wl", NPIECE * PIECE, FR)
        ada_acc = sc("ada_acc", 384, F32)
    pb = [ctx.enter_context(nc.psum_tensor(f"pb{i}", [128, 512], F32)) for i in range(8)]

    def v3(t, c0, n, w):
        return t[:, c0:c0 + n * w].rearrange("p (n w) -> p n w", w=w)

    def C(name, rows=128):
        a, n = ccol[name]
        return cst[0:rows, a:a + n]

    def pc(name, i=0, n=1, rows=128):
        return prm[0:rows, pcol[name] + i:pcol[name] + i + n]

    ident = C("ident")
    X3, H3, Q3 = (v3(t, 0, 8, T) for t in (xT, hT, sq))

    def tt(q, out, a, b, op, *w):
        return q(lambda e: e.tensor_tensor(out, a, b, op), *w)

    def ts(q, out, a, s1, s2, op0, op1, *w):
        if op1 is None:
            return q(lambda e: e.tensor_scalar(out, a, s1, None, op0), *w)
        return q(lambda e: e.tensor_scalar(out, a, s1, s2, op0, op1), *w)

    def stt(out, a, s, b, op0, op1, *w):
        return V(lambda e: e.scalar_tensor_tensor(out=out, in0=a, scalar=s, in1=b, op0=op0, op1=op1), *w)

    def cp(q, out, a, *w):
        if q is A:
            return q(lambda e: e.activation(out, a, ACT.Copy), *w)
        return q(lambda e: e.tensor_copy(out, a), *w)

    def act(out, a, func, *w, bias=0.0, scale=1.0, accum=None):
        return A(lambda e: e.activation(out, a, func, bias=bias, scale=scale, accum_out=accum), *w)

    def mm(out, l, r, start, stop, *w, inc=False, skip=False):
        return PE(lambda e: e.matmul(out, l, r, start=start, stop=stop, skip_group_check=skip), *w, inc=inc)

    def tp(out, a, *w, inc=False):
        n = a.shape[0]
        base = a.base_partition() if callable(a.base_partition) else a.base_partition
        idn = cst[base:base + n, ccol["ident"][0] + base:ccol["ident"][0] + base + n]
        return PE(lambda e: e.transpose(out, a, idn), *w, inc=inc)

    def recip(out, a, *w):
        return V(lambda e: e.reciprocal(out, a), *w)

    def red(out, a, op, *w):
        return V(lambda e: e.tensor_reduce(out, a, AX.X, op), *w)

    class Banks:
        def __init__(self):
            self.free = [None] * 8
            self.ids, self.at = list(range(8)), 0

        def use(self, ids):
            self.ids, self.at = list(ids), 0

        def get(self):
            i = self.ids[self.at % len(self.ids)]
            self.at += 1
            return i, pb[i], self.free[i]

        def put(self, i, *toks):
            self.free[i] = toks

    bk = Banks()

    class Ring:
        def __init__(self):
            self.sems = [sem(f"s_ring{i}") for i in range(NSLOT)]
            self.free = [None] * NSLOT
            self.uses = [0] * NSLOT
            self.at = 0

        def get(self, rows, cols, fn):
            assert cols <= SLOT
            i = self.at % NSLOT
            self.at += 1
            self.uses[i] += 1
            off = L.chunk(rows, cols, fn)
            dst = ring[0:rows, i * SLOT:i * SLOT + cols]
            loads.append((off, rows, cols, dst, self.sems[i], self.free[i]))
            return i, dst, (self.sems[i], 16 * self.uses[i])

        def put(self, i, tok):
            self.free[i] = tok

    loads = []
    rg = Ring()
    s_in, s_out = sem("s_in"), sem("s_out")
    loaded = (s_in, 48)

    def rsqrt(out, src, P, N, mult, add, tok):
        a, b, c = nv[0:P, 0:N], nm[0:P, 0:N], nt[0:P, 0:N]
        t0 = ts(V, a, src, mult, add, ALU.mult, ALU.add, tok, V.last)
        return t0, rsqrt_of(out, a, b, c)

    def rsqrt_of(out, a, b, c):
        ts(V, out.bitcast(I32), a.bitcast(I32), -0.5, RSQRT_MAGIC, ALU.mult, ALU.add, V.last)
        t = ts(V, b, a, -0.5, None, ALU.mult, None, V.last)
        for _ in range(3):
            t = tt(V, c, out, out, ALU.mult, t)
            t = tt(V, c, c, b, ALU.mult, t)
            t = stt(out, c, 1.5, out, ALU.add, ALU.mult, t)
        return t

    def dnorm(tok, between=lambda: None):
        t1 = act(sq[:, 0:1024], xT[:, 0:1024], ACT.Square, tok, now())
        t2 = tt(V, sq[:, 1024:2048], xT[:, 1024:2048], xT[:, 1024:2048], ALU.mult, tok, now())
        between()
        i, ps, fr = bk.get()
        for k in range(KD):
            t = mm(ps[:, 0:T], ones[:, 0:128], Q3[:, k, :], k == 0, k == KD - 1,
                   fr, t1 if k < 4 else t2, inc=(k == KD - 1))
        t0, t = rsqrt(rsb[:, :], ps[:, 0:T], 128, T, 1.0 / D, 1e-6, (t, PE.last))
        bk.put(i, t0)
        return t

    def apply_norm(gain, tok, ph):
        for k in range(KD):
            t = stt(H3[:, k, :], X3[:, k, :], gain(k), rsb[:, :], ALU.mult, ALU.mult, tok, ph)
        return t

    def lin(N, K, fn, rhs, rhs_tok, evac, tiles=None):
        KT = K // 128
        per = max(1, SLOT // (KT * 128))
        M = N // 128
        for m0 in range(0, M, per):
            n = min(per, M - m0)
            s, wt, wtok = rg.get(128, KT * n * 128,
                                 lambda I, a=m0 * 128, b=(m0 + n) * 128: ktiles(fn(I, a, b)))
            w = wt.rearrange("p (k n) -> p k n", k=KT)
            for j in range(n):
                i, ps, fr = bk.get()
                for k in range(KT):
                    t = mm(ps[:, 0:T], w[:, k, j * 128:(j + 1) * 128], rhs[:, k, :], k == 0, k == KT - 1,
                           fr, wtok, rhs_tok, inc=(k == KT - 1))
                if j == n - 1:
                    rg.put(s, t)
                bk.put(i, evac(m0 + j, ps[:, 0:T], t))
        return None

    def tokmajor(rhs, n, wtok, h_tok, evac):
        t = None
        for tb in range(2):
            i, ps, fr = bk.get()
            for k in range(KD):
                t = mm(ps[:, 0:n], H3[:, k, tb * 128:(tb + 1) * 128], rhs[:, k, :], k == 0, k == KD - 1,
                       fr, wtok, h_tok, inc=(k == KD - 1))
            bk.put(i, evac(tb, ps[:, 0:n], t))
        return t

    def half_select(k):
        return selw[:, k * 16:(k + 1) * 16]

    def head_rows(src, nt_, n, tok):
        i, ps, fr = bk.get()
        for k in range(nt_):
            t = mm(ps[0:16, 0:n], half_select(k), src[:, k, :], k == 0, k == nt_ - 1, fr, tok, inc=(k == nt_ - 1))
        return i, ps[0:2 * nt_, 0:n], t

    def head_bcast(rows, k, n, tok):
        i, ps, fr = bk.get()
        sel = C("half", 16)[:, k * 128:(k + 1) * 128]
        t = mm(ps[:, 0:n], sel, rows, True, True, fr, tok, inc=True)
        return i, ps[:, 0:n], t

    def head_norm(src, dst, nt_, n, gain, scale, tok):
        w = nt_ * n
        sq3 = sq[:, 0:w].rearrange("p (k n) -> p k n", n=n)
        t1 = act(sq3, src, ACT.Square, tok, now())
        i, ps, t = head_rows(sq3, nt_, n, t1)
        rows = hr[0:16, 0:n]
        if nt_ < 8:
            t0 = ts(V, nv[0:16, 0:n], pb[i][0:16, 0:n], 1.0 / 64, 1e-6, ALU.mult, ALU.add, t, V.last)
        else:
            t0 = ts(V, nv[0:16, 0:n], ps, 1.0 / 64, 1e-6, ALU.mult, ALU.add, t, V.last)
        bk.put(i, t0)
        t = rsqrt_of(rows, nv[0:16, 0:n], nm[0:16, 0:n], nt[0:16, 0:n])
        t = ts(V, rows, rows, scale, None, ALU.mult, None, t)
        for k in range(nt_):
            i, ps, tb = head_bcast(rows, k, n, t)
            tl = stt(dst[:, k, :], src[:, k, :], gain, ps, ALU.mult, ALU.mult, tb, tok)
            bk.put(i, tl)
        return tl

    V(lambda e: e.memset(ones[:, :], 1.0))
    V(lambda e: e.memset(selw[:, :], 0.0))
    t_sel = V.last
    for k in range(8):
        V(lambda e, k=k: e.memset(selw[0:64, k * 16 + 2 * k:k * 16 + 2 * k + 1], 1.0), t_sel)
        V(lambda e, k=k: e.memset(selw[64:128, k * 16 + 2 * k + 1:k * 16 + 2 * k + 2], 1.0), t_sel)
    t_sel = V.last

    state = {"x": (loaded, t_sel)}
    act(cact[:, :], pc("c", 0, 8), ACT.Silu, loaded)

    ada = {"at": 0, "tok": {}, "free": None, "pend": None}

    def ada_next(*free):
        if ada["at"] >= 96:
            return
        l, c = divmod(ada["at"], 24)
        ada["at"] += 1
        s, wt, wtok = rg.get(128, 3072, lambda I: ktiles(np.asarray(I["ada_w_2"])[l][:, c * 384:(c + 1) * 384]))
        w = wt.rearrange("p (k n) -> p k n", k=8)
        t = act(ada_acc[:, :], w[:, 0, :], ACT.Copy, wtok, t_cact, ada["free"], free, scale=cact[:, 0:1])
        for k in range(1, 8):
            t = stt(ada_acc[:, :], w[:, k, :], cact[:, k:k + 1], ada_acc[:, :], ALU.mult, ALU.add, t)
        rg.put(s, t)
        ada["pend"] = (l, c, t)

    def ada_sum():
        if ada["pend"] is None:
            return
        (l, c, t), ada["pend"] = ada["pend"], None
        i, ps, fr = bk.get()
        for j in range(3):
            tp_ = mm(ps[:, j:j + 1], ada_acc[:, j * 128:(j + 1) * 128], ones[:, 0:1], True, True, fr, t, inc=(j == 2))
        ada["free"] = tp_
        a = c * 3
        tl = tt(V, mods[:, l * 72 + a:l * 72 + a + 3], ps[:, 0:3], pc(f"ada_b{l}", a, 3), ALU.add, tp_)
        bk.put(i, tl)
        ada["tok"][l] = tl

    t_cact = A.last

    def mod(l, s, which, k):
        return mods[:, l * 72 + s * 24 + which * 8 + k:l * 72 + s * 24 + which * 8 + k + 1]

    Hh, Hl = v3(hx, 0, 8, T), v3(hx, 2048, 8, T)
    piece = {"n": 0, "free": [None] * NPIECE}

    def split_piece(raw, q, *w):
        i = piece["n"] % NPIECE
        piece["n"] += 1
        hi, lo = (t[:, i * PIECE:(i + 1) * PIECE] for t in (wh, wl))
        ta = act(hi, raw, ACT.Copy, w, piece["free"][i])
        tl = tt(q, lo, raw, hi, ALU.subtract, ta)
        return i, tl

    def mm3(out, wi, c, xh, xl, start, stop, *w, inc=False):
        a = wi * PIECE + c
        hi, lo = wh[:, a:a + 128], wl[:, a:a + 128]
        mm(out, hi, xh, start, False, w, skip=True)
        mm(out, hi, xl, False, False, skip=True)
        return mm(out, lo, xh, False, stop, inc=inc, skip=True)

    class Units:

        def __init__(self, fn):
            self.fn, self.u, self.ph, self.ready = fn, 0, now(), []

        def fetch(self):
            u = self.u
            self.u += 1
            s, w, wtok = rg.get(128, 3072, lambda I: self.fn(I, u))
            ps = [split_piece(w[:, j * PIECE:(j + 1) * PIECE], q, wtok, self.ph) for j, q in enumerate((V, V, G))]
            rg.put(s, [t for _, t in ps])
            self.ready.append(ps)

    def glu(units, src, h_tok, evac, cw=None):
        ph = now()
        bk.use([4, 5, 6, 7])
        Y = [pb[i] for i in range(4)]
        yfree = [bk.free[i] for i in range(4)]
        sg = [sq[:, 768 + i * 256:768 + (i + 1) * 256] for i in range(3)]
        eh = [ex[:, i * 512:i * 512 + 256] for i in range(3)]
        el = [ex[:, i * 512 + 256:(i + 1) * 512] for i in range(3)]
        e_free = [ph, ph, ph]
        pend = []

        def down(u, wi, wtok, t_hid):
            for m in range(8):
                t = mm3(Y[m // 2][:, (m % 2) * T:(m % 2 + 1) * T], wi, m * 128, eh[u % 3], el[u % 3],
                        u == 0 and m % 2 == 0, u == units - 1, t_hid, wtok, yfree, inc=(m == 7))
            piece["free"][wi] = t
            e_free[u % 3] = t

        for u in range(units):
            (wa, ta), (wb, tb), (wd, td) = src.ready.pop(0)
            i, ps, fr = bk.get()
            for b, (wi, wtok) in enumerate(((wa, ta), (wb, tb))):
                for k in range(KD):
                    t = mm3(ps[:, b * T:(b + 1) * T], wi, k * 128, Hh[:, k, :], Hl[:, k, :],
                            k == 0, k == KD - 1, fr, wtok, h_tok[k], inc=(k == KD - 1))
                piece["free"][wi] = t
            if cw is not None:
                ic, pcw, frc = bk.get()
                sel = cst[0:32, ccol["ident"][0] + u:ccol["ident"][0] + u + 1].to_broadcast([32, 128])
                tc = mm(pcw[:, 0:T], sel, cw[0], True, True, frc, cw[1], inc=True)
            if src.u == u + 1 < units:
                src.fetch()
            g_, n = sg[u % 3], u % 3
            t1 = act(g_, ps[:, 0:T], ACT.Silu, t, e_free[n])
            t2 = tt(V, g_, g_, ps[:, T:2 * T], ALU.mult, t, t1)
            bk.put(i, t1, t2)
            if cw is not None:
                t2 = tt(V, g_, g_, pcw[:, 0:T], ALU.mult, tc, t2)
                bk.put(ic, t2)
            t1 = act(eh[n], g_, ACT.Copy, t2, e_free[n])
            t2 = tt(V, el[n], g_, eh[n], ALU.subtract, t1)
            pend.append((u, wd, td, t2))
            if len(pend) > 1:
                down(*pend.pop(0))
            if u % 2:
                ada_next(ph)
            else:
                ada_sum()
        down(*pend.pop(0))
        ada_sum()
        t = PE.last
        for m in range(8):
            tl = evac(m, Y[m // 2][:, (m % 2) * T:(m % 2 + 1) * T], t)
        for i in range(4):
            bk.put(i, tl)
        bk.use(range(8))
        return tl

    def attention(units, off, evac):
        ph = now()
        bk.use([2, 3, 4, 5, 6, 7])
        NB = 3
        sbuf = [wk[:, off + i * 384:off + (i + 1) * 384] for i in range(NB)]
        ptb = [wk[:, off + 1152 + i * 384:off + 1152 + (i + 1) * 384] for i in range(NB)]
        stb = [wk[:, off + 2304 + i * 8:off + 2304 + (i + 1) * 8] for i in range(NB)]
        sfree, pfree = [ph] * NB, [ph] * NB
        st = {}

        def scores(n, u):
            i, ps, fr = bk.get()
            mm(ps[:, 0:128], u["q"][:, 0:128], u["k"][:, 0:128], True, True, fr, u["tok"])
            t = mm(ps[:, 128:384], u["q"][:, 128:256], u["k"][:, 0:256], True, True, inc=True)
            b, s = sbuf[n % NB], stb[n % NB]
            init = u["sink"] if u["sink"] is not None else -3e38
            for qb, (a, z) in enumerate(((0, 128), (128, 384))):
                tm = V(lambda e, qb=qb, a=a, z=z: e.tensor_tensor_reduce(
                    out=b[:, a:z], in0=u["bias"][:, a:z], in1=ps[:, a:z], scale=1.0, scalar=init,
                    op0=ALU.add, op1=ALU.max, accum_out=s[:, qb:qb + 1]), t, sfree[n % NB], u["btok"])
            bk.put(i, tm)
            tm = ts(V, s[:, 2:4], s[:, 0:2], -1.0, None, ALU.mult, None, tm)
            te = None
            for qb, (a, z) in enumerate(((0, 128), (128, 384))):
                te = act(b[:, a:z], b[:, a:z], ACT.Exp, tm, bias=s[:, 2 + qb:3 + qb], accum=s[:, 4 + qb:5 + qb])
            if u["sink"] is not None:
                te = act(s[:, 6:8], s[:, 2:4], ACT.Exp, tm, bias=u["sink"])
            st[n] = te

        def normalise(n, u):
            b, s = sbuf[n % NB], stb[n % NB]
            t = st[n]
            if u["sink"] is not None:
                t = tt(V, s[:, 4:6], s[:, 4:6], s[:, 6:8], ALU.add, t)
            else:
                t = ts(V, s[:, 4:6], s[:, 4:6], 1e-30, None, ALU.max, None, t)
            t = recip(s[:, 4:6], s[:, 4:6], t)
            for qb, (a, z) in enumerate(((0, 128), (128, 384))):
                if u["gate"] is None:
                    tn = ts(V, b[:, a:z], b[:, a:z], s[:, 4 + qb:5 + qb], None, ALU.mult, None, t)
                else:
                    tn = ts(V, b[:, a:z], b[:, a:z], s[:, 4 + qb:5 + qb], u["gate"](qb), ALU.mult, ALU.mult, t, u["tok"])
            i, ps, fr = bk.get()
            for j in range(3):
                t = tp(ps[:, j * 128:(j + 1) * 128], b[:, j * 128:(j + 1) * 128], fr, tn, inc=(j == 2))
            sfree[n % NB] = t
            p = ptb[n % NB]
            tc = A(lambda e: e.activation(p[:, 0:128], ps[:, 0:128], ACT.Copy), t, pfree[n % NB])
            tc = A(lambda e: e.activation(p[:, 128:256], ps[:, 128:256], ACT.Copy))
            tc = A(lambda e: e.activation(p[:, 256:384], ps[:, 256:384], ACT.Copy))
            bk.put(i, tc)
            st[n] = tc

        def values(n, u):
            h = u["h"]
            hp = h % 2
            ob = pb[(h // 2) % 2]
            o = ob[64 * hp:64 * hp + 64, :]
            p = ptb[n % NB]
            fr = bk.free[(h // 2) % 2]
            first = u["first"]
            if first:
                for j, (l, r, et) in enumerate(u["extra"]):
                    mm(o[:, 0:T], l, r, first, False, fr, et, skip=True)
                    first = False
            mm(o[:, 0:T], u["v"](0), p[:, 0:256], first, False, fr, st[n], u["tok"], skip=True)
            t = mm(o[:, 128:256], u["v"](1), p[:, 256:384], False, u["last"], inc=True, skip=True)
            pfree[n % NB] = t
            if u["last"] and hp == 1:
                bk.put((h // 2) % 2, evac(h // 2, ob[:, 0:T], t))

        n = len(units)
        for i in range(n + 2):
            if i < n:
                scores(i, units[i])
            if 1 <= i <= n:
                normalise(i - 1, units[i - 1])
            if i >= 2:
                values(i - 2, units[i - 2])
        bk.use(range(8))

    def residual(m, ps, t):
        return tt(V, X3[:, m, :], X3[:, m, :], ps, ALU.add, t)

    def gated_residual(l, s):
        return lambda m, ps, t: stt(X3[:, m, :], ps, mod(l, s, 2, m), X3[:, m, :], ALU.mult, ALU.add, t)

    def alibi(off, ph):
        b3 = v3(wk, off, 16, 384)
        for h in range(16):
            t = ts(G, b3[:, h, :], C("dist"), -SLOPES[h], None, ALU.mult, None, ph, loaded)
        return b3, t

    def nsa():
        ph = now()
        t = dnorm(state["x"])
        t_h = apply_norm(lambda k: pc("ln_mix0", k), t, ph)
        ph = now()
        o = 0

        def take(n):
            nonlocal o
            o += n
            return o - n

        qT = v3(wk, take(2048), 8, T)
        ksT, kwT = v3(wk, take(1024), 4, T), v3(wk, take(1024), 4, T)
        vS, vW = v3(wk, take(512), 2, T), v3(wk, take(512), 2, T)
        gts = v3(wk, take(96), 2, 48)
        b_off = take(16 * 384)
        pct_off = take(4096)
        oT_off = take(2048)
        kcT = wk[:, take(60):o].rearrange("p (k n) -> p k n", n=60)
        vc = wk[0:15, take(256):o]
        a_off = take(2336)
        oT = v3(wk, oT_off, 8, T)
        bias, t_bias = alibi(b_off, ph)
        W = lambda a, b: (lambda I: np.asarray(I["a_w_in"])[0][:, a:b])

        Xc = wk[:, pct_off:pct_off + 960].rearrange("p (k n) -> p k n", n=60)
        hid = wk[:, pct_off + 1024:pct_off + 1024 + 120].rearrange("p (m n) -> p m n", n=60)
        t_free = ph
        for which, name, a in ((0, "ck", 1024), (1, "cv", 1280)):
            pos = pc(f"{name}_pos", 0, 16)

            def to_windows(g, ps, t):
                pv = ps.rearrange("p (n k two) -> p two k n", k=8, two=2)
                for hf in range(2):
                    r = slice(64 * hf, 64 * hf + 64)
                    for kh in range(2):
                        tl = tt(V, Xc[r, kh * 8:(kh + 1) * 8, g * 15:(g + 1) * 15], pv[r, hf, :, kh:kh + 15],
                                pos[r, kh * 8:(kh + 1) * 8].unsqueeze(2).to_broadcast([64, 8, 15]), ALU.add, t, t_free)
                return tl

            lin(512, D, lambda I, n0, n1, a=a: dup_heads(W(a, a + 256)(I))[:, n0:n1], H3, t_h, to_windows)
            t_x = V.last
            for m in range(2):
                s, wt, wtok = rg.get(128, 2048, lambda I, m=m, name=name: ktiles(
                    np.asarray(I[f"a_{name}_w1"])[0][:, m * 128:(m + 1) * 128]))
                w1 = wt.rearrange("p (k n) -> p k n", k=16)
                i, ps, fr = bk.get()
                for k in range(16):
                    t = mm(ps[:, 0:60], w1[:, k, :], Xc[:, k, :], k == 0, k == 15, fr, wtok, t_x, inc=(k == 15))
                rg.put(s, t)
                t_g = act(hid[:, m, :], ps[:, 0:60], ACT.Gelu_apprx_tanh, t, t_free)
                bk.put(i, t_g)
            if which == 0:
                s, wt, wtok = rg.get(128, 256, lambda I: ktiles(dup_heads(np.asarray(I["a_ck_w2"])[0])))
                w2 = wt.rearrange("p (k n) -> p k n", k=2)
                i, ps, fr = bk.get()
                for m in range(2):
                    t = mm(ps[:, 0:60], w2[:, m, :], hid[:, m, :], m == 0, m == 1, fr, wtok, t_g, inc=(m == 1))
                rg.put(s, t)
                t = cp(V, kcT[:, 0, :], ps[:, 0:60], t)
                bk.put(i, t)
                t_kc = head_norm(kcT, kcT, 1, 60, pc("a_k0"), 1.0, t)
            else:
                s, wt, wtok = rg.get(128, 128, lambda I: ktiles(np.asarray(I["a_cv_w2"])[0]))
                w2 = wt.rearrange("p (k n) -> p k n", k=2)
                i, ps, fr = bk.get()
                for g in range(4):
                    for m in range(2):
                        t = mm(ps[0:15, g * 64:(g + 1) * 64], hid[:, m, g * 15:(g + 1) * 15], w2[:, m, :], m == 0, m == 1,
                               fr, wtok, t_g, inc=(m == 1 and g == 3))
                rg.put(s, t)
                t_vc = cp(V, vc, ps[0:15, 0:256], t)
                bk.put(i, t_vc)
            t_free = now()

        lin(D, D, lambda I, n0, n1: W(n0, n1)(I), H3, t_h, lambda m, ps, t: cp(A, qT[:, m, :], ps, t, ph))
        t_q = head_norm(qT, qT, 8, T, pc("a_q"), 0.125, A.last)
        for kT, a, gain in ((ksT, 1536, "a_k1"), (kwT, 2048, "a_k2")):
            lin(512, D, lambda I, n0, n1, a=a: dup_heads(W(a, a + 256)(I))[:, n0:n1], H3, t_h,
                lambda m, ps, t, kT=kT: cp(A, kT[:, m, :], ps, t, ph))
            t_k = head_norm(kT, kT, 4, T, pc(gain), 1.0, A.last)
        for vv, a in ((vS, 1792), (vW, 2304)):
            s, wt, wtok = rg.get(128, 2048, lambda I, a=a: ktiles(W(a, a + 256)(I)))
            t = tokmajor(wt.rearrange("p (k n) -> p k n", k=8), 256, wtok, t_h,
                         lambda tb, ps, t, vv=vv: cp(A, vv[:, tb, :], ps, t, ph))
            rg.put(s, t)
        s, wt, wtok = rg.get(128, 384, lambda I: ktiles(W(2560, 2608)(I)))
        t = tokmajor(wt.rearrange("p (k n) -> p k n", k=8), 48, wtok, t_h,
                     lambda tb, ps, t: act(gts[:, tb, :], ps, ACT.Sigmoid, t, ph))
        rg.put(s, t)
        t_all = now()

        pct = wk[0:15, pct_off:pct_off + 4096].rearrange("p (h t) -> p h t", t=T)
        cs = wk[:, a_off:a_off + 240]
        c3 = cs.rearrange("p (h n) -> p h n", n=15)
        cst1 = wk[:, a_off + 240:a_off + 272]
        for qb in range(2):
            cm = C(f"cmp{qb}").rearrange("p (h two n) -> p two h n", two=2, n=15)
            ch = cs.rearrange("p (h two n) -> p two h n", two=2, n=15)
            ready = now()
            for hp in range(2):
                i, ps, fr = bk.get()
                for n in range(8):
                    h = 2 * n + hp
                    t = mm(ps[:, n * 15:(n + 1) * 15], qT[64 * hp:64 * hp + 64, n, qb * 128:(qb + 1) * 128],
                           kcT[64 * hp:64 * hp + 64, 0, (h // 4) * 15:(h // 4 + 1) * 15], True, True, fr, t_all, inc=(n == 7))
                t = tt(V, ch[:, hp], ps[:, 0:120].rearrange("p (h n) -> p h n", n=15), cm[:, hp], ALU.add, t, ready)
                bk.put(i, t)
            mx, sm = cst1[:, 0:16], cst1[:, 16:32]
            t = red(mx, c3, ALU.max, t)
            t = ts(V, mx, mx, -1e20, None, ALU.max, None, t)
            t = tt(V, c3, c3, mx.unsqueeze(2).to_broadcast([128, 16, 15]), ALU.subtract, t)
            t = act(cs, cs, ACT.Exp, t)
            t = red(sm, c3, ALU.add, t)
            t = ts(V, sm, sm, 1e-30, None, ALU.max, None, t)
            t = recip(sm, sm, t)
            gq = gts[:, qb, :].rearrange("p (h b) -> p b h", b=3)[:, 0, :]
            t = tt(V, sm, sm, gq, ALU.mult, t)
            t = tt(V, c3, c3, sm.unsqueeze(2).to_broadcast([128, 16, 15]), ALU.mult, t)
            for h4 in range(4):
                i, ps, fr = bk.get()
                for j in range(4):
                    tk = tp(ps[0:15, j * 128:(j + 1) * 128], c3[:, h4 * 4 + j, :], fr, t, inc=(j == 3))
                tl = cp(V, pct[:, h4 * 4:h4 * 4 + 4, qb * 128:(qb + 1) * 128],
                        ps[0:15, 0:512].rearrange("p (h t) -> p h t", t=128), tk, t_all)
                bk.put(i, tl)
        t_pc = now()
        units = []
        for h in range(16):
            g, r = h // 4, slice(64 * (h % 2), 64 * (h % 2) + 64)
            for b, (kT, vv) in enumerate(((ksT, vS), (kwT, vW))):
                units.append(dict(
                    h=h, q=qT[r, h // 2, :], k=kT[r, g, :], bias=bias[:, h, :], btok=t_bias, tok=t_pc, sink=None,
                    v=lambda kb, vv=vv, g=g: vv[:, kb, g * 64:(g + 1) * 64],
                    gate=lambda qb, h=h, b=b: gts[:, qb, h * 3 + 1 + b:h * 3 + 2 + b],
                    first=(b == 0), last=(b == 1),
                    extra=[(vc[:, g * 64:(g + 1) * 64], pct[:, h, :], t_pc)]))
        attention(units, a_off, lambda m, ps, t: cp(V, oT[:, m, :], ps, t, ph))
        lin(D, D, lambda I, n0, n1: np.asarray(I["a_w_out"])[0][:, n0:n1], oT, V.last, residual)
        state["x"] = V.last

    def moba():
        ph = now()
        t = dnorm(state["x"])
        t_h = apply_norm(lambda k: pc("kv_norm", k), t, ph)
        ph = now()
        qT, kT, vv = v3(wk, 0, 8, T), v3(wk, 2048, 4, T), v3(wk, 3072, 2, T)
        oT = v3(wk, 3584, 8, T)
        bias, t_bias = alibi(5632, ph)
        a_off = 5632 + 16 * 384
        W = lambda a, b: (lambda I: np.asarray(I["w_kv_shared"])[:, a:b])
        lin(512, D, lambda I, n0, n1: dup_heads(W(0, 256)(I))[:, n0:n1], H3, t_h,
            lambda m, ps, t: cp(A, kT[:, m, :], ps, t, ph))
        t_k = head_norm(kT, kT, 4, T, pc("k_shared"), 1.0, A.last)
        s, wt, wtok = rg.get(128, 2048, lambda I: ktiles(W(256, 512)(I)))
        t = tokmajor(wt.rearrange("p (k n) -> p k n", k=8), 256, wtok, t_h,
                     lambda tb, ps, t: cp(A, vv[:, tb, :], ps, t, ph))
        rg.put(s, t)
        t_h = apply_norm(lambda k: pc("ln_mix1", k), None, now())
        lin(D, D, lambda I, n0, n1: np.asarray(I["b_w_q"])[0][:, n0:n1], H3, t_h,
            lambda m, ps, t: cp(A, qT[:, m, :], ps, t, ph))
        head_norm(qT, qT, 8, T, pc("b_q"), 0.125, A.last)
        t_all = now()
        units = []
        for h in range(16):
            g, r = h // 4, slice(64 * (h % 2), 64 * (h % 2) + 64)
            units.append(dict(h=h, q=qT[r, h // 2, :], k=kT[r, g, :], bias=bias[:, h, :], btok=t_bias, tok=t_all,
                              sink=None, gate=None, first=True, last=True, extra=[],
                              v=lambda kb, g=g: vv[:, kb, g * 64:(g + 1) * 64]))
        attention(units, a_off, lambda m, ps, t: cp(V, oT[:, m, :], ps, t, ph))
        lin(D, D, lambda I, n0, n1: np.asarray(I["b_w_out"])[0][:, n0:n1], oT, V.last, residual)
        state["x"] = V.last

    def moe(l):
        def unit(I, u):
            a = ktiles(np.asarray(I["moe_w_gate"])[l, u])
            b = ktiles(np.asarray(I["moe_w_up"])[l, u])
            return np.concatenate([a, b, np.asarray(I["moe_w_down"])[l, u]], 1)

        ph = now()
        src = Units(unit)
        t = dnorm(state["x"], src.fetch)
        t_n = []
        for k in range(KD):
            t_n.append(stt(H3[:, k, :], X3[:, k, :], pc(f"ln_ffn{l}", k), rsb[:, :], ALU.mult, ALU.mult, t, ph))
        t_h = t_n[-1]
        t_hx = []
        for k in range(KD):
            t1 = act(Hh[:, k, :], H3[:, k, :], ACT.Copy, t_n[k], ph)
            t_hx.append(tt(V if k % 3 else G, Hl[:, k, :], H3[:, k, :], Hh[:, k, :], ALU.subtract, t1))
        ph = now()
        src.fetch()
        o = 0

        def take(n):
            nonlocal o
            o += n
            return sq[:, o - n:o]

        lg = take(72).rearrange("p (b n) -> p b n", b=2)
        wr = pc(f"moe_w{l}", 0, 288).rearrange("p (k n) -> p k n", k=8)
        for tb in range(2):
            i, ps, fr = bk.get()
            for k in range(8):
                mm(ps[:, 0:36], H3[:, k, tb * 128:(tb + 1) * 128], wr[:, k, :], k == 0, False, fr, t_h, loaded)
            t = mm(ps[:, 0:36], ones[0:1, 0:128], pc(f"moe_b{l}", 0, 36, 1), False, True, inc=True)
            t = cp(V, lg[:, tb, :], ps[:, 0:36], t, ph)
            bk.put(i, t)

        def first_max(src, n, t):
            mx, eq, cum, oh = take(2), take(2 * n), take(2 * n), take(2 * n)
            eq, cum, oh = (a.rearrange("p (b n) -> p b n", b=2) for a in (eq, cum, oh))
            t = red(mx, src, ALU.max, t)
            t = tt(V, eq, src, mx.unsqueeze(2).to_broadcast([128, 2, n]), ALU.is_equal, t)
            for b in range(2):
                tb_ = V(lambda e, b=b: e.tensor_tensor_scan(cum[:, b, :], ones[:, 0:n], eq[:, b, :], 0.0, ALU.mult, ALU.add), t)
            t = stt(oh, cum, 1.0, eq, ALU.is_equal, ALU.mult, tb_)
            return mx, oh, t

        gl = lg[:, :, 0:4]
        gm, goh, t = first_max(gl, 4, t)
        ge = take(8).rearrange("p (b n) -> p b n", b=2)
        gw = take(2)
        t = tt(V, ge, gl, gm.unsqueeze(2).to_broadcast([128, 2, 4]), ALU.subtract, t)
        t = act(ge, ge, ACT.Exp, t)
        t = red(gw, ge, ALU.add, t)
        t = recip(gw, gw, t)
        pr = take(64).rearrange("p (b e g) -> p b e g", b=2, g=4)
        el = take(16).rearrange("p (b n) -> p b n", b=2)
        for b in range(2):
            t = tt(V, pr[:, b], lg[:, b, 4:36].rearrange("p (g e) -> p e g", g=4),
                   goh[:, b, :].unsqueeze(1).to_broadcast([128, 8, 4]), ALU.mult, t)
        t = red(el, pr, ALU.add, t)
        m1, oh1, t = first_max(el, 8, t)
        el2 = take(16).rearrange("p (b n) -> p b n", b=2)
        t = stt(el2, oh1, -3e38, el, ALU.mult, ALU.add, t)
        m2, oh2, t = first_max(el2, 8, t)
        e2, den = take(2), take(2)
        t = tt(V, e2, m2, m1, ALU.subtract, t)
        t = act(e2, e2, ACT.Exp, t)
        t = ts(V, den, e2, 1.0, None, ALU.add, None, t)
        t = recip(den, den, t)
        t = tt(V, den, den, gw, ALU.mult, t)
        wgt = take(16).rearrange("p (b n) -> p b n", b=2)
        cw = take(64).rearrange("p (b g e) -> p b g e", b=2, g=4)
        for b in range(2):
            t = stt(wgt[:, b, :], oh2[:, b, :], e2[:, b:b + 1], oh1[:, b, :], ALU.mult, ALU.add, t)
            t = ts(V, wgt[:, b, :], wgt[:, b, :], den[:, b:b + 1], None, ALU.mult, None, t)
            t = tt(V, cw[:, b], goh[:, b, :].unsqueeze(2).to_broadcast([128, 4, 8]),
                   wgt[:, b, :].unsqueeze(1).to_broadcast([128, 4, 8]), ALU.mult, t)
        cwT = take(256)[0:32, :]
        i, ps, fr = bk.get()
        for b in range(2):
            tk = tp(ps[0:32, b * 128:(b + 1) * 128], cw[:, b].rearrange("p g e -> p (g e)"), fr, t, inc=(b == 1))
        t = cp(V, cwT, ps[0:32, 0:T], tk)
        bk.put(i, t)

        assert o <= 768
        state["x"] = glu(32, src, t_hx, residual, cw=(cwT, t))

    def ple(l):
        ph = now()
        t = dnorm(state["x"])
        t_h = apply_norm(lambda k: pc(f"ln_ple{l}", k), t, ph)
        ph = now()
        gt = v3(wk, 0, 8, T)
        lin(D, D, lambda I, n0, n1: np.asarray(I["ple_w_gate"])[l][:, n0:n1], H3, t_h,
            lambda m, ps, t: act(gt[:, m, :], ps, ACT.Sigmoid, t, ph))
        t_g = A.last
        pT = pc(f"p{l}", 0, 512).rearrange("p (k n) -> p k n", k=2)

        def add(m, ps, t):
            t1 = tt(V, gt[:, m, :], gt[:, m, :], ps, ALU.mult, t, t_g)
            tt(V, X3[:, m, :], X3[:, m, :], gt[:, m, :], ALU.add, t1)
            return t1

        lin(D, 256, lambda I, n0, n1: np.asarray(I["ple_w_proj"])[l][:, n0:n1], pT, loaded, add)
        state["x"] = V.last

    def adaln(l, s, src=None):
        while ada["at"] < 24 * (l + 1):
            ada_next(now())
            ada_sum()
        ph = now()
        t = dnorm(state["x"], src.fetch if src else lambda: None)
        tg = ts(V, gs[:, 0:8], mods[:, l * 72 + s * 24 + 8:l * 72 + s * 24 + 16], 1.0, None, ALU.add, None, ada["tok"][l])
        tg = tt(V, gs[:, 0:8], gs[:, 0:8], pc(f"ng{l}{s}", 0, 8), ALU.mult, tg)
        t_n = []
        for k in range(8):
            t1 = stt(H3[:, k, :], X3[:, k, :], gs[:, k:k + 1], rsb[:, :], ALU.mult, ALU.mult, t, tg, ph)
            if src is None:
                t_n.append(act(H3[:, k, :], H3[:, k, :], ACT.Identity, t1, bias=mod(l, s, 0, k)))
            else:
                t_n.append(act(Hh[:, k, :], H3[:, k, :], ACT.Identity, t1, ph, bias=mod(l, s, 0, k)))
        if src is None:
            return t_n[-1]
        return [stt(Hl[:, k, :], H3[:, k, :], mod(l, s, 0, k), Hh[:, k, :], ALU.add, ALU.subtract, t_n[k], ph)
                for k in range(8)]

    def ffn(l, s, w):
        def unit(I, u):
            wi, wo = np.asarray(I["ffn_w_in_2"])[l, w], np.asarray(I["ffn_w_out_2"])[l, w]
            return np.concatenate([ktiles(wi[:, u * 128:(u + 1) * 128]),
                                   ktiles(wi[:, 2816 + u * 128:2816 + (u + 1) * 128]), wo[u * 128:(u + 1) * 128]], 1)

        src = Units(unit)
        t_h = adaln(l, s, src)
        th = ts(V, gs[:, 8:16], mods[:, l * 72 + s * 24 + 16:l * 72 + s * 24 + 24], 0.5, None, ALU.mult, None, V.last)
        state["x"] = glu(22, src, t_h, lambda m, ps, t: stt(
            X3[:, m, :], ps, gs[:, 8 + m:9 + m], X3[:, m, :], ALU.mult, ALU.add, t, th))

    def swa(l):
        t_h = adaln(l, 1)
        ph = now()
        qT, kT, vv = v3(wk, 0, 8, T), v3(wk, 2048, 4, T), v3(wk, 3072, 2, T)
        oT = v3(wk, 3584, 8, T)
        W = lambda a, b: (lambda I: np.asarray(I["sw_w_qkv_2"])[0][:, a:b])
        lin(512, D, lambda I, n0, n1: dup_heads(W(1024, 1280)(I))[:, n0:n1], H3, t_h,
            lambda m, ps, t: cp(A, kT[:, m, :], ps, t, ph))
        head_norm(kT, kT, 4, T, pc("sw_k"), 1.0, A.last)
        s, wt, wtok = rg.get(128, 2048, lambda I: ktiles(W(1280, 1536)(I)))
        t = tokmajor(wt.rearrange("p (k n) -> p k n", k=8), 256, wtok, t_h,
                     lambda tb, ps, t: cp(A, vv[:, tb, :], ps, t, ph))
        rg.put(s, t)
        lin(D, D, lambda I, n0, n1: W(n0, n1)(I), H3, t_h, lambda m, ps, t: cp(A, qT[:, m, :], ps, t, ph))
        head_norm(qT, qT, 8, T, pc("sw_q"), 0.125, A.last)
        t_all = now()
        units = []
        for h in range(16):
            g, r = h // 4, slice(64 * (h % 2), 64 * (h % 2) + 64)
            units.append(dict(h=h, q=qT[r, h // 2, :], k=kT[r, g, :], bias=C("swa"), btok=loaded, tok=t_all,
                              sink=pc("sinks", h), gate=None, first=True, last=True, extra=[],
                              v=lambda kb, g=g: vv[:, kb, g * 64:(g + 1) * 64]))
        attention(units, 5632, lambda m, ps, t: cp(V, oT[:, m, :], ps, t, ph))
        lin(D, D, lambda I, n0, n1: np.asarray(I["sw_w_o_2"])[0][:, n0:n1], oT, V.last, gated_residual(l, 1))
        state["x"] = V.last

    def mamba(l):
        t_h = adaln(l, 1)
        ph = now()
        o = 0

        def take(n):
            nonlocal o
            o += n
            return o - n

        zT, xsT = v3(wk, take(4096), 16, T), v3(wk, take(4096), 16, T)
        BT, CT = v3(wk, take(2048), 8, T), v3(wk, take(2048), 8, T)
        Xt = v3(wk, take(4096), 2, 2048)
        xp = [wk[:, take(260):o] for _ in range(3)]
        acc = [wk[:, take(256):o] for _ in range(3)]
        cbm = [wk[:, take(384):o] for _ in range(2)]
        Gb = [wk[:, take(384):o] for _ in range(3)]
        sm = [wk[0:32, take(256):o] for _ in range(5)]
        dtT, acT = v3(wk, take(64), 2, 32), v3(wk, take(64), 2, 32)
        eA = wk[0:32, take(1):o]
        W = lambda a, b: (lambda I: np.asarray(I["mb_w_in_2"])[0][:, a:b])

        s, wt, wtok = rg.get(128, 256, lambda I: ktiles(W(6144, 6176)(I)))
        w = wt.rearrange("p (k n) -> p k n", k=8)
        i, ps, fr = bk.get()
        for k in range(8):
            t = mm(ps[0:32, 0:T], w[:, k, :], H3[:, k, :], k == 0, k == 7, fr, wtok, t_h, inc=(k == 7))
        rg.put(s, t)
        v, e, r, s2, p = sm
        t = ts(V, v, ps[0:32, 0:T], pc("dt_bias", 0, 1, 32), None, ALU.add, None, t, ph)
        bk.put(i, t)
        t = act(e, v, ACT.Abs, t)
        t = act(e, e, ACT.Exp, t, scale=-1.0)
        t = ts(V, r, e, 2.0, None, ALU.add, None, t)
        t = recip(r, r, t)
        t = tt(V, e, e, r, ALU.mult, t)
        t = tt(V, s2, e, e, ALU.mult, t)
        t = ts(V, p, s2, 1.0 / 19, None, ALU.mult, None, t)
        for n in (17, 15, 13, 11, 9, 7, 5, 3):
            t = stt(p, p, 1.0 / n, s2, ALU.add, ALU.mult, t)
        t = stt(p, p, 1.0, e, ALU.add, ALU.mult, t)
        t = ts(V, p, p, 2.0, None, ALU.mult, None, t)
        t = stt(v, v, 0.0, p, ALU.max, ALU.add, t)
        ta = act(eA, pc("A_log", 0, 1, 32), ACT.Exp, ph)
        t = ts(V, e, v, eA, -1.0, ALU.mult, ALU.mult, t, ta)
        t = V(lambda q: q.tensor_tensor_scan(r, ones[0:32, 0:T], e, 0.0, ALU.mult, ALU.add), t)
        dt, acum = v, r
        for src, dst in ((dt, dtT), (acum, acT)):
            i, ps, fr = bk.get()
            for b in range(2):
                tk = tp(ps[:, b * 32:(b + 1) * 32], src[:, b * 128:(b + 1) * 128], fr, t, inc=(b == 1))
            tl = cp(V, dst, ps[:, 0:64].rearrange("p (b n) -> p b n", b=2), tk)
            bk.put(i, tl)
        t_dt = V.last

        for j in range(3):
            V(lambda q, j=j: q.memset(xp[j][:, 0:3], 0.0), ph)
        t_xp = V.last
        cfree = [ph, ph, ph]
        afree = [ph, ph, ph]
        n_conv = [0]

        def conv(dst, ct):
            def evac(m, ps, t):
                c = ct + m
                j = n_conv[0] % 3
                n_conv[0] += 1
                x, a = xp[j], acc[j]
                t1 = act(x[:, 3:259], ps, ACT.Copy, t, cfree[j], t_xp)
                t2 = ts(V, a, x[:, 0:T], pc("conv0", c), pc("conv_b", c), ALU.mult, ALU.add, t1, afree[j])
                for k in (1, 2, 3):
                    t2 = stt(a, x[:, k:k + T], pc(f"conv{k}", c), a, ALU.mult, ALU.add, t2)
                cfree[j] = t2
                afree[j] = act(dst[:, m, :], a, ACT.Silu, t2, ph)
                return t1
            return evac

        lin(2048, D, lambda I, n0, n1: W(2048 + n0, 2048 + n1)(I), H3, t_h, conv(xsT, 0))
        lin(1024, D, lambda I, n0, n1: W(4096 + n0, 4096 + n1)(I), H3, t_h, conv(BT, 16))
        lin(1024, D, lambda I, n0, n1: W(5120 + n0, 5120 + n1)(I), H3, t_h, conv(CT, 24))
        t_c = A.last
        lin(2048, D, lambda I, n0, n1: W(n0, n1)(I), H3, t_h, lambda m, ps, t: act(zT[:, m, :], ps, ACT.Silu, t, ph))
        t_z = A.last
        for m in range(16):
            i, ps, fr = bk.get()
            for b in range(2):
                tk = tp(ps[:, b * 128:(b + 1) * 128], xsT[:, m, b * 128:(b + 1) * 128], fr, t_c, inc=(b == 1))
            for b in range(2):
                tl = tt(V, Xt[:, b, m * 128:(m + 1) * 128].rearrange("p (h d) -> p h d", h=2),
                        ps[:, b * 128:(b + 1) * 128].rearrange("p (h d) -> p h d", h=2),
                        dtT[:, b, 2 * m:2 * m + 2].unsqueeze(2).to_broadcast([128, 2, 64]), ALU.mult, tk, t_dt, ph)
            bk.put(i, tl)
        t_X = V.last

        bk.use(range(2, 8))
        gfree, mfree = [ph] * 3, [ph] * 2
        heads = []

        def group(g):
            i, ps, fr = bk.get()
            mm(ps[:, 0:256], BT[:, g, 0:128], CT[:, g, :], True, True, fr, t_c)
            t = mm(ps[:, 256:384], BT[:, g, 128:256], CT[:, g, 128:256], True, True, inc=True)
            t = tt(V, cbm[g % 2], ps[:, 0:384], C("S384"), ALU.mult, t, mfree[g % 2])
            bk.put(i, t)

        def weights(h):
            g = h // 4
            i, ps, fr = bk.get()
            sel = cst[0:32, ccol["ident"][0] + h:ccol["ident"][0] + h + 1].to_broadcast([32, 128])
            t = mm(ps[:, 0:T], sel, acum, True, True, fr, t_dt, inc=True)
            b = Gb[h % 3]
            ts(V, b[:, 0:256], ps[:, 0:256], acT[:, 0, h:h + 1], 0.0, ALU.subtract, ALU.min, t, gfree[h % 3])
            t = ts(V, b[:, 256:384], ps[:, 128:256], acT[:, 1, h:h + 1], 0.0, ALU.subtract, ALU.min, t)
            bk.put(i, t)
            t = act(b, b, ACT.Exp, t)
            t = tt(V, b, b, cbm[g % 2], ALU.mult, t)
            mfree[g % 2] = t
            heads.append(t)

        def output(h):
            m, hp = h // 2, h % 2
            ob = pb[m % 2]
            b = Gb[h % 3]
            mm(ob[64 * hp:64 * hp + 64, 0:T], Xt[:, 0, h * 64:(h + 1) * 64], b[:, 0:256], True, False,
               bk.free[m % 2], heads[h], t_X, skip=True)
            t = mm(ob[64 * hp:64 * hp + 64, 128:256], Xt[:, 1, h * 64:(h + 1) * 64], b[:, 256:384], False, True,
                   inc=True, skip=True)
            gfree[h % 3] = t
            if hp == 1:
                t = stt(xsT[:, m, :], xsT[:, m, :], pc("mb_D", m), ob[:, 0:T], ALU.mult, ALU.add, t)
                bk.put(m % 2, t)
                tt(G, xsT[:, m, :], xsT[:, m, :], zT[:, m, :], ALU.mult, t, t_z)

        for h in range(33):
            if h < 32:
                if h % 4 == 0:
                    group(h // 4)
                weights(h)
            if h >= 1:
                output(h - 1)
        bk.use(range(8))
        t_y = G.last

        t1 = act(wk[:, 0:4096], wk[:, 4096:8192], ACT.Square, t_y)
        i, ps, fr = bk.get()
        sel8 = lambda g: selg[:, g * 8:(g + 1) * 8]
        for m in range(16):
            t = mm(ps[0:8, 0:T], sel8(m // 2), zT[:, m, :], m == 0, m == 15, fr, t1, t_selg, inc=(m == 15))
        t0 = ts(V, nv[0:8, :], ps[0:8, 0:T], 1.0 / 256, 1e-6, ALU.mult, ALU.add, t, V.last)
        bk.put(i, t0)
        t = rsqrt_of(hr[0:8, :], nv[0:8, :], nm[0:8, :], nt[0:8, :])
        for g in range(8):
            i, ps, fr = bk.get()
            sel = cst[0:8, ccol["ident"][0] + g:ccol["ident"][0] + g + 1].to_broadcast([8, 128])
            tb = mm(ps[:, 0:T], sel, hr[0:8, :], True, True, fr, t, inc=True)
            for m in (2 * g, 2 * g + 1):
                tl = stt(xsT[:, m, :], xsT[:, m, :], pc("mb_g", m), ps[:, 0:T], ALU.mult, ALU.mult, tb, t_y, t1)
            bk.put(i, tl)
        lin(D, 2048, lambda I, n0, n1: np.asarray(I["mb_w_out_2"])[0][:, n0:n1], xsT, V.last, gated_residual(l, 1))
        state["x"] = V.last

    V(lambda e: e.memset(selg[:, :], 0.0))
    t_selg = V.last
    for k in range(8):
        V(lambda e, k=k: e.memset(selg[:, k * 9:k * 9 + 1], 1.0), t_selg)
    t_selg = V.last

    def rwkv(l, j):
        t_h = adaln(l, 1)
        ph = now()
        o = 0

        def take(n):
            nonlocal o
            o += n
            return o - n

        offs = {n: take(2048) for n in ("r", "k", "v", "kk", "a", "lw", "c")}
        fl = {n: wk[:, a:a + 2048] for n, a in offs.items()}
        r3, k3, v3_, kk3, a3, lw3, c3 = (v3(wk, offs[n], 8, T) for n in ("r", "k", "v", "kk", "a", "lw", "c"))
        lo = wk[:, take(512):o].rearrange("p (k n) -> p k n", n=T)
        base = o
        dx3 = c3
        W = lambda n: (lambda I, a, b: np.asarray(I[n])[j][:, a:b])

        def shift_diff(ph):
            for k in range(8):
                tt(V, dx3[:, k, 1:T], H3[:, k, 0:T - 1], H3[:, k, 1:T], ALU.subtract, t_h, ph)
                t = ts(V, dx3[:, k, 0:1], H3[:, k, 0:1], -1.0, None, ALU.mult, None)
            return t

        def mix(dst, m, tok):
            for k in range(8):
                t = stt(dst[:, k, :], dx3[:, k, :], pc(f"mu{j}{m}", k), H3[:, k, :], ALU.mult, ALU.add, t_dx, tok)
            return t

        def lora(rank, w1, w2, src, tok, func, evac):
            parts = [(a, min(128, rank - a)) for a in range(0, rank, 128)]
            s, wt, wtok = rg.get(128, 8 * rank, lambda I: ktiles(w1(I)))
            w = wt.rearrange("p (k n) -> p k n", k=8)
            before = now()
            for n, (a, z) in enumerate(parts):
                i, ps, fr = bk.get()
                for k in range(8):
                    t = mm(ps[0:z, 0:T], w[:, k, a:a + z], src[:, k, :], k == 0, k == 7, fr, wtok, tok, inc=(k == 7))
                te = act(lo[0:z, n, :], ps[0:z, 0:T], func, t, before)
                bk.put(i, te)
            rg.put(s, t)
            ws = []
            for n, (a, z) in enumerate(parts):
                ws.append(rg.get(z, 1024, lambda I, a=a, z=z: np.asarray(w2(I))[a:a + z]))
            for m in range(8):
                i, ps, fr = bk.get()
                for n, (a, z) in enumerate(parts):
                    t = mm(ps[:, 0:T], ws[n][1][:, m * 128:(m + 1) * 128], lo[0:z, n, :], n == 0, n == len(parts) - 1,
                           fr, ws[n][2], te, inc=(n == len(parts) - 1))
                bk.put(i, evac(m, ps[:, 0:T], t))
            for s, _, _ in ws:
                rg.put(s, t)

        t_dx = shift_diff(ph)
        xm = [Q3, lw3]
        xfree = [ph, ph]

        for n, (m, dst) in enumerate(((0, r3), (2, k3), (3, v3_))):
            t = mix(xm[n % 2], m, xfree[n % 2])
            lin(D, D, lambda I, n0, n1, n=n: np.asarray(I["rw_w_rkv_2"])[j, n][:, n0:n1], xm[n % 2], t,
                lambda m, ps, t, dst=dst: cp(A, dst[:, m, :], ps, t, ph))
            xfree[n % 2] = PE.last
        if j == 0:
            t_v = cp(G, vfirst[:, :], fl["v"], A.last)
        else:
            t_vl = A.last

            def mix_v(m, ps, t):
                t1 = act(kk3[:, m, :], ps, ACT.Sigmoid, t, ph, bias=pc("v01", m))
                t2 = tt(V, a3[:, m, :], vfirst[:, m * T:(m + 1) * T], v3_[:, m, :], ALU.subtract, t_vl, ph)
                t2 = tt(V, a3[:, m, :], a3[:, m, :], kk3[:, m, :], ALU.mult, t1, t2)
                tt(V, v3_[:, m, :], v3_[:, m, :], a3[:, m, :], ALU.add, t2)
                return t1

            lora(32, lambda I: np.asarray(I["rw_v1_2"])[0], lambda I: np.asarray(I["rw_v2_2"])[0], xm[0], t,
                 ACT.Copy, mix_v)
            xfree[0] = PE.last
            t_v = V.last
        ph2 = now()
        t = mix(xm[1], 4, xfree[1])
        lora(64, lambda I: np.asarray(I["rw_a1_2"])[j], lambda I: np.asarray(I["rw_a2_2"])[j], xm[1], t, ACT.Copy,
             lambda m, ps, t: act(a3[:, m, :], ps, ACT.Sigmoid, t, ph2, bias=pc(f"a0{j}", m)))
        xfree[1] = PE.last
        t = mix(xm[0], 1, xfree[0])
        ph2 = now()
        lora(64, lambda I: np.asarray(I["rw_w1_2"])[j], lambda I: np.asarray(I["rw_w2_2"])[j], xm[0], t, ACT.Tanh,
             lambda m, ps, t: act(lw3[:, m, :], ps, ACT.Sigmoid, t, ph2, bias=pc(f"w0{j}", m)))
        t = ts(V, fl["lw"], fl["lw"], -float(np.exp(-0.5)), None, ALU.mult, None, A.last)
        for k in range(8):
            V(lambda q, k=k: q.tensor_tensor_scan(c3[:, k, :], C("reset"), lw3[:, k, :], 0.0, ALU.mult, ALU.add), t, now())

        ph3 = now()
        for k in range(8):
            t1 = ts(V, kk3[:, k, :], k3[:, k, :], pc(f"k_k{j}", k), None, ALU.mult, None, ph3)
        t1 = act(sq[:, :], fl["kk"], ACT.Square, t1, ph3)
        i, ps, t = head_rows(Q3, 8, T, t1)
        t0 = ts(V, nv[0:16, :], ps, 1e-24, None, ALU.max, None, t, V.last)
        bk.put(i, t0)
        t = rsqrt_of(hr[:, :], nv[0:16, :], nm[0:16, :], nt[0:16, :])
        for k in range(8):
            i, ps, tb = head_bcast(hr[:, :], k, T, t)
            tl = tt(V, kk3[:, k, :], kk3[:, k, :], ps, ALU.mult, tb)
            bk.put(i, tl)
        t_kk = V.last
        for k in range(8):
            t1 = ts(V, Q3[:, k, :], a3[:, k, :], -1.0, pc(f"k_a{j}", k), ALU.add, ALU.mult, now())
        t1 = stt(fl["k"], sq[:, :], 1.0, fl["k"], ALU.add, ALU.mult, t1)
        t1 = tt(V, sq[:, :], fl["r"], fl["k"], ALU.mult, t1)
        for k in range(8):
            t2 = ts(V, Q3[:, k, :], Q3[:, k, :], pc(f"r_k{j}", k), None, ALU.mult, None, t1)
        i, ps, t = head_rows(Q3, 8, T, t2)
        t_bs = cp(V, bsum[:, :], ps, t, now())
        bk.put(i, t_bs)
        t1 = tt(V, fl["a"], fl["a"], fl["kk"], ALU.mult, t_kk, V.last)
        t2 = tt(V, fl["lw"], fl["c"], fl["lw"], ALU.subtract, t1)
        t3 = act(fl["lw"], fl["lw"], ACT.Exp, t2)
        t_at = stt(fl["kk"], fl["kk"], -1.0, fl["lw"], ALU.mult, ALU.mult, t3)
        te = act(sq[:, :], fl["c"], ACT.Exp, t2, now())
        t1 = tt(V, fl["r"], fl["r"], sq[:, :], ALU.mult, te, V.last)
        t1 = cp(V, dl[:, :], sq[:, :].rearrange("p (n c) -> p n c", c=64)[:, :, 63], te)
        te = act(fl["lw"], fl["c"], ACT.Exp, t_at, scale=-1.0)
        t1 = tt(V, fl["a"], fl["a"], fl["lw"], ALU.mult, te)
        t1 = tt(V, fl["k"], fl["k"], fl["lw"], ALU.mult, te)
        t_in = now()

        o = base
        names = ["M16", "M16T", "Mo32", "Mo32T", "Mo64", "ArbT", "ArkT", "AakT", "M2", "M2T", "M4", "M4T", "TI", "TT"]
        mat = {n: wk[:, take(512):o].rearrange("p (u n) -> p u n", u=4) for n in names}
        Bt, Kt, Vt = (wk[:, take(256):o].rearrange("p (b n) -> p b n", b=2) for _ in range(3))
        W0, Ub = (wk[:, take(256):o].rearrange("p (b n) -> p b n", b=2) for _ in range(2))
        Pb, Pd = wk[:, take(128):o], wk[:, take(64):o]
        t_pb = V(lambda e: e.memset(Pb, 0.0), t_in)
        t_u0 = V(lambda e: e.memset(Ub, 0.0), t_in)
        y3 = r3
        uns = [(hp, hf) for hp in range(2) for hf in range(2)]
        mask = lambda n: C(n).unsqueeze(1).to_broadcast([128, 2, 128])
        tok = {n: t_in for n in names}
        idm = ident.unsqueeze(1).to_broadcast([128, 4, 128])

        def product(l_, r_, *w):
            i, ps, fr = bk.get()
            for u in range(4):
                t = mm(ps[:, u * 128:(u + 1) * 128], l_(u), r_(u), True, True, fr, w, inc=(u == 3))
            return i, ps[:, :].rearrange("p (u n) -> p u n", u=4), t

        def of(n):
            return lambda u: mat[n][:, u, :]

        free = t_in
        for m in range(8):
            def fm(x3):
                return lambda u: x3[64 * uns[u][0]:64 * uns[u][0] + 64, m, uns[u][1] * 128:(uns[u][1] + 1) * 128]
            at_, bt_, kt_, rt_ = fm(kk3), fm(a3), fm(k3), fm(r3)

            def by_head(l_, r_, outs):
                for hp in range(2):
                    i, ps, fr = bk.get()
                    for hf in range(2):
                        u = 2 * hp + hf
                        t = mm(ps[:, hf * 128:(hf + 1) * 128], l_(u), r_(u), True, True, fr, t_in, inc=(hf == 1))
                    p3 = ps[:, 0:256].rearrange("p (u n) -> p u n", u=2)
                    for n, mk in outs:
                        t1 = tt(V, mat[n][:, 2 * hp:2 * hp + 2, :], p3, mask(mk), ALU.mult, t, free)
                    bk.put(i, t1)
                return t1

            by_head(at_, bt_, (("M16", "L16"), ("Mo32", "Lo32"), ("Mo64", "Lo64")))
            t_m = by_head(bt_, at_, (("M16T", "U16"), ("Mo32T", "Uo32")))
            tt(G, mat["TI"], mat["M16"], idm, ALU.add, t_m, free)
            t_t = tt(G, mat["TT"], mat["M16T"], idm, ALU.add, t_m, free)
            by_head(kt_, at_, (("AakT", "U64"),))
            by_head(bt_, rt_, (("ArbT", "Ui64"),))
            t_A = by_head(kt_, rt_, (("ArkT", "Ui64"),))
            for x3, dst in ((a3, Bt), (k3, Kt), (v3_, Vt)):
                i, ps, fr = bk.get()
                for b in range(2):
                    t = tp(ps[:, b * 128:(b + 1) * 128], x3[:, m, b * 128:(b + 1) * 128], fr, t_in, t_v, inc=(b == 1))
                t1 = cp(A, dst, ps[:, 0:256].rearrange("p (b n) -> p b n", b=2), t, free)
                bk.put(i, t1)
            t_tok = t1
            i, ps, t = product(of("M16T"), of("M16"), t_m)
            t2 = cp(A, mat["M2"], ps, t, free)
            bk.put(i, t2)
            i, ps, t = product(of("M16"), of("M16T"), t_m)
            t2 = cp(A, mat["M2T"], ps, t, free)
            bk.put(i, t2)

            def grow(n, *w):
                i1, p1, ta = product(of(n), of("TT"), *w)
                i2, p2, tb = product(of("TT"), of(n), *w)
                tt(V, mat["TT"], mat["TT"], p1, ALU.add, ta, tb, t_t)
                bk.put(i1, V.last)
                tt(V, mat["TI"], mat["TI"], p2, ALU.add, tb)
                bk.put(i2, V.last)
                return V.last

            i, ps, t = product(of("M2T"), of("M2"), t2)
            t4 = cp(A, mat["M4"], ps, t, free)
            bk.put(i, t4)
            i, ps, t = product(of("M2"), of("M2T"), t2)
            t4 = cp(A, mat["M4T"], ps, t, free)
            bk.put(i, t4)
            tg = grow("M2", t2, t_t)
            i, ps, t = product(of("M4T"), of("M4"), t4)
            t8 = cp(A, mat["M2"], ps, t, tg)
            bk.put(i, t8)
            tg = grow("M4", t4, tg)
            tg = grow("M2", t8, tg)
            i1, p1, ta = product(of("Mo32T"), of("TI"), tg)
            t1 = cp(A, mat["M4"], p1, ta, tg)
            bk.put(i1, t1)
            i1, p1, ta = product(of("Mo32"), of("TT"), tg)
            t1 = cp(A, mat["M4T"], p1, ta, tg)
            bk.put(i1, t1)
            i1, p1, ta = product(of("TT"), of("M4"), t1)
            i2, p2, tb = product(of("TI"), of("M4T"), t1)
            tt(V, mat["TI"], mat["TI"], p1, ALU.add, ta, tb)
            bk.put(i1, V.last)
            tg = tt(V, mat["TT"], mat["TT"], p2, ALU.add, tb)
            bk.put(i2, tg)
            i1, p1, ta = product(of("Mo64"), of("TT"), tg)
            t1 = cp(A, mat["M4"], p1, ta, tg)
            bk.put(i1, t1)
            i1, p1, ta = product(of("TI"), of("M4"), t1)
            tg = tt(V, mat["TT"], mat["TT"], p1, ALU.add, ta)
            bk.put(i1, tg)

            i, ps, fr = bk.get()
            for u, (hp, hf) in enumerate(uns):
                t = mm(ps[:, hf * 128 + hp * 64:hf * 128 + hp * 64 + 64], mat["AakT"][:, u, :], Vt[:, hf, 64 * hp:64 * hp + 64],
                       True, True, fr, t_A, t_tok, inc=(u == 3))
            tw0 = cp(V, W0[:, :, :], ps[:, 0:256].rearrange("p (b n) -> p b n", b=2), t, free)
            bk.put(i, tw0)
            iy, py, fry = bk.get()
            bk.use([x for x in range(8) if x != iy])
            for u, (hp, hf) in enumerate(uns):
                mm(py[64 * hp:64 * hp + 64, hf * 128:(hf + 1) * 128], Vt[:, hf, 64 * hp:64 * hp + 64], mat["ArkT"][:, u, :],
                   hf == 0, False, fry, t_A, t_tok, skip=True)
            t_P = t_Pd = None
            for c in range(4):
                hf, c2 = divmod(c, 2)
                rs_ = slice(64 * c2, 64 * c2 + 64)
                cs_ = slice(c * 64, (c + 1) * 64)
                if c:
                    i, ps, fr = bk.get()
                    t = mm(ps[rs_, 0:128], kk3[:, m, cs_], Pb[:, :], True, True, fr, t_P, inc=True)
                    tw = tt(V, W0[rs_, hf, :], ps[rs_, 0:128], W0[rs_, hf, :], ALU.add, t, tw0)
                    bk.put(i, tw)
                    mm(py[:, cs_], Pb[:, :], r3[:, m, cs_], False, False, fry, t_P, skip=True)
                else:
                    tw = tw0
                i, ps, fr = bk.get()
                for hp in range(2):
                    t = mm(ps[rs_, hp * 64:(hp + 1) * 64], mat["TT"][:, hp * 2 + hf, rs_], W0[:, hf, hp * 64:(hp + 1) * 64],
                           True, True, fr, tw, tg, inc=(hp == 1))
                tu = cp(V, Ub[rs_, hf, :], ps[rs_, 0:128], t, free, t_u0)
                bk.put(i, tu)
                for hp in range(2):
                    hs = slice(64 * hp, 64 * hp + 64)
                    t_y = mm(py[hs, cs_], Ub[:, hf, hs], mat["ArbT"][:, hp * 2 + hf, rs_], False, c == 3, tu, t_A,
                             inc=(hp == 1), skip=True)
                if c < 3:
                    i, ps, fr = bk.get()
                    for hp in range(2):
                        hs = slice(64 * hp, 64 * hp + 64)
                        mm(ps[hs, 0:64], Bt[rs_, hf, hs], Ub[rs_, hf, hs], True, False, fr, tu, t_tok, skip=True)
                        t = mm(ps[hs, 0:64], Kt[rs_, hf, hs], Vt[rs_, hf, hs], False, True, inc=(hp == 1), skip=True)
                    for hp in range(2):
                        hs = slice(64 * hp, 64 * hp + 64)
                        d = dl[hs, m * 4 + c:m * 4 + c + 1]
                        if c == 0:
                            t_P = ts(V, Pb[hs, hs], ps[hs, 0:64], d, None, ALU.mult, None, t, free, t_pb)
                        else:
                            t_P = stt(Pb[hs, hs], ps[hs, 0:64], d, Pd[hs, :], ALU.mult, ALU.add, t, t_y, t_Pd)
                    bk.put(i, t_P)
                    if c < 2:
                        for hp in range(2):
                            hs = slice(64 * hp, 64 * hp + 64)
                            t_Pd = ts(V, Pd[hs, :], Pb[hs, hs], dl[hs, m * 4 + c + 1:m * 4 + c + 2], None, ALU.mult, None, t_P)
            t1 = cp(V, y3[:, m, :], py[:, 0:T], t_y)
            bk.put(iy, t1)
            bk.use(range(8))
            free = now()

        t_y = now()
        for m in range(8):
            i, ps, fr = bk.get()
            t = mm(ps[:, 0:T], C("blk64"), y3[:, m, :], True, True, fr, t_y, inc=True)
            t1 = stt(y3[:, m, :], ps[:, 0:T], -1.0 / 64, y3[:, m, :], ALU.mult, ALU.add, t)
            bk.put(i, t1)
        t1 = act(sq[:, :], fl["r"], ACT.Square, V.last, t_y)
        i, ps, t = head_rows(Q3, 8, T, t1)
        t0 = ts(V, nv[0:16, :], ps, 1.0 / 64, 64e-5, ALU.mult, ALU.add, t, V.last)
        bk.put(i, t0)
        t = rsqrt_of(hr[:, :], nv[0:16, :], nm[0:16, :], nt[0:16, :])
        for k in range(8):
            i, ps, tb = head_bcast(hr[:, :], k, T, t)
            tl = stt(y3[:, k, :], y3[:, k, :], pc(f"ln_w{j}", k), ps, ALU.mult, ALU.mult, tb)
            bk.put(i, tl)
            i, ps, tb = head_bcast(bsum[:, :], k, T, t_bs)
            t2 = tt(V, v3_[:, k, :], v3_[:, k, :], ps, ALU.mult, tb, t_y)
            bk.put(i, t2)
            t2 = stt(y3[:, k, :], y3[:, k, :], pc(f"ln_b{j}", k), v3_[:, k, :], ALU.add, ALU.add, t2)
        t_o = V.last
        t_dx = shift_diff(now())
        t = mix(Q3, 5, now())

        def gate(m, ps, t):
            return tt(V, y3[:, m, :], y3[:, m, :], ps, ALU.mult, t, t_o)

        lora(160, lambda I: np.asarray(I["rw_g1_2"])[j], lambda I: np.asarray(I["rw_g2_2"])[j], Q3, t, ACT.Sigmoid, gate)
        lin(D, D, lambda I, n0, n1: np.asarray(I["rw_w_o_2"])[j][:, n0:n1], y3, V.last, gated_residual(l, 1))
        state["x"] = V.last

    phases = [nsa, lambda: moe(0), lambda: ple(0), moba, lambda: moe(1), lambda: ple(1)]

    def make(l, mixer):
        return [lambda: ffn(l, 0, 0), mixer, lambda: ffn(l, 2, 1)]

    phases += make(0, lambda: rwkv(0, 0)) + make(1, lambda: mamba(1)) + make(2, lambda: swa(2)) + make(3, lambda: rwkv(3, 1))
    for n, phase in enumerate(phases):
        if stop is not None and n not in stop:
            continue
        phase()

    d_x = nc.dram_tensor("xT_in", [128, 2048], F32, kind="ExternalInput").ap()
    d_p = nc.dram_tensor("params", [128, L.cols], F32, kind="ExternalInput").ap()
    d_c = nc.dram_tensor("consts", [128, NC], F32, kind="ExternalInput").ap()
    d_w = nc.dram_tensor("weights", [L.size], F32, kind="ExternalInput").ap()
    d_o = nc.dram_tensor("xT_out", [128, 2048], F32, kind="ExternalOutput").ap()

    def start(e):
        e.dma_start(xT[:, :], d_x).then_inc(s_in, 16)
        e.dma_start(prm[:, :], d_p).then_inc(s_in, 16)
        return e.dma_start(cst[:, :], d_c).then_inc(s_in, 16)

    SP(start, inc=False)
    for off, rows, cols, dst, sm_, fr in loads:
        src = d_w[off:off + rows * cols].rearrange("(p n) -> p n", p=rows)
        SP(lambda e, dst=dst, src=src, sm_=sm_: e.dma_start(dst, src).then_inc(sm_, 16), fr, inc=False)
    SP(lambda e: e.dma_start(d_o, xT[:, :]).then_inc(s_out, 16), state["x"], inc=False)

    with ctx, nc.Block() as block:
        @block.sync
        def _(e):
            SP.emit(e)
            e.wait_ge(s_out, 16)

        @block.tensor
        def _(e):
            e.wait_ge(s_in, 48)
            PE.emit(e)

        @block.vector
        def _(e):
            e.wait_ge(s_in, 48)
            V.emit(e)

        @block.scalar
        def _(e):
            e.wait_ge(s_in, 48)
            A.emit(e)

        @block.gpsimd
        def _(e):
            e.wait_ge(s_in, 48)
            G.emit(e)

    return L, consts


STOP = None


def kernel(**inputs):
    import concourse.bacc as bacc
    from concourse.bass_utils import run_bass_kernel_spmd as run

    nc = bacc.Bacc("TRN2", target_bir_lowering=False, num_devices=1)
    L, consts = build_program(nc, STOP)
    inputs = {k: np.asarray(v) for k, v in inputs.items()}
    small, flat = L.fill(inputs)
    maps = {"xT_in": np.ascontiguousarray(ktiles(inputs["x"][0].T)), "params": small, "consts": consts, "weights": flat}
    r = run(nc, [maps], core_ids=[0])
    o = np.asarray(r.results[0]["xT_out"])
    return np.ascontiguousarray(o.reshape(128, 8, 256).transpose(2, 1, 0).reshape(1, 256, 1024))
```

```python
from contextlib import ExitStack

import numpy as np

import concourse.bass as bass
import concourse.mybir as mybir
from concourse.alu_op_type import AluOpType as ALU

F32 = mybir.dt.float32
FR = mybir.dt.float32r
I32 = mybir.dt.int32
ACT = mybir.ActivationFunctionType
AX = mybir.AxisListType

T = 256
D = 1024
KD = 8
SLOT = 3072
NSLOT = 4
PIECE = 1024
NPIECE = 8
BIG = 1e30
RSQRT_MAGIC = 1597463007.0
SLOPES = [float(2.0 ** (-8.0 * (i + 1) / 16)) for i in range(16)]


class Queue:

    def __init__(self, sem):
        self.sem, self.ops, self.n = sem, [], 0

    def __call__(self, fn, *waits, inc=True):
        self.ops.append((waits, fn, inc))
        self.n += inc
        return (self.sem, self.n)

    @property
    def last(self):
        return (self.sem, self.n)

    def emit(self, eng):
        seen = {}

        def wait(w):
            if w is None:
                return
            if isinstance(w, (list, tuple)) and not (len(w) == 2 and isinstance(w[1], int)):
                for x in w:
                    wait(x)
                return
            sem, value = w
            if value > seen.get(sem.name, 0):
                eng.wait_ge(sem, value)
                seen[sem.name] = value

        for waits, fn, inc in self.ops:
            wait(waits)
            ins = fn(eng)
            if inc:
                ins.then_inc(self.sem, 1)


def shape_constants():
    p = np.arange(128)[:, None]
    f = np.arange(128)[None, :]
    cols, at = {}, 0
    parts = []

    def add(name, a):
        nonlocal at
        a = np.asarray(a, np.float32)
        cols[name] = (at, a.shape[1])
        at += a.shape[1]
        parts.append(a)

    add("ident", p == f)
    add("blk64", (p // 64) == (f // 64))
    q = np.arange(128)[:, None]
    tri = np.where(q >= f, q - f, BIG)
    add("dist", np.concatenate([tri, q + 128 - f, tri], 1))
    add("swa", np.concatenate([np.where(q >= f, 0, -BIG), np.where(f > q, 0, -BIG), np.where(q >= f, 0, -BIG)], 1))
    slopes = np.array(SLOPES)[None, :, None]
    for qb in range(2):
        t = (np.arange(128) + 128 * qb)[:, None, None]
        end = (np.arange(15) * 16 + 31)[None, None, :]
        dist = (t - end).astype(np.float32)
        add(f"cmp{qb}", np.where(dist >= 0, -slopes * dist, -BIG).reshape(128, 240))
    same = lambda n: (p // n) == (f // n)
    add("L16", same(16) & (f < p))
    add("U16", same(16) & (f > p))
    add("Lo32", same(32) & ~same(16) & (f < p))
    add("Uo32", same(32) & ~same(16) & (f > p))
    add("Lo64", same(64) & ~same(32) & (f < p))
    add("U64", same(64) & (f > p))
    add("Ui64", same(64) & (f >= p))
    add("S384", np.concatenate([f >= p, np.ones((128, 128)), f >= p], 1))
    add("half", p == (np.arange(1024)[None, :] // 64))
    add("reset", np.broadcast_to((np.arange(256) % 64 != 0)[None, :], (128, 256)))
    return np.concatenate(parts, 1), cols


def feat(v):
    v = np.asarray(v).reshape(-1, 128)
    return v.T


def twice(v):
    v = np.asarray(v).reshape(64, 1)
    return np.concatenate([v, v], 0)


def ktiles(w):
    w = np.asarray(w)
    k = w.shape[0] // 128
    return w.reshape(k, 128, w.shape[1]).transpose(1, 0, 2).reshape(128, k * w.shape[1])


def dup_heads(w):
    w = np.asarray(w)
    w = w.reshape(w.shape[0], -1, 1, 64)
    return np.concatenate([w, w], 2).reshape(w.shape[0], -1)


class Layout:

    def __init__(self):
        self.params, self.chunks = [], []
        self.cols, self.size = 0, 0

    def param(self, rows, cols, fn):
        at = self.cols
        self.params.append((at, rows, cols, fn))
        self.cols += cols
        return at

    def chunk(self, rows, cols, fn):
        at = self.size
        self.chunks.append((at, rows, cols, fn))
        self.size += rows * cols
        return at

    def fill(self, inputs):
        small = np.zeros((128, self.cols), np.float32)
        for at, rows, cols, fn in self.params:
            a = np.asarray(fn(inputs))
            assert a.shape == (rows, cols), (a.shape, rows, cols)
            small[:rows, at:at + cols] = a
        flat = np.empty((self.size,), np.float32)
        for at, rows, cols, fn in self.chunks:
            a = np.asarray(fn(inputs))
            assert a.shape == (rows, cols), (a.shape, rows, cols)
            flat[at:at + rows * cols] = a.reshape(-1)
        return small, flat


def plan_params(L):
    c = {}

    def vec(name, n, fn):
        c[name] = L.param(128, n, fn)

    for i in range(2):
        vec(f"ln_mix{i}", 8, lambda I, i=i: feat(I["ln_mix"][i]))
        vec(f"ln_ffn{i}", 8, lambda I, i=i: feat(I["ln_ffn"][i]))
        vec(f"ln_ple{i}", 8, lambda I, i=i: feat(I["ln_ple"][i]))
        c[f"moe_b{i}"] = L.param(1, 36, lambda I, i=i: np.concatenate(
            [np.asarray(I["moe_b_group"])[i], np.asarray(I["moe_b_expert"])[i]])[None, :])
        vec(f"moe_w{i}", 288, lambda I, i=i: ktiles(np.concatenate(
            [np.asarray(I["moe_w_group"])[i], np.asarray(I["moe_w_expert"])[i]], 1)))
        vec(f"p{i}", 512, lambda I, i=i: ktiles(np.asarray(I["p"])[i, 0].T))
    vec("kv_norm", 8, lambda I: feat(I["kv_norm"]))
    vec("a_q", 1, lambda I: twice(np.asarray(I["a_q_norm"])[0]))
    for j in range(3):
        vec(f"a_k{j}", 1, lambda I, j=j: twice(np.asarray(I["a_k_norm"])[0, j]))
    vec("k_shared", 1, lambda I: twice(I["k_norm_shared"]))
    vec("b_q", 1, lambda I: twice(np.asarray(I["b_q_norm"])[0]))
    vec("sw_q", 1, lambda I: twice(np.asarray(I["sw_q_norm_2"])[0]))
    vec("sw_k", 1, lambda I: twice(np.asarray(I["sw_k_norm_2"])[0]))
    vec("sinks", 16, lambda I: np.broadcast_to(np.asarray(I["sw_sinks_2"])[0][None, :], (128, 16)))
    for n in ("ck", "cv"):
        vec(f"{n}_pos", 16, lambda I, n=n: np.asarray(I[f"a_{n}_pos"])[0].reshape(16, 128).T)
    vec("c", 8, lambda I: feat(np.asarray(I["c_2"])[0]))
    for l in range(4):
        vec(f"ada_b{l}", 72, lambda I, l=l: feat(np.asarray(I["ada_b_2"])[l]))
        for s in range(3):
            vec(f"ng{l}{s}", 8, lambda I, l=l, s=s: feat(np.asarray(I["norm_g_2"])[l, s]))
    for j in range(2):
        for m in range(6):
            vec(f"mu{j}{m}", 8, lambda I, j=j, m=m: feat(np.asarray(I["rw_mu_2"])[j, m]))
        for n in ("w0", "a0", "k_k", "k_a", "ln_w", "ln_b"):
            vec(f"{n}{j}", 8, lambda I, j=j, n=n: feat(np.asarray(I[f"rw_{n}_2"])[j]))
        vec(f"r_k{j}", 8, lambda I, j=j: feat(np.asarray(I["rw_r_k_2"])[j].reshape(-1)))
    vec("v01", 8, lambda I: feat(np.asarray(I["rw_v0_2"])[0]))
    for k in range(4):
        vec(f"conv{k}", 32, lambda I, k=k: feat(np.asarray(I["mb_conv_w_2"])[0, k]))
    vec("conv_b", 32, lambda I: feat(np.asarray(I["mb_conv_b_2"])[0]))
    vec("mb_g", 16, lambda I: feat(np.asarray(I["mb_norm_g_2"])[0]))
    vec("mb_D", 16, lambda I: feat(np.repeat(np.asarray(I["mb_D_2"])[0], 64)))
    c["dt_bias"] = L.param(32, 1, lambda I: np.asarray(I["mb_dt_bias_2"])[0][:, None])
    c["A_log"] = L.param(32, 1, lambda I: np.asarray(I["mb_A_log_2"])[0][:, None])
    return c


def build_program(nc, stop=None):
    consts, ccol = shape_constants()
    L = Layout()
    pcol = plan_params(L)
    ctx = ExitStack()
    NC = consts.shape[1]

    def sb(name, cols, dt=F32, rows=128):
        return ctx.enter_context(nc.sbuf_tensor(name, [rows, cols], dt))

    def sem(name):
        return ctx.enter_context(nc.semaphore(name))

    PE, V, A, G, SP = (Queue(sem(f"s_{n}")) for n in ("pe", "dve", "act", "pool", "sp"))

    def now():
        return (PE.last, V.last, A.last, G.last)

    xT = sb("xT", 2048)
    hT = sb("hT", 2048)
    sq = sb("sq", 2048)
    vfirst = sb("vfirst", 2048)
    prm = sb("prm", L.cols)
    cst = sb("cst", NC)
    ones = sb("ones", 256)
    mods = sb("mods", 288)
    cact = sb("cact", 8)
    rsb = sb("rsb", 256)
    nv, nm, nt = sb("nv", 256), sb("nm", 256), sb("nt", 256)
    gs = sb("gs", 16)
    ring = sb("ring", NSLOT * SLOT)
    selw, selg = sb("selw", 128), sb("selg", 64)
    hr, bsum = sb("hr", 256, rows=16), sb("bsum", 256, rows=16)
    dl = sb("dl", 32)
    WK = 23 * 1024 - 64
    with nc.sbuf_tensor("wk", [128, WK], F32) as region:
        wk = region
    with ExitStack() as other:
        def sc(name, cols, dt):
            return other.enter_context(nc.sbuf_tensor(name, [128, cols], dt))

        hx = sc("hx", 4096, FR)
        ex = sc("ex", 3 * 512, FR)
        wh, wl = sc("wh", NPIECE * PIECE, FR), sc("wl", NPIECE * PIECE, FR)
        ada_acc = sc("ada_acc", 384, F32)
    pb = [ctx.enter_context(nc.psum_tensor(f"pb{i}", [128, 512], F32)) for i in range(8)]

    def v3(t, c0, n, w):
        return t[:, c0:c0 + n * w].rearrange("p (n w) -> p n w", w=w)

    def C(name, rows=128):
        a, n = ccol[name]
        return cst[0:rows, a:a + n]

    def pc(name, i=0, n=1, rows=128):
        return prm[0:rows, pcol[name] + i:pcol[name] + i + n]

    ident = C("ident")
    X3, H3, Q3 = (v3(t, 0, 8, T) for t in (xT, hT, sq))

    def tt(q, out, a, b, op, *w):
        return q(lambda e: e.tensor_tensor(out, a, b, op), *w)

    def ts(q, out, a, s1, s2, op0, op1, *w):
        if op1 is None:
            return q(lambda e: e.tensor_scalar(out, a, s1, None, op0), *w)
        return q(lambda e: e.tensor_scalar(out, a, s1, s2, op0, op1), *w)

    def stt(out, a, s, b, op0, op1, *w):
        return V(lambda e: e.scalar_tensor_tensor(out=out, in0=a, scalar=s, in1=b, op0=op0, op1=op1), *w)

    def cp(q, out, a, *w):
        if q is A:
            return q(lambda e: e.activation(out, a, ACT.Copy), *w)
        return q(lambda e: e.tensor_copy(out, a), *w)

    def act(out, a, func, *w, bias=0.0, scale=1.0, accum=None):
        return A(lambda e: e.activation(out, a, func, bias=bias, scale=scale, accum_out=accum), *w)

    def mm(out, l, r, start, stop, *w, inc=False, skip=False):
        return PE(lambda e: e.matmul(out, l, r, start=start, stop=stop, skip_group_check=skip), *w, inc=inc)

    def tp(out, a, *w, inc=False):
        n = a.shape[0]
        base = a.base_partition() if callable(a.base_partition) else a.base_partition
        idn = cst[base:base + n, ccol["ident"][0] + base:ccol["ident"][0] + base + n]
        return PE(lambda e: e.transpose(out, a, idn), *w, inc=inc)

    def recip(out, a, *w):
        return V(lambda e: e.reciprocal(out, a), *w)

    def red(out, a, op, *w):
        return V(lambda e: e.tensor_reduce(out, a, AX.X, op), *w)

    class Banks:
        def __init__(self):
            self.free = [None] * 8
            self.ids, self.at = list(range(8)), 0

        def use(self, ids):
            self.ids, self.at = list(ids), 0

        def get(self):
            i = self.ids[self.at % len(self.ids)]
            self.at += 1
            return i, pb[i], self.free[i]

        def put(self, i, *toks):
            self.free[i] = toks

    bk = Banks()

    class Ring:
        def __init__(self):
            self.sems = [sem(f"s_ring{i}") for i in range(NSLOT)]
            self.free = [None] * NSLOT
            self.uses = [0] * NSLOT
            self.at = 0

        def get(self, rows, cols, fn):
            assert cols <= SLOT
            i = self.at % NSLOT
            self.at += 1
            self.uses[i] += 1
            off = L.chunk(rows, cols, fn)
            dst = ring[0:rows, i * SLOT:i * SLOT + cols]
            loads.append((off, rows, cols, dst, self.sems[i], self.free[i]))
            return i, dst, (self.sems[i], 16 * self.uses[i])

        def put(self, i, tok):
            self.free[i] = tok

    loads = []
    rg = Ring()
    s_in, s_out = sem("s_in"), sem("s_out")
    loaded = (s_in, 48)

    def rsqrt(out, src, P, N, mult, add, tok):
        a, b, c = nv[0:P, 0:N], nm[0:P, 0:N], nt[0:P, 0:N]
        t0 = ts(V, a, src, mult, add, ALU.mult, ALU.add, tok, V.last)
        return t0, rsqrt_of(out, a, b, c)

    def rsqrt_of(out, a, b, c):
        ts(V, out.bitcast(I32), a.bitcast(I32), -0.5, RSQRT_MAGIC, ALU.mult, ALU.add, V.last)
        t = ts(V, b, a, -0.5, None, ALU.mult, None, V.last)
        for _ in range(3):
            t = tt(V, c, out, out, ALU.mult, t)
            t = tt(V, c, c, b, ALU.mult, t)
            t = stt(out, c, 1.5, out, ALU.add, ALU.mult, t)
        return t

    def dnorm(between=lambda: None):
        i, ps, fr = bk.get()
        for k in range(KD):
            t = act(Q3[:, k, :], X3[:, k, :], ACT.Square, state["x"][k])
            t = mm(ps[:, 0:T], ones[:, 0:128], Q3[:, k, :], k == 0, k == KD - 1, fr, t, inc=(k == KD - 1))
        between()
        t0, t = rsqrt(rsb[:, :], ps[:, 0:T], 128, T, 1.0 / D, 1e-6, (t, PE.last))
        bk.put(i, t0)
        return t

    def apply_norm(gain, tok, ph):
        for k in range(KD):
            t = stt(H3[:, k, :], X3[:, k, :], gain(k), rsb[:, :], ALU.mult, ALU.mult, tok, ph)
        return t

    def lin(N, K, fn, rhs, rhs_tok, evac, tiles=None):
        KT = K // 128
        per = max(1, SLOT // (KT * 128))
        M = N // 128
        toks = []
        for m0 in range(0, M, per):
            n = min(per, M - m0)
            s, wt, wtok = rg.get(128, KT * n * 128,
                                 lambda I, a=m0 * 128, b=(m0 + n) * 128: ktiles(fn(I, a, b)))
            w = wt.rearrange("p (k n) -> p k n", k=KT)
            for j in range(n):
                i, ps, fr = bk.get()
                for k in range(KT):
                    t = mm(ps[:, 0:T], w[:, k, j * 128:(j + 1) * 128], rhs[:, k, :], k == 0, k == KT - 1,
                           fr, wtok, rhs_tok, inc=(k == KT - 1))
                if j == n - 1:
                    rg.put(s, t)
                toks.append(evac(m0 + j, ps[:, 0:T], t))
                bk.put(i, toks[-1])
        return toks

    def tokmajor(rhs, n, wtok, h_tok, evac):
        t = None
        for tb in range(2):
            i, ps, fr = bk.get()
            for k in range(KD):
                t = mm(ps[:, 0:n], H3[:, k, tb * 128:(tb + 1) * 128], rhs[:, k, :], k == 0, k == KD - 1,
                       fr, wtok, h_tok, inc=(k == KD - 1))
            bk.put(i, evac(tb, ps[:, 0:n], t))
        return t

    def half_select(k):
        return selw[:, k * 16:(k + 1) * 16]

    def head_rows(src, nt_, n, tok):
        i, ps, fr = bk.get()
        for k in range(nt_):
            t = mm(ps[0:16, 0:n], half_select(k), src[:, k, :], k == 0, k == nt_ - 1, fr, tok, inc=(k == nt_ - 1))
        return i, ps[0:2 * nt_, 0:n], t

    def head_bcast(rows, k, n, tok):
        i, ps, fr = bk.get()
        sel = C("half", 16)[:, k * 128:(k + 1) * 128]
        t = mm(ps[:, 0:n], sel, rows, True, True, fr, tok, inc=True)
        return i, ps[:, 0:n], t

    def head_norm(src, dst, nt_, n, gain, scale, tok):
        w = nt_ * n
        sq3 = sq[:, 0:w].rearrange("p (k n) -> p k n", n=n)
        t1 = act(sq3, src, ACT.Square, tok, now())
        i, ps, t = head_rows(sq3, nt_, n, t1)
        rows = hr[0:16, 0:n]
        if nt_ < 8:
            t0 = ts(V, nv[0:16, 0:n], pb[i][0:16, 0:n], 1.0 / 64, 1e-6, ALU.mult, ALU.add, t, V.last)
        else:
            t0 = ts(V, nv[0:16, 0:n], ps, 1.0 / 64, 1e-6, ALU.mult, ALU.add, t, V.last)
        bk.put(i, t0)
        t = rsqrt_of(rows, nv[0:16, 0:n], nm[0:16, 0:n], nt[0:16, 0:n])
        t = ts(V, rows, rows, scale, None, ALU.mult, None, t)
        for k in range(nt_):
            i, ps, tb = head_bcast(rows, k, n, t)
            tl = stt(dst[:, k, :], src[:, k, :], gain, ps, ALU.mult, ALU.mult, tb, tok)
            bk.put(i, tl)
        return tl

    V(lambda e: e.memset(ones[:, :], 1.0))
    V(lambda e: e.memset(selw[:, :], 0.0))
    t_sel = V.last
    for k in range(8):
        V(lambda e, k=k: e.memset(selw[0:64, k * 16 + 2 * k:k * 16 + 2 * k + 1], 1.0), t_sel)
        V(lambda e, k=k: e.memset(selw[64:128, k * 16 + 2 * k + 1:k * 16 + 2 * k + 2], 1.0), t_sel)
    t_sel = V.last

    state = {"x": [(loaded, t_sel)] * 8}
    act(cact[:, :], pc("c", 0, 8), ACT.Silu, loaded)

    ada = {"at": 0, "tok": {}, "free": None, "pend": None}

    def ada_next(*free):
        if ada["at"] >= 96:
            return
        l, c = divmod(ada["at"], 24)
        ada["at"] += 1
        s, wt, wtok = rg.get(128, 3072, lambda I: ktiles(np.asarray(I["ada_w_2"])[l][:, c * 384:(c + 1) * 384]))
        w = wt.rearrange("p (k n) -> p k n", k=8)
        t = act(ada_acc[:, :], w[:, 0, :], ACT.Copy, wtok, t_cact, ada["free"], free, scale=cact[:, 0:1])
        for k in range(1, 8):
            t = stt(ada_acc[:, :], w[:, k, :], cact[:, k:k + 1], ada_acc[:, :], ALU.mult, ALU.add, t)
        rg.put(s, t)
        ada["pend"] = (l, c, t)

    def ada_sum():
        if ada["pend"] is None:
            return
        (l, c, t), ada["pend"] = ada["pend"], None
        i, ps, fr = bk.get()
        for j in range(3):
            tp_ = mm(ps[:, j:j + 1], ada_acc[:, j * 128:(j + 1) * 128], ones[:, 0:1], True, True, fr, t, inc=(j == 2))
        ada["free"] = tp_
        a = c * 3
        tl = tt(V, mods[:, l * 72 + a:l * 72 + a + 3], ps[:, 0:3], pc(f"ada_b{l}", a, 3), ALU.add, tp_)
        bk.put(i, tl)
        ada["tok"][l] = tl

    t_cact = A.last

    def mod(l, s, which, k):
        return mods[:, l * 72 + s * 24 + which * 8 + k:l * 72 + s * 24 + which * 8 + k + 1]

    Hh, Hl = v3(hx, 0, 8, T), v3(hx, 2048, 8, T)
    piece = {"n": 0, "free": [None] * NPIECE}

    def split_piece(raw, q, *w):
        i = piece["n"] % NPIECE
        piece["n"] += 1
        hi, lo = (t[:, i * PIECE:(i + 1) * PIECE] for t in (wh, wl))
        ta = act(hi, raw, ACT.Copy, w, piece["free"][i])
        tl = tt(q, lo, raw, hi, ALU.subtract, ta)
        return i, tl

    def mm3(out, wi, c, xh, xl, start, stop, *w, inc=False):
        a = wi * PIECE + c
        hi, lo = wh[:, a:a + 128], wl[:, a:a + 128]
        mm(out, hi, xh, start, False, w, skip=True)
        mm(out, hi, xl, False, False, skip=True)
        return mm(out, lo, xh, False, stop, inc=inc, skip=True)

    class Units:

        def __init__(self, fn):
            self.fn, self.u, self.ph, self.ready = fn, 0, now(), []

        def fetch(self, first=V):
            u = self.u
            self.u += 1
            s, w, wtok = rg.get(128, 3072, lambda I: self.fn(I, u))
            ps = [split_piece(w[:, j * PIECE:(j + 1) * PIECE], q, wtok, self.ph) for j, q in enumerate((first, first, G))]
            rg.put(s, [t for _, t in ps])
            self.ready.append(ps)

    def glu(units, src, h_tok, evac, cw=None):
        ph = now()
        bk.use([4, 5, 6, 7])
        Y = [pb[i] for i in range(4)]
        yfree = [bk.free[i] for i in range(4)]
        sg = [sq[:, 768 + i * 256:768 + (i + 1) * 256] for i in range(3)]
        eh = [ex[:, i * 512:i * 512 + 256] for i in range(3)]
        el = [ex[:, i * 512 + 256:(i + 1) * 512] for i in range(3)]
        e_free = [ph, ph, ph]
        pend = []

        def down(u, wi, wtok, t_hid):
            toks = []
            for m in range(8):
                t = mm3(Y[m // 2][:, (m % 2) * T:(m % 2 + 1) * T], wi, m * 128, eh[u % 3], el[u % 3],
                        u == 0 and m % 2 == 0, u == units - 1, t_hid, wtok, yfree, inc=(m % 2 == 1))
                toks.append(t)
            piece["free"][wi] = t
            e_free[u % 3] = t
            return toks

        for u in range(units):
            (wa, ta), (wb, tb), (wd, td) = src.ready.pop(0)
            i, ps, fr = bk.get()
            for b, (wi, wtok) in enumerate(((wa, ta), (wb, tb))):
                for k in range(KD):
                    t = mm3(ps[:, b * T:(b + 1) * T], wi, k * 128, Hh[:, k, :], Hl[:, k, :],
                            k == 0, k == KD - 1, fr, wtok, h_tok[k], inc=(k == KD - 1))
                piece["free"][wi] = t
            if cw is not None:
                ic, pcw, frc = bk.get()
                sel = cst[0:32, ccol["ident"][0] + u:ccol["ident"][0] + u + 1].to_broadcast([32, 128])
                tc = mm(pcw[:, 0:T], sel, cw[0], True, True, frc, cw[1], inc=True)
            if src.u == u + 1 < units:
                src.fetch()
            g_, n = sg[u % 3], u % 3
            t1 = act(g_, ps[:, 0:T], ACT.Silu, t, e_free[n])
            t2 = tt(V, g_, g_, ps[:, T:2 * T], ALU.mult, t, t1)
            bk.put(i, t1, t2)
            if cw is not None:
                t2 = tt(V, g_, g_, pcw[:, 0:T], ALU.mult, tc, t2)
                bk.put(ic, t2)
            t1 = act(eh[n], g_, ACT.Copy, t2, e_free[n])
            t2 = tt(V, el[n], g_, eh[n], ALU.subtract, t1)
            pend.append((u, wd, td, t2))
            if len(pend) > 1:
                down(*pend.pop(0))
            if u % 2:
                ada_next(ph)
            else:
                ada_sum()
        ada_sum()
        t_y = down(*pend.pop(0))
        toks = [evac(m, Y[m // 2][:, (m % 2) * T:(m % 2 + 1) * T], t_y[m | 1]) for m in range(8)]
        for i in range(4):
            bk.put(i, toks[2 * i + 1])
        bk.use(range(8))
        return toks

    def attention(units, off, evac):
        ph = now()
        bk.use([2, 3, 4, 5, 6, 7])
        NB = 4
        sbuf = [wk[:, off + i * 384:off + (i + 1) * 384] for i in range(NB)]
        ptb = [wk[:, off + (NB + i) * 384:off + (NB + i + 1) * 384] for i in range(NB)]
        stb = [wk[:, off + 2 * NB * 384 + i * 8:off + 2 * NB * 384 + (i + 1) * 8] for i in range(NB)]
        sfree, pfree = [ph] * NB, [ph] * NB
        st = {}

        def scores(n, u):
            i, ps, fr = bk.get()
            mm(ps[:, 0:128], u["q"][:, 0:128], u["k"][:, 0:128], True, True, fr, u["tok"])
            t = mm(ps[:, 128:384], u["q"][:, 128:256], u["k"][:, 0:256], True, True, inc=True)
            st[n] = (i, ps, t)

        def softmax(n, u):
            i, ps, t = st[n]
            b, s = sbuf[n % NB], stb[n % NB]
            init = u["sink"] if u["sink"] is not None else -3e38
            for qb, (a, z) in enumerate(((0, 128), (128, 384))):
                tm = V(lambda e, qb=qb, a=a, z=z: e.tensor_tensor_reduce(
                    out=b[:, a:z], in0=u["bias"][:, a:z], in1=ps[:, a:z], scale=1.0, scalar=init,
                    op0=ALU.add, op1=ALU.max, accum_out=s[:, qb:qb + 1]), t, sfree[n % NB], u["btok"])
            bk.put(i, tm)
            tm = ts(V, s[:, 2:4], s[:, 0:2], -1.0, None, ALU.mult, None, tm)
            te = None
            for qb, (a, z) in enumerate(((0, 128), (128, 384))):
                te = act(b[:, a:z], b[:, a:z], ACT.Exp, tm, bias=s[:, 2 + qb:3 + qb], accum=s[:, 4 + qb:5 + qb])
            if u["sink"] is not None:
                te = act(s[:, 6:8], s[:, 2:4], ACT.Exp, tm, bias=u["sink"])
            st[n] = te

        def normalise(n, u):
            b, s = sbuf[n % NB], stb[n % NB]
            t = st[n]
            if u["sink"] is not None:
                t = tt(V, s[:, 4:6], s[:, 4:6], s[:, 6:8], ALU.add, t)
            else:
                t = ts(V, s[:, 4:6], s[:, 4:6], 1e-30, None, ALU.max, None, t)
            t = recip(s[:, 4:6], s[:, 4:6], t)
            for qb, (a, z) in enumerate(((0, 128), (128, 384))):
                if u["gate"] is None:
                    tn = ts(V, b[:, a:z], b[:, a:z], s[:, 4 + qb:5 + qb], None, ALU.mult, None, t)
                else:
                    tn = ts(V, b[:, a:z], b[:, a:z], s[:, 4 + qb:5 + qb], u["gate"](qb), ALU.mult, ALU.mult, t, u["tok"])
            i, ps, fr = bk.get()
            for j in range(3):
                t = tp(ps[:, j * 128:(j + 1) * 128], b[:, j * 128:(j + 1) * 128], fr, tn, inc=(j == 2))
            sfree[n % NB] = t
            st[n] = (i, ps, t)

        def transposed(n, u):
            i, ps, t = st[n]
            st[n] = act(ptb[n % NB], ps[:, 0:384], ACT.Copy, t, pfree[n % NB])
            bk.put(i, st[n])

        def values(n, u):
            h = u["h"]
            hp = h % 2
            ob = pb[(h // 2) % 2]
            o = ob[64 * hp:64 * hp + 64, :]
            p = ptb[n % NB]
            fr = bk.free[(h // 2) % 2]
            first = u["first"]
            if first:
                for j, (l, r, et) in enumerate(u["extra"]):
                    mm(o[:, 0:T], l, r, first, False, fr, et, skip=True)
                    first = False
            mm(o[:, 0:T], u["v"](0), p[:, 0:256], first, False, fr, st[n], u["tok"], skip=True)
            t = mm(o[:, 128:256], u["v"](1), p[:, 256:384], False, u["last"], inc=True, skip=True)
            pfree[n % NB] = t
            if u["last"] and hp == 1:
                bk.put((h // 2) % 2, evac(h // 2, ob[:, 0:T], t))

        n = len(units)
        stages = ((scores, 0), (values, 3), (normalise, 2), (softmax, 1), (transposed, 2))
        for i in range(n + 3):
            for stage, lag in stages:
                if 0 <= i - lag < n:
                    stage(i - lag, units[i - lag])
        bk.use(range(8))

    def residual(m, ps, t):
        return tt(V, X3[:, m, :], X3[:, m, :], ps, ALU.add, t)

    def gated_residual(l, s):
        return lambda m, ps, t: stt(X3[:, m, :], ps, mod(l, s, 2, m), X3[:, m, :], ALU.mult, ALU.add, t)

    def alibi(off, ph):
        b3 = v3(wk, off, 16, 384)
        for h in range(16):
            t = ts(G, b3[:, h, :], C("dist"), -SLOPES[h], None, ALU.mult, None, ph, loaded)
        return b3, t

    def nsa():
        ph = now()
        t = dnorm()
        t_h = apply_norm(lambda k: pc("ln_mix0", k), t, ph)
        ph = now()
        o = 0

        def take(n):
            nonlocal o
            o += n
            return o - n

        qT = v3(wk, take(2048), 8, T)
        ksT, kwT = v3(wk, take(1024), 4, T), v3(wk, take(1024), 4, T)
        vS, vW = v3(wk, take(512), 2, T), v3(wk, take(512), 2, T)
        gts = v3(wk, take(96), 2, 48)
        b_off = take(16 * 384)
        pct_off = take(4096)
        oT_off = take(2048)
        kcT = wk[:, take(60):o].rearrange("p (k n) -> p k n", n=60)
        vc = wk[0:15, take(256):o]
        a_off = take(3104)
        oT = v3(wk, oT_off, 8, T)
        bias, t_bias = alibi(b_off, ph)
        W = lambda a, b: (lambda I: np.asarray(I["a_w_in"])[0][:, a:b])

        Xc = wk[:, pct_off:pct_off + 960].rearrange("p (k n) -> p k n", n=60)
        hid = wk[:, pct_off + 1024:pct_off + 1024 + 120].rearrange("p (m n) -> p m n", n=60)
        t_free = ph
        for which, name, a in ((0, "ck", 1024), (1, "cv", 1280)):
            pos = pc(f"{name}_pos", 0, 16)

            def to_windows(g, ps, t):
                pv = ps.rearrange("p (n k two) -> p two k n", k=8, two=2)
                for hf in range(2):
                    r = slice(64 * hf, 64 * hf + 64)
                    for kh in range(2):
                        tl = tt(V, Xc[r, kh * 8:(kh + 1) * 8, g * 15:(g + 1) * 15], pv[r, hf, :, kh:kh + 15],
                                pos[r, kh * 8:(kh + 1) * 8].unsqueeze(2).to_broadcast([64, 8, 15]), ALU.add, t, t_free)
                return tl

            lin(512, D, lambda I, n0, n1, a=a: dup_heads(W(a, a + 256)(I))[:, n0:n1], H3, t_h, to_windows)
            t_x = V.last
            for m in range(2):
                s, wt, wtok = rg.get(128, 2048, lambda I, m=m, name=name: ktiles(
                    np.asarray(I[f"a_{name}_w1"])[0][:, m * 128:(m + 1) * 128]))
                w1 = wt.rearrange("p (k n) -> p k n", k=16)
                i, ps, fr = bk.get()
                for k in range(16):
                    t = mm(ps[:, 0:60], w1[:, k, :], Xc[:, k, :], k == 0, k == 15, fr, wtok, t_x, inc=(k == 15))
                rg.put(s, t)
                t_g = act(hid[:, m, :], ps[:, 0:60], ACT.Gelu_apprx_tanh, t, t_free)
                bk.put(i, t_g)
            if which == 0:
                s, wt, wtok = rg.get(128, 256, lambda I: ktiles(dup_heads(np.asarray(I["a_ck_w2"])[0])))
                w2 = wt.rearrange("p (k n) -> p k n", k=2)
                i, ps, fr = bk.get()
                for m in range(2):
                    t = mm(ps[:, 0:60], w2[:, m, :], hid[:, m, :], m == 0, m == 1, fr, wtok, t_g, inc=(m == 1))
                rg.put(s, t)
                t = cp(V, kcT[:, 0, :], ps[:, 0:60], t)
                bk.put(i, t)
                t_kc = head_norm(kcT, kcT, 1, 60, pc("a_k0"), 1.0, t)
            else:
                s, wt, wtok = rg.get(128, 128, lambda I: ktiles(np.asarray(I["a_cv_w2"])[0]))
                w2 = wt.rearrange("p (k n) -> p k n", k=2)
                i, ps, fr = bk.get()
                for g in range(4):
                    for m in range(2):
                        t = mm(ps[0:15, g * 64:(g + 1) * 64], hid[:, m, g * 15:(g + 1) * 15], w2[:, m, :], m == 0, m == 1,
                               fr, wtok, t_g, inc=(m == 1 and g == 3))
                rg.put(s, t)
                t_vc = cp(V, vc, ps[0:15, 0:256], t)
                bk.put(i, t_vc)
            t_free = now()

        lin(D, D, lambda I, n0, n1: W(n0, n1)(I), H3, t_h, lambda m, ps, t: cp(A, qT[:, m, :], ps, t, ph))
        t_q = head_norm(qT, qT, 8, T, pc("a_q"), 0.125, A.last)
        for kT, a, gain in ((ksT, 1536, "a_k1"), (kwT, 2048, "a_k2")):
            lin(512, D, lambda I, n0, n1, a=a: dup_heads(W(a, a + 256)(I))[:, n0:n1], H3, t_h,
                lambda m, ps, t, kT=kT: cp(A, kT[:, m, :], ps, t, ph))
            t_k = head_norm(kT, kT, 4, T, pc(gain), 1.0, A.last)
        for vv, a in ((vS, 1792), (vW, 2304)):
            s, wt, wtok = rg.get(128, 2048, lambda I, a=a: ktiles(W(a, a + 256)(I)))
            t = tokmajor(wt.rearrange("p (k n) -> p k n", k=8), 256, wtok, t_h,
                         lambda tb, ps, t, vv=vv: cp(A, vv[:, tb, :], ps, t, ph))
            rg.put(s, t)
        s, wt, wtok = rg.get(128, 384, lambda I: ktiles(W(2560, 2608)(I)))
        t = tokmajor(wt.rearrange("p (k n) -> p k n", k=8), 48, wtok, t_h,
                     lambda tb, ps, t: act(gts[:, tb, :], ps, ACT.Sigmoid, t, ph))
        rg.put(s, t)
        t_all = now()

        pct = wk[0:15, pct_off:pct_off + 4096].rearrange("p (h t) -> p h t", t=T)
        cs = wk[:, a_off:a_off + 240]
        c3 = cs.rearrange("p (h n) -> p h n", n=15)
        cst1 = wk[:, a_off + 240:a_off + 272]
        for qb in range(2):
            cm = C(f"cmp{qb}").rearrange("p (h two n) -> p two h n", two=2, n=15)
            ch = cs.rearrange("p (h two n) -> p two h n", two=2, n=15)
            ready = now()
            for hp in range(2):
                i, ps, fr = bk.get()
                for n in range(8):
                    h = 2 * n + hp
                    t = mm(ps[:, n * 15:(n + 1) * 15], qT[64 * hp:64 * hp + 64, n, qb * 128:(qb + 1) * 128],
                           kcT[64 * hp:64 * hp + 64, 0, (h // 4) * 15:(h // 4 + 1) * 15], True, True, fr, t_all, inc=(n == 7))
                t = tt(V, ch[:, hp], ps[:, 0:120].rearrange("p (h n) -> p h n", n=15), cm[:, hp], ALU.add, t, ready)
                bk.put(i, t)
            mx, sm = cst1[:, 0:16], cst1[:, 16:32]
            t = red(mx, c3, ALU.max, t)
            t = ts(V, mx, mx, -1e20, None, ALU.max, None, t)
            t = tt(V, c3, c3, mx.unsqueeze(2).to_broadcast([128, 16, 15]), ALU.subtract, t)
            t = act(cs, cs, ACT.Exp, t)
            t = red(sm, c3, ALU.add, t)
            t = ts(V, sm, sm, 1e-30, None, ALU.max, None, t)
            t = recip(sm, sm, t)
            gq = gts[:, qb, :].rearrange("p (h b) -> p b h", b=3)[:, 0, :]
            t = tt(V, sm, sm, gq, ALU.mult, t)
            t = tt(V, c3, c3, sm.unsqueeze(2).to_broadcast([128, 16, 15]), ALU.mult, t)
            for h4 in range(4):
                i, ps, fr = bk.get()
                for j in range(4):
                    tk = tp(ps[0:15, j * 128:(j + 1) * 128], c3[:, h4 * 4 + j, :], fr, t, inc=(j == 3))
                tl = cp(V, pct[:, h4 * 4:h4 * 4 + 4, qb * 128:(qb + 1) * 128],
                        ps[0:15, 0:512].rearrange("p (h t) -> p h t", t=128), tk, t_all)
                bk.put(i, tl)
        t_pc = now()
        units = []
        for h in range(16):
            g, r = h // 4, slice(64 * (h % 2), 64 * (h % 2) + 64)
            for b, (kT, vv) in enumerate(((ksT, vS), (kwT, vW))):
                units.append(dict(
                    h=h, q=qT[r, h // 2, :], k=kT[r, g, :], bias=bias[:, h, :], btok=t_bias, tok=t_pc, sink=None,
                    v=lambda kb, vv=vv, g=g: vv[:, kb, g * 64:(g + 1) * 64],
                    gate=lambda qb, h=h, b=b: gts[:, qb, h * 3 + 1 + b:h * 3 + 2 + b],
                    first=(b == 0), last=(b == 1),
                    extra=[(vc[:, g * 64:(g + 1) * 64], pct[:, h, :], t_pc)]))
        attention(units, a_off, lambda m, ps, t: cp(V, oT[:, m, :], ps, t, ph))
        state["x"] = lin(D, D, lambda I, n0, n1: np.asarray(I["a_w_out"])[0][:, n0:n1], oT, V.last, residual)

    def moba():
        ph = now()
        t = dnorm()
        t_h = apply_norm(lambda k: pc("kv_norm", k), t, ph)
        ph = now()
        qT, kT, vv = v3(wk, 0, 8, T), v3(wk, 2048, 4, T), v3(wk, 3072, 2, T)
        oT = v3(wk, 3584, 8, T)
        bias, t_bias = alibi(5632, ph)
        a_off = 5632 + 16 * 384
        W = lambda a, b: (lambda I: np.asarray(I["w_kv_shared"])[:, a:b])
        lin(512, D, lambda I, n0, n1: dup_heads(W(0, 256)(I))[:, n0:n1], H3, t_h,
            lambda m, ps, t: cp(A, kT[:, m, :], ps, t, ph))
        t_k = head_norm(kT, kT, 4, T, pc("k_shared"), 1.0, A.last)
        s, wt, wtok = rg.get(128, 2048, lambda I: ktiles(W(256, 512)(I)))
        t = tokmajor(wt.rearrange("p (k n) -> p k n", k=8), 256, wtok, t_h,
                     lambda tb, ps, t: cp(A, vv[:, tb, :], ps, t, ph))
        rg.put(s, t)
        t_h = apply_norm(lambda k: pc("ln_mix1", k), None, now())
        lin(D, D, lambda I, n0, n1: np.asarray(I["b_w_q"])[0][:, n0:n1], H3, t_h,
            lambda m, ps, t: cp(A, qT[:, m, :], ps, t, ph))
        head_norm(qT, qT, 8, T, pc("b_q"), 0.125, A.last)
        t_all = now()
        units = []
        for h in range(16):
            g, r = h // 4, slice(64 * (h % 2), 64 * (h % 2) + 64)
            units.append(dict(h=h, q=qT[r, h // 2, :], k=kT[r, g, :], bias=bias[:, h, :], btok=t_bias, tok=t_all,
                              sink=None, gate=None, first=True, last=True, extra=[],
                              v=lambda kb, g=g: vv[:, kb, g * 64:(g + 1) * 64]))
        attention(units, a_off, lambda m, ps, t: cp(V, oT[:, m, :], ps, t, ph))
        state["x"] = lin(D, D, lambda I, n0, n1: np.asarray(I["b_w_out"])[0][:, n0:n1], oT, V.last, residual)

    def moe(l):
        def unit(I, u):
            a = ktiles(np.asarray(I["moe_w_gate"])[l, u])
            b = ktiles(np.asarray(I["moe_w_up"])[l, u])
            return np.concatenate([a, b, np.asarray(I["moe_w_down"])[l, u]], 1)

        ph = now()
        src = Units(unit)
        t = dnorm(lambda: src.fetch(G))
        t_hx = []
        for k in range(KD + 1):
            if k < KD:
                t_h = stt(H3[:, k, :], X3[:, k, :], pc(f"ln_ffn{l}", k), rsb[:, :], ALU.mult, ALU.mult, t, ph)
                t_hx.append(act(Hh[:, k, :], H3[:, k, :], ACT.Copy, t_h, ph))
            if k > 0:
                t_hx[k - 1] = tt(V, Hl[:, k - 1, :], H3[:, k - 1, :], Hh[:, k - 1, :], ALU.subtract, t_hx[k - 1])
        ph = now()
        src.fetch()
        o = 0

        def take(n):
            nonlocal o
            o += n
            return sq[:, o - n:o]

        lg = take(72).rearrange("p (b n) -> p b n", b=2)
        wr = pc(f"moe_w{l}", 0, 288).rearrange("p (k n) -> p k n", k=8)
        for tb in range(2):
            i, ps, fr = bk.get()
            for k in range(8):
                mm(ps[:, 0:36], H3[:, k, tb * 128:(tb + 1) * 128], wr[:, k, :], k == 0, False, fr, t_h, loaded)
            t = mm(ps[:, 0:36], ones[0:1, 0:128], pc(f"moe_b{l}", 0, 36, 1), False, True, inc=True)
            t = cp(V, lg[:, tb, :], ps[:, 0:36], t, ph)
            bk.put(i, t)

        def first_max(src, n, t):
            mx, eq, cum, oh = take(2), take(2 * n), take(2 * n), take(2 * n)
            eq, cum, oh = (a.rearrange("p (b n) -> p b n", b=2) for a in (eq, cum, oh))
            t = red(mx, src, ALU.max, t)
            t = tt(V, eq, src, mx.unsqueeze(2).to_broadcast([128, 2, n]), ALU.is_equal, t)
            for b in range(2):
                tb_ = V(lambda e, b=b: e.tensor_tensor_scan(cum[:, b, :], ones[:, 0:n], eq[:, b, :], 0.0, ALU.mult, ALU.add), t)
            t = stt(oh, cum, 1.0, eq, ALU.is_equal, ALU.mult, tb_)
            return mx, oh, t

        gl = lg[:, :, 0:4]
        gm, goh, t = first_max(gl, 4, t)
        ge = take(8).rearrange("p (b n) -> p b n", b=2)
        gw = take(2)
        t = tt(V, ge, gl, gm.unsqueeze(2).to_broadcast([128, 2, 4]), ALU.subtract, t)
        t = act(ge, ge, ACT.Exp, t)
        t = red(gw, ge, ALU.add, t)
        t = recip(gw, gw, t)
        pr = take(64).rearrange("p (b e g) -> p b e g", b=2, g=4)
        el = take(16).rearrange("p (b n) -> p b n", b=2)
        for b in range(2):
            t = tt(V, pr[:, b], lg[:, b, 4:36].rearrange("p (g e) -> p e g", g=4),
                   goh[:, b, :].unsqueeze(1).to_broadcast([128, 8, 4]), ALU.mult, t)
        t = red(el, pr, ALU.add, t)
        m1, oh1, t = first_max(el, 8, t)
        el2 = take(16).rearrange("p (b n) -> p b n", b=2)
        t = stt(el2, oh1, -3e38, el, ALU.mult, ALU.add, t)
        m2, oh2, t = first_max(el2, 8, t)
        e2, den = take(2), take(2)
        t = tt(V, e2, m2, m1, ALU.subtract, t)
        t = act(e2, e2, ACT.Exp, t)
        t = ts(V, den, e2, 1.0, None, ALU.add, None, t)
        t = recip(den, den, t)
        t = tt(V, den, den, gw, ALU.mult, t)
        wgt = take(16).rearrange("p (b n) -> p b n", b=2)
        cw = take(64).rearrange("p (b g e) -> p b g e", b=2, g=4)
        for b in range(2):
            t = stt(wgt[:, b, :], oh2[:, b, :], e2[:, b:b + 1], oh1[:, b, :], ALU.mult, ALU.add, t)
            t = ts(V, wgt[:, b, :], wgt[:, b, :], den[:, b:b + 1], None, ALU.mult, None, t)
            t = tt(V, cw[:, b], goh[:, b, :].unsqueeze(2).to_broadcast([128, 4, 8]),
                   wgt[:, b, :].unsqueeze(1).to_broadcast([128, 4, 8]), ALU.mult, t)
        cwT = take(256)[0:32, :]
        i, ps, fr = bk.get()
        for b in range(2):
            tk = tp(ps[0:32, b * 128:(b + 1) * 128], cw[:, b].rearrange("p g e -> p (g e)"), fr, t, inc=(b == 1))
        t = cp(V, cwT, ps[0:32, 0:T], tk)
        bk.put(i, t)

        assert o <= 768
        state["x"] = glu(32, src, t_hx, residual, cw=(cwT, t))

    def ple(l):
        ph = now()
        t = dnorm()
        t_h = apply_norm(lambda k: pc(f"ln_ple{l}", k), t, ph)
        ph = now()
        gt = v3(wk, 0, 8, T)
        lin(D, D, lambda I, n0, n1: np.asarray(I["ple_w_gate"])[l][:, n0:n1], H3, t_h,
            lambda m, ps, t: act(gt[:, m, :], ps, ACT.Sigmoid, t, ph))
        t_g = A.last
        pT = pc(f"p{l}", 0, 512).rearrange("p (k n) -> p k n", k=2)

        t_x = []

        def add(m, ps, t):
            t1 = tt(V, gt[:, m, :], gt[:, m, :], ps, ALU.mult, t, t_g)
            t_x.append(tt(V, X3[:, m, :], X3[:, m, :], gt[:, m, :], ALU.add, t1))
            return t1

        lin(D, 256, lambda I, n0, n1: np.asarray(I["ple_w_proj"])[l][:, n0:n1], pT, loaded, add)
        state["x"] = t_x

    def adaln(l, s, src=None):
        while ada["at"] < 24 * (l + 1):
            ada_next(now())
            ada_sum()
        ph = now()
        t = dnorm((lambda: src.fetch(G)) if src else lambda: None)
        tg = ts(V, gs[:, 0:8], mods[:, l * 72 + s * 24 + 8:l * 72 + s * 24 + 16], 1.0, None, ALU.add, None, ada["tok"][l])
        tg = tt(V, gs[:, 0:8], gs[:, 0:8], pc(f"ng{l}{s}", 0, 8), ALU.mult, tg)
        t_n = []
        for k in range(9 if src else 8):
            if k < 8:
                t1 = stt(H3[:, k, :], X3[:, k, :], gs[:, k:k + 1], rsb[:, :], ALU.mult, ALU.mult, t, tg, ph)
                t_n.append(act((Hh if src else H3)[:, k, :], H3[:, k, :], ACT.Identity, t1, ph, bias=mod(l, s, 0, k)))
            if src and k > 0:
                n = k - 1
                t_n[n] = stt(Hl[:, n, :], H3[:, n, :], mod(l, s, 0, n), Hh[:, n, :], ALU.add, ALU.subtract, t_n[n], ph)
        return t_n

    def ffn(l, s, w):
        def unit(I, u):
            wi, wo = np.asarray(I["ffn_w_in_2"])[l, w], np.asarray(I["ffn_w_out_2"])[l, w]
            return np.concatenate([ktiles(wi[:, u * 128:(u + 1) * 128]),
                                   ktiles(wi[:, 2816 + u * 128:2816 + (u + 1) * 128]), wo[u * 128:(u + 1) * 128]], 1)

        src = Units(unit)
        t_h = adaln(l, s, src)
        th = ts(V, gs[:, 8:16], mods[:, l * 72 + s * 24 + 16:l * 72 + s * 24 + 24], 0.5, None, ALU.mult, None, V.last)
        state["x"] = glu(22, src, t_h, lambda m, ps, t: stt(
            X3[:, m, :], ps, gs[:, 8 + m:9 + m], X3[:, m, :], ALU.mult, ALU.add, t, th))

    def swa(l):
        t_h = adaln(l, 1)[-1]
        ph = now()
        qT, kT, vv = v3(wk, 0, 8, T), v3(wk, 2048, 4, T), v3(wk, 3072, 2, T)
        oT = v3(wk, 3584, 8, T)
        W = lambda a, b: (lambda I: np.asarray(I["sw_w_qkv_2"])[0][:, a:b])
        lin(512, D, lambda I, n0, n1: dup_heads(W(1024, 1280)(I))[:, n0:n1], H3, t_h,
            lambda m, ps, t: cp(A, kT[:, m, :], ps, t, ph))
        head_norm(kT, kT, 4, T, pc("sw_k"), 1.0, A.last)
        s, wt, wtok = rg.get(128, 2048, lambda I: ktiles(W(1280, 1536)(I)))
        t = tokmajor(wt.rearrange("p (k n) -> p k n", k=8), 256, wtok, t_h,
                     lambda tb, ps, t: cp(A, vv[:, tb, :], ps, t, ph))
        rg.put(s, t)
        lin(D, D, lambda I, n0, n1: W(n0, n1)(I), H3, t_h, lambda m, ps, t: cp(A, qT[:, m, :], ps, t, ph))
        head_norm(qT, qT, 8, T, pc("sw_q"), 0.125, A.last)
        t_all = now()
        units = []
        for h in range(16):
            g, r = h // 4, slice(64 * (h % 2), 64 * (h % 2) + 64)
            units.append(dict(h=h, q=qT[r, h // 2, :], k=kT[r, g, :], bias=C("swa"), btok=loaded, tok=t_all,
                              sink=pc("sinks", h), gate=None, first=True, last=True, extra=[],
                              v=lambda kb, g=g: vv[:, kb, g * 64:(g + 1) * 64]))
        attention(units, 5632, lambda m, ps, t: cp(V, oT[:, m, :], ps, t, ph))
        state["x"] = lin(D, D, lambda I, n0, n1: np.asarray(I["sw_w_o_2"])[0][:, n0:n1], oT, V.last, gated_residual(l, 1))

    def mamba(l):
        t_h = adaln(l, 1)[-1]
        ph = now()
        o = 0

        def take(n):
            nonlocal o
            o += n
            return o - n

        zT, xsT = v3(wk, take(4096), 16, T), v3(wk, take(4096), 16, T)
        BT, CT = v3(wk, take(2048), 8, T), v3(wk, take(2048), 8, T)
        Xt = v3(wk, take(4096), 2, 2048)
        xp = [wk[:, take(260):o] for _ in range(3)]
        acc = [wk[:, take(256):o] for _ in range(3)]
        cbm = [wk[:, take(384):o] for _ in range(2)]
        Gb = [wk[:, take(384):o] for _ in range(3)]
        sm = [wk[0:32, take(256):o] for _ in range(5)]
        dtT, acT = v3(wk, take(64), 2, 32), v3(wk, take(64), 2, 32)
        eA = wk[0:32, take(1):o]
        W = lambda a, b: (lambda I: np.asarray(I["mb_w_in_2"])[0][:, a:b])

        s, wt, wtok = rg.get(128, 256, lambda I: ktiles(W(6144, 6176)(I)))
        w = wt.rearrange("p (k n) -> p k n", k=8)
        i, ps, fr = bk.get()
        for k in range(8):
            t = mm(ps[0:32, 0:T], w[:, k, :], H3[:, k, :], k == 0, k == 7, fr, wtok, t_h, inc=(k == 7))
        rg.put(s, t)
        v, e, r, s2, p = sm
        t = ts(V, v, ps[0:32, 0:T], pc("dt_bias", 0, 1, 32), None, ALU.add, None, t, ph)
        bk.put(i, t)
        t = act(e, v, ACT.Abs, t)
        t = act(e, e, ACT.Exp, t, scale=-1.0)
        t = ts(V, r, e, 2.0, None, ALU.add, None, t)
        t = recip(r, r, t)
        t = tt(V, e, e, r, ALU.mult, t)
        t = tt(V, s2, e, e, ALU.mult, t)
        t = ts(V, p, s2, 1.0 / 19, None, ALU.mult, None, t)
        for n in (17, 15, 13, 11, 9, 7, 5, 3):
            t = stt(p, p, 1.0 / n, s2, ALU.add, ALU.mult, t)
        t = stt(p, p, 1.0, e, ALU.add, ALU.mult, t)
        t = ts(V, p, p, 2.0, None, ALU.mult, None, t)
        t = stt(v, v, 0.0, p, ALU.max, ALU.add, t)
        ta = act(eA, pc("A_log", 0, 1, 32), ACT.Exp, ph)
        t = ts(V, e, v, eA, -1.0, ALU.mult, ALU.mult, t, ta)
        t = V(lambda q: q.tensor_tensor_scan(r, ones[0:32, 0:T], e, 0.0, ALU.mult, ALU.add), t)
        dt, acum = v, r
        for src, dst in ((dt, dtT), (acum, acT)):
            i, ps, fr = bk.get()
            for b in range(2):
                tk = tp(ps[:, b * 32:(b + 1) * 32], src[:, b * 128:(b + 1) * 128], fr, t, inc=(b == 1))
            tl = cp(V, dst, ps[:, 0:64].rearrange("p (b n) -> p b n", b=2), tk)
            bk.put(i, tl)
        t_dt = V.last

        for j in range(3):
            V(lambda q, j=j: q.memset(xp[j][:, 0:3], 0.0), ph)
        t_xp = V.last
        cfree = [ph, ph, ph]
        afree = [ph, ph, ph]
        n_conv = [0]

        def conv(dst, ct):
            def evac(m, ps, t):
                c = ct + m
                j = n_conv[0] % 3
                n_conv[0] += 1
                x, a = xp[j], acc[j]
                t1 = act(x[:, 3:259], ps, ACT.Copy, t, cfree[j], t_xp)
                t2 = ts(V, a, x[:, 0:T], pc("conv0", c), pc("conv_b", c), ALU.mult, ALU.add, t1, afree[j])
                for k in (1, 2, 3):
                    t2 = stt(a, x[:, k:k + T], pc(f"conv{k}", c), a, ALU.mult, ALU.add, t2)
                cfree[j] = t2
                afree[j] = act(dst[:, m, :], a, ACT.Silu, t2, ph)
                return t1
            return evac

        lin(2048, D, lambda I, n0, n1: W(2048 + n0, 2048 + n1)(I), H3, t_h, conv(xsT, 0))
        lin(1024, D, lambda I, n0, n1: W(4096 + n0, 4096 + n1)(I), H3, t_h, conv(BT, 16))
        lin(1024, D, lambda I, n0, n1: W(5120 + n0, 5120 + n1)(I), H3, t_h, conv(CT, 24))
        t_c = A.last
        lin(2048, D, lambda I, n0, n1: W(n0, n1)(I), H3, t_h, lambda m, ps, t: act(zT[:, m, :], ps, ACT.Silu, t, ph))
        t_z = A.last
        for m in range(16):
            i, ps, fr = bk.get()
            for b in range(2):
                tk = tp(ps[:, b * 128:(b + 1) * 128], xsT[:, m, b * 128:(b + 1) * 128], fr, t_c, inc=(b == 1))
            for b in range(2):
                tl = tt(V, Xt[:, b, m * 128:(m + 1) * 128].rearrange("p (h d) -> p h d", h=2),
                        ps[:, b * 128:(b + 1) * 128].rearrange("p (h d) -> p h d", h=2),
                        dtT[:, b, 2 * m:2 * m + 2].unsqueeze(2).to_broadcast([128, 2, 64]), ALU.mult, tk, t_dt, ph)
            bk.put(i, tl)
        t_X = V.last

        bk.use(range(2, 8))
        gfree, mfree = [ph] * 3, [ph] * 2
        heads = []

        def group(g):
            i, ps, fr = bk.get()
            mm(ps[:, 0:256], BT[:, g, 0:128], CT[:, g, :], True, True, fr, t_c)
            t = mm(ps[:, 256:384], BT[:, g, 128:256], CT[:, g, 128:256], True, True, inc=True)
            t = tt(V, cbm[g % 2], ps[:, 0:384], C("S384"), ALU.mult, t, mfree[g % 2])
            bk.put(i, t)

        def weights(h):
            g = h // 4
            i, ps, fr = bk.get()
            sel = cst[0:32, ccol["ident"][0] + h:ccol["ident"][0] + h + 1].to_broadcast([32, 128])
            t = mm(ps[:, 0:T], sel, acum, True, True, fr, t_dt, inc=True)
            b = Gb[h % 3]
            ts(V, b[:, 0:256], ps[:, 0:256], acT[:, 0, h:h + 1], 0.0, ALU.subtract, ALU.min, t, gfree[h % 3])
            t = ts(V, b[:, 256:384], ps[:, 128:256], acT[:, 1, h:h + 1], 0.0, ALU.subtract, ALU.min, t)
            bk.put(i, t)
            t = act(b, b, ACT.Exp, t)
            t = tt(V, b, b, cbm[g % 2], ALU.mult, t)
            mfree[g % 2] = t
            heads.append(t)

        def output(h):
            m, hp = h // 2, h % 2
            ob = pb[m % 2]
            b = Gb[h % 3]
            mm(ob[64 * hp:64 * hp + 64, 0:T], Xt[:, 0, h * 64:(h + 1) * 64], b[:, 0:256], True, False,
               bk.free[m % 2], heads[h], t_X, skip=True)
            t = mm(ob[64 * hp:64 * hp + 64, 128:256], Xt[:, 1, h * 64:(h + 1) * 64], b[:, 256:384], False, True,
                   inc=True, skip=True)
            gfree[h % 3] = t
            if hp == 1:
                t = stt(xsT[:, m, :], xsT[:, m, :], pc("mb_D", m), ob[:, 0:T], ALU.mult, ALU.add, t)
                bk.put(m % 2, t)
                tt(G, xsT[:, m, :], xsT[:, m, :], zT[:, m, :], ALU.mult, t, t_z)

        for h in range(33):
            if h < 32:
                if h % 4 == 0:
                    group(h // 4)
                weights(h)
            if h >= 1:
                output(h - 1)
        bk.use(range(8))
        t_y = G.last

        t1 = act(wk[:, 0:4096], wk[:, 4096:8192], ACT.Square, t_y)
        i, ps, fr = bk.get()
        sel8 = lambda g: selg[:, g * 8:(g + 1) * 8]
        for m in range(16):
            t = mm(ps[0:8, 0:T], sel8(m // 2), zT[:, m, :], m == 0, m == 15, fr, t1, t_selg, inc=(m == 15))
        t0 = ts(V, nv[0:8, :], ps[0:8, 0:T], 1.0 / 256, 1e-6, ALU.mult, ALU.add, t, V.last)
        bk.put(i, t0)
        t = rsqrt_of(hr[0:8, :], nv[0:8, :], nm[0:8, :], nt[0:8, :])
        for g in range(8):
            i, ps, fr = bk.get()
            sel = cst[0:8, ccol["ident"][0] + g:ccol["ident"][0] + g + 1].to_broadcast([8, 128])
            tb = mm(ps[:, 0:T], sel, hr[0:8, :], True, True, fr, t, inc=True)
            for m in (2 * g, 2 * g + 1):
                tl = stt(xsT[:, m, :], xsT[:, m, :], pc("mb_g", m), ps[:, 0:T], ALU.mult, ALU.mult, tb, t_y, t1)
            bk.put(i, tl)
        state["x"] = lin(D, 2048, lambda I, n0, n1: np.asarray(I["mb_w_out_2"])[0][:, n0:n1], xsT, V.last, gated_residual(l, 1))

    V(lambda e: e.memset(selg[:, :], 0.0))
    t_selg = V.last
    for k in range(8):
        V(lambda e, k=k: e.memset(selg[:, k * 9:k * 9 + 1], 1.0), t_selg)
    t_selg = V.last

    def rwkv(l, j):
        t_h = adaln(l, 1)
        ph = now()
        o = 0

        def take(n):
            nonlocal o
            o += n
            return o - n

        offs = {n: take(2048) for n in ("r", "k", "v", "kk", "a", "lw", "c")}
        fl = {n: wk[:, a:a + 2048] for n, a in offs.items() if n != "lo"}
        r3, k3, v3_, kk3, a3, lw3, c3 = (v3(wk, offs[n], 8, T) for n in ("r", "k", "v", "kk", "a", "lw", "c"))
        offs["lo"] = take(512)
        lo = wk[:, offs["lo"]:o].rearrange("p (k n) -> p k n", n=T)
        base = o
        dx3 = c3
        KAPPA = float(np.exp(-0.5))
        area = [wk[:, base + i * 2048:base + (i + 1) * 2048] for i in range(4)]
        xm = [Q3, v3(wk, base, 8, T), v3(wk, base + 2048, 8, T)]
        hid = [wk[:, base + 8192:base + 8192 + T], area[3][:, 0:T]]

        t_dx = []
        for k in range(8):
            t0 = ts(V, dx3[:, k, 0:1], H3[:, k, 0:1], -1.0, None, ALU.mult, None, t_h[k], ph)
            t_dx.append((t0, tt(G, dx3[:, k, 1:T], H3[:, k, 0:T - 1], H3[:, k, 1:T], ALU.subtract, t_h[k], ph)))

        def mix(n, m, tok):
            for k in range(8):
                t = stt(xm[n][:, k, :], dx3[:, k, :], pc(f"mu{j}{m}", k), H3[:, k, :], ALU.mult, ALU.add, t_dx[k], tok)
            return t

        def lora_in(rank, w1, src, tok, func, outs, *w):
            s, wt, wtok = rg.get(128, 8 * rank, lambda I: ktiles(w1(I)))
            w1_ = wt.rearrange("p (k n) -> p k n", k=8)
            parts = []
            for n, a in enumerate(range(0, rank, 128)):
                z = min(128, rank - a)
                i, ps, fr = bk.get()
                for k in range(8):
                    t = mm(ps[0:z, 0:T], w1_[:, k, a:a + z], src[:, k, :], k == 0, k == 7, fr, wtok, tok, inc=(k == 7))
                te = act(outs[n][0:z, :], ps[0:z, 0:T], func, t, w)
                bk.put(i, te)
                parts.append((a, z, outs[n][0:z, :], te))
            rg.put(s, t)
            return parts

        def lora_out(parts, w2, evac):
            ws = [rg.get(z, 1024, lambda I, a=a, z=z: np.asarray(w2(I))[a:a + z]) for a, z, _, _ in parts]
            toks = []
            for m in range(8):
                i, ps, fr = bk.get()
                for n, (a, z, h, te) in enumerate(parts):
                    t = mm(ps[:, 0:T], ws[n][1][:, m * 128:(m + 1) * 128], h, n == 0, n == len(parts) - 1,
                           fr, ws[n][2], te, inc=(n == len(parts) - 1))
                toks.append(evac(m, ps[:, 0:T], t))
                bk.put(i, toks[-1])
            for s, _, _ in ws:
                rg.put(s, t)
            return toks

        def rkv(n, src, tok, dst):
            return lin(D, D, lambda I, n0, n1: np.asarray(I["rw_w_rkv_2"])[j, n][:, n0:n1], src, tok,
                       lambda m, ps, t: cp(A, dst[:, m, :], ps, t, ph))

        I_ = lambda name, n=j: (lambda I: np.asarray(I[name])[n])
        t_r, t_k, t_v_ = mix(0, 0, ph), mix(1, 2, ph), mix(2, 3, ph)
        rkv(0, xm[0], t_r, r3)
        t_w = mix(0, 1, PE.last)
        t = rkv(1, xm[1], t_k, k3)
        t_a = mix(1, 4, PE.last)
        for k in range(8):
            t1 = ts(V, kk3[:, k, :], k3[:, k, :], pc(f"k_k{j}", k), None, ALU.mult, None, t[k], ph)
        t_sq = act(area[2], fl["kk"], ACT.Square, t1, ph)
        t = rkv(2, xm[2], t_v_, v3_)
        if j == 0:
            t_v = cp(G, vfirst[:, :], fl["v"], t[-1])
        else:
            t_vl = t[-1]
            diff = v3(wk, base + 3 * 2048, 8, T)

            def mix_v(m, ps, t):
                t1 = act(lw3[:, m, :], ps, ACT.Sigmoid, t, ph, bias=pc("v01", m))
                t2 = tt(V, diff[:, m, :], vfirst[:, m * T:(m + 1) * T], v3_[:, m, :], ALU.subtract, t_vl, ph)
                t2 = tt(V, diff[:, m, :], diff[:, m, :], lw3[:, m, :], ALU.mult, t1, t2)
                tt(V, v3_[:, m, :], v3_[:, m, :], diff[:, m, :], ALU.add, t2)
                return t1

            lora_out(lora_in(32, I_("rw_v1_2", 0), xm[2], t_v_, ACT.Copy, hid, ph), I_("rw_v2_2", 0), mix_v)
            t_v = V.last
        t_g = mix(2, 5, PE.last)
        i, ps, t = head_rows(v3(wk, base + 2 * 2048, 8, T), 8, T, t_sq)
        t0 = ts(V, nv[0:16, :], ps, 1e-24, None, ALU.max, None, t, V.last)
        bk.put(i, t0)
        t_hr = rsqrt_of(hr[:, :], nv[0:16, :], nm[0:16, :], nt[0:16, :])
        before = (PE.last, V.last)
        lw_ = lora_in(64, I_("rw_w1_2"), xm[0], t_w, ACT.Tanh, hid[0:1], before)
        la = lora_in(64, I_("rw_a1_2"), xm[1], t_a, ACT.Copy, hid[1:2], before)
        t_lw = lora_out(lw_, I_("rw_w2_2"), lambda m, ps, t: act(lw3[:, m, :], ps, ACT.Sigmoid, t, before, bias=pc(f"w0{j}", m)))
        t_a = lora_out(la, I_("rw_a2_2"), lambda m, ps, t: act(a3[:, m, :], ps, ACT.Sigmoid, t, ph, bias=pc(f"a0{j}", m)))
        t_c = []
        for k in range(8):
            t_c.append(V(lambda q, k=k: q.tensor_tensor_scan(c3[:, k, :], C("reset"), lw3[:, k, :], 0.0, ALU.mult, ALU.add),
                         t_lw[k], V.last))
        lg_ = lora_in(160, I_("rw_g1_2"), xm[2], t_g, ACT.Sigmoid, [lo[:, 0, :], lo[:, 1, :]], ph)
        t_mx = PE.last

        spare = base + 11 * 512 + 5 * 256 + 192
        ex3 = [v3(wk, spare + i * 768, 3, T) for i in range(2)]
        ex_free = [now(), now()]
        ready = []

        def prepare():
            k = len(ready)
            e1, e2, e3 = (ex3[k % 2][:, n, :] for n in range(3))
            ef = ex_free[k % 2]
            t3 = tt(G, lw3[:, k, :], c3[:, k, :], lw3[:, k, :], ALU.subtract, t_c[k])
            te2 = act(e2, c3[:, k, :], ACT.Exp, t_c[k], ef, scale=-KAPPA)
            te3 = act(e3, c3[:, k, :], ACT.Exp, scale=KAPPA)
            te1 = act(e1, lw3[:, k, :], ACT.Exp, t3, scale=-KAPPA)
            i, ps, tb = head_bcast(hr[:, :], k, T, t_hr)
            t_kk = tt(V, kk3[:, k, :], kk3[:, k, :], ps, ALU.mult, tb)
            bk.put(i, t_kk)
            t1 = ts(V, Q3[:, k, :], a3[:, k, :], -1.0, pc(f"k_a{j}", k), ALU.add, ALU.mult, t_a[k], t_mx)
            t1 = stt(k3[:, k, :], Q3[:, k, :], 1.0, k3[:, k, :], ALU.add, ALU.mult, t1)
            t4 = tt(V, a3[:, k, :], a3[:, k, :], kk3[:, k, :], ALU.mult, t_kk)
            t2 = stt(Q3[:, k, :], r3[:, k, :], pc(f"r_k{j}", k), k3[:, k, :], ALU.mult, ALU.mult, t1)
            t7 = tt(G, a3[:, k, :], a3[:, k, :], e3, ALU.mult, te3, t4)
            t8 = tt(G, k3[:, k, :], k3[:, k, :], e3, ALU.mult, te3, t2)
            t6 = tt(V, r3[:, k, :], r3[:, k, :], e2, ALU.mult, te2, t2)
            cp(V, dl[:, 4 * k:4 * k + 4], e2.rearrange("p (n c) -> p n c", c=64)[:, :, 63], te2)
            t5 = stt(kk3[:, k, :], kk3[:, k, :], -1.0, e1, ALU.mult, ALU.mult, te1, t4)
            ready.append((t5, t6, t7, t8))
            ex_free[k % 2] = (t5, t8)
            mm(pb[1][0:16, 0:T], half_select(k), Q3[:, k, :], k == 0, k == 7, bk.free[1], t2, inc=(k == 7))

        names = ["M16", "M16T", "Mo32", "Mo64", "ArbT", "ArkT", "AakT", "M2", "M2T", "TI", "TT"]
        y3 = r3
        uns = [(hp, hf) for hp in range(2) for hf in range(2)]
        mask = lambda n: C(n).unsqueeze(1).to_broadcast([128, 2, 128])
        idm = ident.unsqueeze(1).to_broadcast([128, 4, 128])

        def memory(n):
            if n == 0:
                at = [wk[:, base + i * 512:base + (i + 1) * 512] for i in range(11)]
                o = base + 11 * 512
                sm_ = [wk[:, o + i * 256:o + (i + 1) * 256] for i in range(5)]
                o += 5 * 256
            else:
                at = [fl[x][:, i * 512:(i + 1) * 512] for x in ("lw", "c") for i in range(4)]
                at += [sq[:, i * 512:(i + 1) * 512] for i in range(3)]
                sm_ = [wk[:, spare + i * 256:spare + (i + 1) * 256] for i in range(5)]
                o = spare + 5 * 256
            mat = {x: a.rearrange("p (u n) -> p u n", u=4) for x, a in zip(names, at)}
            mat["M4"], mat["M4T"] = mat["M16"], mat["M16T"]
            return mat, [a.rearrange("p (b n) -> p b n", b=2) for a in sm_], wk[:, o:o + 128], wk[:, o + 128:o + 192]

        def tile(m, n, mem, free):
            mat, (Bt, Kt, Vt, W0, Ub), Pb, Pd = mem
            t_in = ready[m]
            t_pb = V(lambda e: e.memset(Pb, 0.0), free)
            t_u0 = V(lambda e: e.memset(Ub, 0.0), free)

            def of(x):
                return lambda u: mat[x][:, u, :]

            def product(l_, r_, *w):
                i, ps, fr = bk.get()
                for u in range(4):
                    t = mm(ps[:, u * 128:(u + 1) * 128], l_(u), r_(u), True, True, fr, w, inc=(u == 3))
                return i, ps[:, :].rearrange("p (u n) -> p u n", u=4), t

            def fm(x3):
                return lambda u: x3[64 * uns[u][0]:64 * uns[u][0] + 64, m, uns[u][1] * 128:(uns[u][1] + 1) * 128]

            at_, bt_, kt_, rt_ = fm(kk3), fm(a3), fm(k3), fm(r3)

            def by_head(l_, r_, outs):
                for hp in range(2):
                    i, ps, fr = bk.get()
                    for hf in range(2):
                        u = 2 * hp + hf
                        t = mm(ps[:, hf * 128:(hf + 1) * 128], l_(u), r_(u), True, True, fr, t_in, inc=(hf == 1))
                    p3 = ps[:, 0:256].rearrange("p (u n) -> p u n", u=2)
                    for x, mk in outs:
                        t1 = tt(V, mat[x][:, 2 * hp:2 * hp + 2, :], p3, mask(mk), ALU.mult, t, free)
                    bk.put(i, t1)
                return t1

            def turned(x, *w):
                i, ps, fr = bk.get()
                for u in range(4):
                    t = tp(ps[:, u * 128:(u + 1) * 128], mat[x][:, u, :], fr, w, inc=(u == 3))
                return i, ps[:, :].rearrange("p (u n) -> p u n", u=4), t

            def turn(x, dst, *w):
                i, ps, t = turned(x, *w)
                t = cp(A, mat[dst], ps, t, free)
                bk.put(i, t)
                return t

            def power(l_, r_, dst, *w):
                i, ps, t = product(of(l_), of(r_), *w)
                t = cp(A, mat[dst], ps, t, free)
                bk.put(i, t)
                return t

            def grow(x, *w):
                i, ps, t = product(of(x), of("TT"), *w)
                t = tt(V, mat["TT"], mat["TT"], ps, ALU.add, t)
                bk.put(i, t)
                return t

            t_m = by_head(at_, bt_, (("M16", "L16"), ("Mo32", "Lo32"), ("Mo64", "Lo64")))
            yield
            i, ps, t = turned("M16", t_m)
            t1 = cp(A, mat["M16T"], ps, t, free)
            tg = tt(V, mat["TT"], ps, idm, ALU.add, t, t1, free)
            bk.put(i, t1, tg)
            yield
            for x3, dst in ((a3, Bt), (k3, Kt), (v3_, Vt)):
                i, ps, fr = bk.get()
                for b in range(2):
                    t = tp(ps[:, b * 128:(b + 1) * 128], x3[:, m, b * 128:(b + 1) * 128], fr, t_in, t_v, inc=(b == 1))
                t_tok = cp(A, dst, ps[:, 0:256].rearrange("p (b n) -> p b n", b=2), t, free)
                bk.put(i, t_tok)
            t2 = power("M16T", "M16", "M2", t_m, t1)
            yield
            by_head(kt_, at_, (("AakT", "U64"),))
            yield
            t2t = turn("M2", "M2T", t2)
            tg = grow("M2", t2, tg)
            yield
            t4 = power("M2T", "M2", "M4", t2t)
            by_head(bt_, rt_, (("ArbT", "Ui64"),))
            yield
            t4t = turn("M4", "M4T", t4)
            tg = grow("M4", t4, tg)
            yield
            t8 = power("M4T", "M4", "M2", t4t)
            t_A = by_head(kt_, rt_, (("ArkT", "Ui64"),))
            yield
            tg = grow("M2", t8, tg)
            yield
            for n_, x in enumerate(("Mo32", "Mo64")):
                t1 = turn("TT", "TI", tg)
                t2 = power(x, "TT", "M4", tg)
                yield
                if n_ == 0:
                    i, ps, fr = bk.get()
                    for u, (hp, hf) in enumerate(uns):
                        t = mm(ps[:, hf * 128 + hp * 64:hf * 128 + hp * 64 + 64], mat["AakT"][:, u, :],
                               Vt[:, hf, 64 * hp:64 * hp + 64], True, True, fr, t_A, t_tok, inc=(u == 3))
                    tw0 = cp(V, W0[:, :, :], ps[:, 0:256].rearrange("p (b n) -> p b n", b=2), t, free)
                    bk.put(i, tw0)
                    yield
                i, ps, t = product(of("TI"), of("M4"), t1, t2)
                tg = tt(V, mat["TT"], mat["TT"], ps, ALU.add, t)
                bk.put(i, tg)
                yield
            py, fry = pb[n], bk.free[n]
            for u, (hp, hf) in enumerate(uns):
                mm(py[64 * hp:64 * hp + 64, hf * 128:(hf + 1) * 128], Vt[:, hf, 64 * hp:64 * hp + 64], mat["ArkT"][:, u, :],
                   hf == 0, False, fry, t_A, t_tok, skip=True)
            t_P = t_Pd = None
            for c in range(4):
                hf, c2 = divmod(c, 2)
                rs_ = slice(64 * c2, 64 * c2 + 64)
                cs_ = slice(c * 64, (c + 1) * 64)
                if c:
                    i, ps, fr = bk.get()
                    t = mm(ps[rs_, 0:128], kk3[:, m, cs_], Pb[:, :], True, True, fr, t_P, inc=True)
                    tw = tt(V, W0[rs_, hf, :], ps[rs_, 0:128], W0[rs_, hf, :], ALU.add, t, tw0)
                    bk.put(i, tw)
                    mm(py[:, cs_], Pb[:, :], r3[:, m, cs_], False, False, fry, t_P, skip=True)
                    yield
                else:
                    tw = tw0
                i, ps, fr = bk.get()
                for hp in range(2):
                    t = mm(ps[rs_, hp * 64:(hp + 1) * 64], mat["TT"][:, hp * 2 + hf, rs_], W0[:, hf, hp * 64:(hp + 1) * 64],
                           True, True, fr, tw, tg, inc=(hp == 1))
                tu = cp(V, Ub[rs_, hf, :], ps[rs_, 0:128], t, free, t_u0)
                bk.put(i, tu)
                yield
                for hp in range(2):
                    hs = slice(64 * hp, 64 * hp + 64)
                    t_y = mm(py[hs, cs_], Ub[:, hf, hs], mat["ArbT"][:, hp * 2 + hf, rs_], False, c == 3, tu, t_A,
                             inc=(hp == 1), skip=True)
                if c < 3:
                    i, ps, fr = bk.get()
                    for hp in range(2):
                        hs = slice(64 * hp, 64 * hp + 64)
                        mm(ps[hs, 0:64], Bt[rs_, hf, hs], Ub[rs_, hf, hs], True, False, fr, tu, t_tok, skip=True)
                        t = mm(ps[hs, 0:64], Kt[rs_, hf, hs], Vt[rs_, hf, hs], False, True, inc=(hp == 1), skip=True)
                    for hp in range(2):
                        hs = slice(64 * hp, 64 * hp + 64)
                        d = dl[hs, m * 4 + c:m * 4 + c + 1]
                        if c == 0:
                            t_P = ts(V, Pb[hs, hs], ps[hs, 0:64], d, None, ALU.mult, None, t, free, t_pb)
                        else:
                            t_P = stt(Pb[hs, hs], ps[hs, 0:64], d, Pd[hs, :], ALU.mult, ALU.add, t, t_y, t_Pd)
                    bk.put(i, t_P)
                    if c < 2:
                        for hp in range(2):
                            hs = slice(64 * hp, 64 * hp + 64)
                            t_Pd = ts(V, Pd[hs, :], Pb[hs, hs], dl[hs, m * 4 + c + 1:m * 4 + c + 2], None, ALU.mult, None, t_P)
                    yield
            t1 = cp(V, y3[:, m, :], py[:, 0:T], t_y)
            bk.put(n, t1)
            yield
            i, ps, fr = bk.get()
            t = mm(ps[:, 0:T], C("blk64"), y3[:, m, :], True, True, fr, t1, inc=True)
            t1 = stt(y3[:, m, :], ps[:, 0:T], -1.0 / 64, y3[:, m, :], ALU.mult, ALU.add, t)
            bk.put(i, t1)
            t_sq[m] = act(kk3[:, m, :], y3[:, m, :], ACT.Square, t1)
            i, ps, tb = head_bcast(bsum[:, :], m, T, t_bs)
            t2 = tt(V, v3_[:, m, :], v3_[:, m, :], ps, ALU.mult, tb, t_v)
            bk.put(i, t2)

        t_sq, t_bs = [None] * 8, None
        bk.use(range(2, 8))
        mems = [memory(0), memory(1)]
        waiting = list(range(8))
        frees = [now(), None]
        slots = [None, None]
        prepare()
        while waiting or any(slots):
            if len(ready) < 8:
                prepare()
                if len(ready) == 8:
                    t_bs = cp(V, bsum[:, :], pb[1][0:16, 0:T], PE.last)
                    bk.put(1, t_bs)
                    frees[1] = now()
            for n in range(2):
                if slots[n] is None and waiting and frees[n] is not None:
                    slots[n] = tile(waiting.pop(0), n, mems[n], frees[n])
                if slots[n] is not None and next(slots[n], "end") == "end":
                    slots[n], frees[n] = None, now()
        bk.use(range(8))

        i, ps, t = head_rows(kk3, 8, T, t_sq)
        t0 = ts(V, nv[0:16, :], ps, 1.0 / 64, 64e-5, ALU.mult, ALU.add, t, V.last)
        bk.put(i, t0)
        t = rsqrt_of(hr[:, :], nv[0:16, :], nm[0:16, :], nt[0:16, :])
        t_l = now()
        t_g = lora_out(lg_, I_("rw_g2_2"), lambda m, ps, t: cp(A, a3[:, m, :], ps, t, t_l))
        for k in range(8):
            i, ps, tb = head_bcast(hr[:, :], k, T, t)
            tl = stt(y3[:, k, :], y3[:, k, :], pc(f"ln_w{j}", k), ps, ALU.mult, ALU.mult, tb)
            bk.put(i, tl)
            tl = stt(y3[:, k, :], y3[:, k, :], pc(f"ln_b{j}", k), v3_[:, k, :], ALU.add, ALU.add, tl)
            t_o = tt(G, y3[:, k, :], y3[:, k, :], a3[:, k, :], ALU.mult, tl, t_g[k])
        state["x"] = lin(D, D, lambda I, n0, n1: np.asarray(I["rw_w_o_2"])[j][:, n0:n1], y3, t_o, gated_residual(l, 1))

    phases = [nsa, lambda: moe(0), lambda: ple(0), moba, lambda: moe(1), lambda: ple(1)]

    def make(l, mixer):
        return [lambda: ffn(l, 0, 0), mixer, lambda: ffn(l, 2, 1)]

    phases += make(0, lambda: rwkv(0, 0)) + make(1, lambda: mamba(1)) + make(2, lambda: swa(2)) + make(3, lambda: rwkv(3, 1))
    for n, phase in enumerate(phases):
        if stop is not None and n not in stop:
            continue
        phase()

    d_x = nc.dram_tensor("xT_in", [128, 2048], F32, kind="ExternalInput").ap()
    d_p = nc.dram_tensor("params", [128, L.cols], F32, kind="ExternalInput").ap()
    d_c = nc.dram_tensor("consts", [128, NC], F32, kind="ExternalInput").ap()
    d_w = nc.dram_tensor("weights", [L.size], F32, kind="ExternalInput").ap()
    d_o = nc.dram_tensor("xT_out", [128, 2048], F32, kind="ExternalOutput").ap()

    def start(e):
        e.dma_start(xT[:, :], d_x).then_inc(s_in, 16)
        e.dma_start(prm[:, :], d_p).then_inc(s_in, 16)
        return e.dma_start(cst[:, :], d_c).then_inc(s_in, 16)

    SP(start, inc=False)
    for off, rows, cols, dst, sm_, fr in loads:
        src = d_w[off:off + rows * cols].rearrange("(p n) -> p n", p=rows)
        SP(lambda e, dst=dst, src=src, sm_=sm_: e.dma_start(dst, src).then_inc(sm_, 16), fr, inc=False)
    SP(lambda e: e.dma_start(d_o, xT[:, :]).then_inc(s_out, 16), state["x"], inc=False)

    with ctx, nc.Block() as block:
        @block.sync
        def _(e):
            SP.emit(e)
            e.wait_ge(s_out, 16)

        @block.tensor
        def _(e):
            e.wait_ge(s_in, 48)
            PE.emit(e)

        @block.vector
        def _(e):
            e.wait_ge(s_in, 48)
            V.emit(e)

        @block.scalar
        def _(e):
            e.wait_ge(s_in, 48)
            A.emit(e)

        @block.gpsimd
        def _(e):
            e.wait_ge(s_in, 48)
            G.emit(e)

    return L, consts


STOP = None


def kernel(**inputs):
    import concourse.bacc as bacc
    from concourse.bass_utils import run_bass_kernel_spmd as run

    nc = bacc.Bacc("TRN2", target_bir_lowering=False, num_devices=1)
    L, consts = build_program(nc, STOP)
    inputs = {k: np.asarray(v) for k, v in inputs.items()}
    small, flat = L.fill(inputs)
    maps = {"xT_in": np.ascontiguousarray(ktiles(inputs["x"][0].T)), "params": small, "consts": consts, "weights": flat}
    r = run(nc, [maps], core_ids=[0])
    o = np.asarray(r.results[0]["xT_out"])
    return np.ascontiguousarray(o.reshape(128, 8, 256).transpose(2, 1, 0).reshape(1, 256, 1024))
```

```python
from contextlib import ExitStack

import numpy as np

import concourse.bass as bass
import concourse.mybir as mybir
from concourse.alu_op_type import AluOpType as ALU

F32 = mybir.dt.float32
FR = mybir.dt.float32r
I32 = mybir.dt.int32
ACT = mybir.ActivationFunctionType
AX = mybir.AxisListType

T = 256
D = 1024
KD = 8
SLOT = 3072
NSLOT = 4
PIECE = 1024
NPIECE = 8
BIG = 1e30
RSQRT_MAGIC = 1597463007.0
HEADS = [(2 * t + hp) * 4 + r for t in range(2) for r in range(4) for hp in range(2)]
SLOPES = [float(2.0 ** (-8.0 * (i + 1) / 16)) for i in range(16)]


class Queue:

    def __init__(self, sem):
        self.sem, self.ops, self.n = sem, [], 0

    def __call__(self, fn, *waits, inc=True):
        self.ops.append((waits, fn, inc))
        self.n += inc
        return (self.sem, self.n)

    @property
    def last(self):
        return (self.sem, self.n)

    def emit(self, eng):
        seen = {}

        def wait(w):
            if w is None:
                return
            if isinstance(w, (list, tuple)) and not (len(w) == 2 and isinstance(w[1], int)):
                for x in w:
                    wait(x)
                return
            sem, value = w
            if value > seen.get(sem.name, 0):
                eng.wait_ge(sem, value)
                seen[sem.name] = value

        for waits, fn, inc in self.ops:
            wait(waits)
            ins = fn(eng)
            if inc:
                ins.then_inc(self.sem, 1)


def shape_constants():
    p = np.arange(128)[:, None]
    f = np.arange(128)[None, :]
    cols, at = {}, 0
    parts = []

    def add(name, a):
        nonlocal at
        a = np.asarray(a, np.float32)
        cols[name] = (at, a.shape[1])
        at += a.shape[1]
        parts.append(a)

    add("ident", p == f)
    add("blk64", (p // 64) == (f // 64))
    q = np.arange(128)[:, None]
    tri = np.where(q >= f, q - f, BIG)
    add("dist", np.concatenate([tri, q + 128 - f, tri], 1))
    add("swa", np.concatenate([np.where(q >= f, 0, -BIG), np.where(f > q, 0, -BIG), np.where(q >= f, 0, -BIG)], 1))
    slopes = np.array(SLOPES)[HEADS][None, :, None]
    for qb in range(2):
        t = (np.arange(128) + 128 * qb)[:, None, None]
        end = (np.arange(15) * 16 + 31)[None, None, :]
        dist = (t - end).astype(np.float32)
        add(f"cmp{qb}", np.where(dist >= 0, -slopes * dist, -BIG).reshape(128, 240))
    same = lambda n: (p // n) == (f // n)
    add("L16", same(16) & (f < p))
    add("U16", same(16) & (f > p))
    add("Lo32", same(32) & ~same(16) & (f < p))
    add("Uo32", same(32) & ~same(16) & (f > p))
    add("Lo64", same(64) & ~same(32) & (f < p))
    add("U64", same(64) & (f > p))
    add("Ui64", same(64) & (f >= p))
    add("S384", np.concatenate([f >= p, np.ones((128, 128)), f >= p], 1))
    add("half", p % 32 == (np.arange(1024)[None, :] // 64))
    add("reset", np.broadcast_to((np.arange(256) % 64 != 0)[None, :], (128, 256)))
    return np.concatenate(parts, 1), cols


def feat(v):
    v = np.asarray(v).reshape(-1, 128)
    return v.T


def twice(v):
    v = np.asarray(v).reshape(64, 1)
    return np.concatenate([v, v], 0)


def ktiles(w):
    w = np.asarray(w)
    k = w.shape[0] // 128
    return w.reshape(k, 128, w.shape[1]).transpose(1, 0, 2).reshape(128, k * w.shape[1])


def head_cols(w):
    w = np.asarray(w)
    return w.reshape(w.shape[0], 16, -1)[:, HEADS].reshape(w.shape)


def head_rows_of(w):
    w = np.asarray(w)
    return w.reshape(16, 64, -1)[HEADS].reshape(w.shape)


def dup_heads(w):
    w = np.asarray(w)
    w = w.reshape(w.shape[0], -1, 1, 64)
    return np.concatenate([w, w], 2).reshape(w.shape[0], -1)


class Layout:

    def __init__(self):
        self.params, self.chunks = [], []
        self.cols, self.size = 0, 0

    def param(self, rows, cols, fn):
        at = self.cols
        self.params.append((at, rows, cols, fn))
        self.cols += cols
        return at

    def chunk(self, rows, cols, fn):
        at = self.size
        self.chunks.append((at, rows, cols, fn))
        self.size += rows * cols
        return at

    def fill(self, inputs):
        small = np.zeros((128, self.cols), np.float32)
        for at, rows, cols, fn in self.params:
            a = np.asarray(fn(inputs))
            assert a.shape == (rows, cols), (a.shape, rows, cols)
            small[:rows, at:at + cols] = a
        flat = np.empty((self.size,), np.float32)
        for at, rows, cols, fn in self.chunks:
            a = np.asarray(fn(inputs))
            assert a.shape == (rows, cols), (a.shape, rows, cols)
            flat[at:at + rows * cols] = a.reshape(-1)
        return small, flat


def plan_params(L):
    c = {}

    def vec(name, n, fn):
        c[name] = L.param(128, n, fn)

    for i in range(2):
        vec(f"ln_mix{i}", 8, lambda I, i=i: feat(I["ln_mix"][i]))
        vec(f"ln_ffn{i}", 8, lambda I, i=i: feat(I["ln_ffn"][i]))
        vec(f"ln_ple{i}", 8, lambda I, i=i: feat(I["ln_ple"][i]))
        c[f"moe_b{i}"] = L.param(36, 1, lambda I, i=i: np.concatenate(
            [np.asarray(I["moe_b_group"])[i], np.asarray(I["moe_b_expert"])[i]])[:, None])
        vec(f"moe_w{i}", 288, lambda I, i=i: ktiles(np.concatenate(
            [np.asarray(I["moe_w_group"])[i], np.asarray(I["moe_w_expert"])[i]], 1)))
        vec(f"p{i}", 512, lambda I, i=i: ktiles(np.asarray(I["p"])[i, 0].T))
    vec("kv_norm", 8, lambda I: feat(I["kv_norm"]))
    vec("a_q", 1, lambda I: twice(np.asarray(I["a_q_norm"])[0]))
    for j in range(3):
        vec(f"a_k{j}", 1, lambda I, j=j: twice(np.asarray(I["a_k_norm"])[0, j]))
    vec("k_shared", 1, lambda I: twice(I["k_norm_shared"]))
    vec("b_q", 1, lambda I: twice(np.asarray(I["b_q_norm"])[0]))
    vec("sw_q", 1, lambda I: twice(np.asarray(I["sw_q_norm_2"])[0]))
    vec("sw_k", 1, lambda I: twice(np.asarray(I["sw_k_norm_2"])[0]))
    vec("sinks", 16, lambda I: np.broadcast_to(np.asarray(I["sw_sinks_2"])[0][HEADS][None, :], (128, 16)))
    for n in ("ck", "cv"):
        vec(f"{n}_pos", 16, lambda I, n=n: np.asarray(I[f"a_{n}_pos"])[0].reshape(16, 128).T)
    vec("c", 8, lambda I: feat(np.asarray(I["c_2"])[0]))
    for l in range(4):
        vec(f"ada_b{l}", 72, lambda I, l=l: feat(np.asarray(I["ada_b_2"])[l]))
        for s in range(3):
            vec(f"ng{l}{s}", 8, lambda I, l=l, s=s: feat(np.asarray(I["norm_g_2"])[l, s]))
    for j in range(2):
        for m in range(6):
            vec(f"mu{j}{m}", 8, lambda I, j=j, m=m: feat(np.asarray(I["rw_mu_2"])[j, m]))
        for n in ("w0", "a0", "k_k", "k_a", "ln_w", "ln_b"):
            vec(f"{n}{j}", 8, lambda I, j=j, n=n: feat(np.asarray(I[f"rw_{n}_2"])[j]))
        vec(f"r_k{j}", 8, lambda I, j=j: feat(np.asarray(I["rw_r_k_2"])[j].reshape(-1)))
    vec("v01", 8, lambda I: feat(np.asarray(I["rw_v0_2"])[0]))
    for k in range(4):
        vec(f"conv{k}", 32, lambda I, k=k: feat(np.asarray(I["mb_conv_w_2"])[0, k]))
    vec("conv_b", 32, lambda I: feat(np.asarray(I["mb_conv_b_2"])[0]))
    vec("mb_g", 16, lambda I: feat(np.asarray(I["mb_norm_g_2"])[0]))
    vec("mb_D", 16, lambda I: feat(np.repeat(np.asarray(I["mb_D_2"])[0], 64)))
    c["dt_bias"] = L.param(32, 1, lambda I: np.asarray(I["mb_dt_bias_2"])[0][:, None])
    c["A_log"] = L.param(32, 1, lambda I: np.asarray(I["mb_A_log_2"])[0][:, None])
    return c


def build_program(nc, stop=None):
    consts, ccol = shape_constants()
    L = Layout()
    pcol = plan_params(L)
    ctx = ExitStack()
    NC = consts.shape[1]

    def sb(name, cols, dt=F32, rows=128):
        return ctx.enter_context(nc.sbuf_tensor(name, [rows, cols], dt))

    def sem(name):
        return ctx.enter_context(nc.semaphore(name))

    PE, V, A, G, SP = (Queue(sem(f"s_{n}")) for n in ("pe", "dve", "act", "pool", "sp"))

    def now():
        return (PE.last, V.last, A.last, G.last)

    xT = sb("xT", 2048)
    hT = sb("hT", 2048)
    sq = sb("sq", 2048)
    vfirst = sb("vfirst", 2048)
    prm = sb("prm", L.cols)
    cst = sb("cst", NC)
    ones = sb("ones", 256)
    mods = sb("mods", 288)
    cact = sb("cact", 8)
    rsb = sb("rsb", 256)
    nv, nm, nt = sb("nv", 256), sb("nm", 256), sb("nt", 256)
    gs = sb("gs", 16)
    ring = sb("ring", NSLOT * SLOT)
    selw, selg = sb("selw", 128), sb("selg", 64)
    hr, bsum = sb("hr", 256, rows=48), sb("bsum", 256, rows=16)
    dl = sb("dl", 32)
    WK = 23 * 1024 - 64
    with nc.sbuf_tensor("wk", [128, WK], F32) as region:
        wk = region
    with ExitStack() as other:
        def sc(name, cols, dt):
            return other.enter_context(nc.sbuf_tensor(name, [128, cols], dt))

        ex = sc("ex", 3 * 512, FR)
        ada_acc = sc("ada_acc", 768, F32)
        sc("pad", WK - 2304 - 2 * NPIECE * PIECE - 4096, F32)
        wp = sc("wp", 2 * NPIECE * PIECE, FR)
        hx = sc("hx", 4096, FR)
    with ExitStack() as other:
        other.enter_context(nc.sbuf_tensor("below_hz", [128, 4096], F32))
        hz = other.enter_context(nc.sbuf_tensor("hz", [128, 4096], FR))
        ha = other.enter_context(nc.sbuf_tensor("ha", [128, 4096], FR))
    pb = [ctx.enter_context(nc.psum_tensor(f"pb{i}", [128, 512], F32)) for i in range(8)]

    def v3(t, c0, n, w):
        return t[:, c0:c0 + n * w].rearrange("p (n w) -> p n w", w=w)

    def C(name, rows=128):
        a, n = ccol[name]
        return cst[0:rows, a:a + n]

    def pc(name, i=0, n=1, rows=128):
        return prm[0:rows, pcol[name] + i:pcol[name] + i + n]

    ident = C("ident")
    X3, H3, Q3 = (v3(t, 0, 8, T) for t in (xT, hT, sq))

    def tt(q, out, a, b, op, *w):
        return q(lambda e: e.tensor_tensor(out, a, b, op), *w)

    def ts(q, out, a, s1, s2, op0, op1, *w):
        if op1 is None:
            return q(lambda e: e.tensor_scalar(out, a, s1, None, op0), *w)
        return q(lambda e: e.tensor_scalar(out, a, s1, s2, op0, op1), *w)

    def stt(out, a, s, b, op0, op1, *w):
        return V(lambda e: e.scalar_tensor_tensor(out=out, in0=a, scalar=s, in1=b, op0=op0, op1=op1), *w)

    def cp(q, out, a, *w):
        if q is A:
            return q(lambda e: e.activation(out, a, ACT.Copy), *w)
        return q(lambda e: e.tensor_copy(out, a), *w)

    def act(out, a, func, *w, bias=0.0, scale=1.0, accum=None):
        return A(lambda e: e.activation(out, a, func, bias=bias, scale=scale, accum_out=accum), *w)

    def mm(out, l, r, start, stop, *w, inc=False, skip=False):
        return PE(lambda e: e.matmul(out, l, r, start=start, stop=stop, skip_group_check=skip), *w, inc=inc)

    def tp(out, a, *w, inc=False):
        n = a.shape[0]
        base = a.base_partition() if callable(a.base_partition) else a.base_partition
        idn = cst[base:base + n, ccol["ident"][0] + base:ccol["ident"][0] + base + n]
        return PE(lambda e: e.transpose(out, a, idn), *w, inc=inc)

    def recip(out, a, *w):
        return V(lambda e: e.reciprocal(out, a), *w)

    def red(out, a, op, *w):
        return V(lambda e: e.tensor_reduce(out, a, AX.X, op), *w)

    class Banks:
        def __init__(self):
            self.free = [None] * 8
            self.ids, self.at = list(range(8)), 0

        def use(self, ids):
            self.ids, self.at = list(ids), 0

        def get(self):
            i = self.ids[self.at % len(self.ids)]
            self.at += 1
            return i, pb[i], self.free[i]

        def put(self, i, *toks):
            self.free[i] = toks

    bk = Banks()

    class Ring:
        def __init__(self):
            self.sems = [sem(f"s_ring{i}") for i in range(NSLOT)]
            self.free = [None] * NSLOT
            self.uses = [0] * NSLOT
            self.at = 0

        def get(self, rows, cols, fn):
            assert cols <= SLOT
            i = self.at % NSLOT
            self.at += 1
            self.uses[i] += 1
            off = L.chunk(rows, cols, fn)
            dst = ring[0:rows, i * SLOT:i * SLOT + cols]
            loads.append((off, rows, cols, dst, self.sems[i], self.free[i]))
            return i, dst, (self.sems[i], 16 * self.uses[i])

        def put(self, i, tok):
            self.free[i] = tok

    loads = []
    rg = Ring()
    s_in, s_out = sem("s_in"), sem("s_out")
    loaded = (s_in, 48)

    def rsqrt(out, src, P, N, mult, add, tok):
        a, b, c = nv[0:P, 0:N], nm[0:P, 0:N], nt[0:P, 0:N]
        t0 = ts(V, a, src, mult, add, ALU.mult, ALU.add, tok, V.last)
        return t0, rsqrt_of(out, a, b, c)

    def rsqrt_of(out, a, b, c):
        ts(V, out.bitcast(I32), a.bitcast(I32), -0.5, RSQRT_MAGIC, ALU.mult, ALU.add, V.last)
        t = ts(V, b, a, -0.5, None, ALU.mult, None, V.last)
        for _ in range(3):
            t = tt(V, c, out, out, ALU.mult, t)
            t = tt(V, c, c, b, ALU.mult, t)
            t = stt(out, c, 1.5, out, ALU.add, ALU.mult, t)
        return t

    def dnorm(between=lambda: None):
        (i0, p0, f0), (i1, p1, f1) = bk.get(), bk.get()
        t_sum = [None, None]
        for k in range(KD):
            t = act(Q3[:, k, :], X3[:, k, :], ACT.Square, state["x"][k])
            t_sum[k % 2] = t if k < 2 else tt(V, Q3[:, k % 2, :], Q3[:, k % 2, :], Q3[:, k, :], ALU.add, t, t_sum[k % 2])
        for k in range(2):
            mm(p0[:, 0:1], Q3[:, k, 0:128], ones[:, 0:1], k == 0, k == 1, f0, t_sum[k])
            mm(p1[:, 0:1], Q3[:, k, 128:256], ones[:, 0:1], k == 0, k == 1, f1, inc=(k == 1))
        between()
        a, b, c, r = nv[:, 0:2], nm[:, 0:2], nt[:, 0:2], nt[:, 2:4]
        for n, ps in enumerate((p0, p1)):
            t1 = ts(V, nv[:, n:n + 1], ps[:, 0:1], 1.0 / D, 1e-6, ALU.mult, ALU.add, PE.last, V.last)
        bk.put(i0, t1)
        bk.put(i1, t1)
        t = rsqrt_of(r, a, b, c)
        i, ps, fr = bk.get()
        for n in range(2):
            d = rsb[:, n * 128:(n + 1) * 128]
            t1 = ts(V, d, ident, nt[:, 2 + n:3 + n], None, ALU.mult, None, t, PE.last)
            t2 = mm(ps[:, n * 128:(n + 1) * 128], ones[:, 0:128], d, True, True, fr, t1, inc=(n == 1))
        t = cp(V, rsb[:, :], ps[:, 0:T], t2)
        bk.put(i, t)
        return t

    def tokmajor(rhs, n, wtok, h, h_tok, evac):
        t = None
        for tb in range(2):
            i, ps, fr = bk.get()
            for k in range(KD):
                t = mm(ps[:, 0:n], h[:, k, tb * 128:(tb + 1) * 128], rhs[:, k, :], k == 0, k == KD - 1,
                       fr, wtok, h_tok, inc=(k == KD - 1))
            bk.put(i, evac(tb, ps[:, 0:n], t))
        return t

    def half_select(k):
        return selw[:, k * 16:(k + 1) * 16]

    def head_rows(src, nt_, n, tok):
        i, ps, fr = bk.get()
        for k in range(nt_):
            t = mm(ps[0:16, 0:n], half_select(k), src[:, k, :], k == 0, k == nt_ - 1, fr, tok, inc=(k == nt_ - 1))
        return i, ps[0:2 * nt_, 0:n], t

    def head_bcast(rows, k, n, tok):
        i, ps, fr = bk.get()
        sel = C("half", 16)[:, k * 128:(k + 1) * 128]
        t = mm(ps[:, 0:n], sel, rows, True, True, fr, tok, inc=True)
        return i, ps[:, 0:n], t

    def head_norms(groups):
        for base, g in zip((0, 32), groups):
            n, sq3 = g["n"], g["sq"]
            i, ps, fr = bk.get()
            nt_ = len(g["toks"])
            for k in range(nt_):
                t = mm(ps[base:base + 16, 0:n], half_select(k), sq3[:, k, :], k == 0, k == nt_ - 1,
                       fr, g["toks"][k], inc=(k == nt_ - 1))
            m = 1.0 / (64 * g["scale"] ** 2)
            t0 = ts(V, nv[base:base + 16, 0:n], ps[base:base + 16, 0:n], m, 64 * m * 1e-6, ALU.mult, ALU.add, t, V.last)
            bk.put(i, t0)
        rows, n = (16 if len(groups) == 1 else 48), groups[0]["n"]
        t = rsqrt_of(hr[0:rows, 0:n], nv[0:rows, 0:n], nm[0:rows, 0:n], nt[0:rows, 0:n])

        def finish():
            out = []
            for base, g in zip((0, 32), groups):
                toks = []
                for k in range(len(g["toks"])):
                    i, ps, fr = bk.get()
                    sel = cst[base:base + 16, ccol["half"][0] + k * 128:ccol["half"][0] + (k + 1) * 128]
                    tb = mm(ps[:, 0:n], sel, hr[base:base + 16, 0:n], True, True, fr, t, inc=True)
                    d = g["dst"][:, k, :]
                    gain = g["gain"](k)
                    toks.append(stt(d, d, gain, ps[:, 0:n], ALU.mult, ALU.mult, tb, g["toks"][k]))
                    bk.put(i, toks[-1])
                out.append(toks)
            return out

        return finish

    def keep_squares(dst, sq3, toks, ph, at=0):
        def evac(m, ps, t):
            t1 = cp(V, dst[:, at + m, :], ps, t, ph)
            toks.append(act(sq3[:, at + m, :], dst[:, at + m, :], ACT.Square, t1, ph))
            return t1
        return evac

    V(lambda e: e.memset(ones[:, :], 1.0))
    V(lambda e: e.memset(nv[:, :], 1.0))
    V(lambda e: e.memset(selw[:, :], 0.0))
    t_sel = V.last
    for k in range(8):
        V(lambda e, k=k: e.memset(selw[0:64, k * 16 + 2 * k:k * 16 + 2 * k + 1], 1.0), t_sel)
        V(lambda e, k=k: e.memset(selw[64:128, k * 16 + 2 * k + 1:k * 16 + 2 * k + 2], 1.0), t_sel)
    t_sel = V.last

    state = {"x": [(loaded, t_sel)] * 8}
    act(cact[:, :], pc("c", 0, 8), ACT.Silu, loaded)

    ada = {"at": 0, "tok": {}, "free": None, "pend": None}

    def ada_next(*free):
        if ada["at"] >= 96:
            return
        l, c = divmod(ada["at"], 24)
        ada["at"] += 1
        s, wt, wtok = rg.get(128, 3072, lambda I: ktiles(np.asarray(I["ada_w_2"])[l][:, c * 384:(c + 1) * 384]))
        w = wt.rearrange("p (k n) -> p k n", k=8)
        acc = [ada_acc[:, n * 384:(n + 1) * 384] for n in range(2)]
        tk = [act(acc[n], w[:, n, :], ACT.Copy, wtok, t_cact, ada["free"], free, scale=cact[:, n:n + 1]) for n in range(2)]
        for k in range(2, 8):
            n = k % 2
            t = tk[n] = stt(acc[n], w[:, k, :], cact[:, k:k + 1], acc[n], ALU.mult, ALU.add, tk[n])
        rg.put(s, t)
        ada["pend"] = (l, c, tt(V, acc[0], acc[0], acc[1], ALU.add, tk))

    def ada_sum():
        if ada["pend"] is None:
            return None
        (l, c, t), ada["pend"] = ada["pend"], None
        i, ps, fr = bk.get()
        for j in range(3):
            t_p = mm(ps[:, j:j + 1], ada_acc[:, j * 128:(j + 1) * 128], ones[:, 0:1], True, True, fr, t, inc=(j == 2))
        ada["free"] = t_p
        a = c * 3

        def add():
            tl = tt(V, mods[:, l * 72 + a:l * 72 + a + 3], ps[:, 0:3], pc(f"ada_b{l}", a, 3), ALU.add, t_p)
            bk.put(i, tl)
            ada["tok"][l] = tl

        return add

    t_cact = A.last

    def mod(l, s, which, k):
        return mods[:, l * 72 + s * 24 + which * 8 + k:l * 72 + s * 24 + which * 8 + k + 1]

    Hh, Hl = v3(hx, 0, 8, T), v3(hx, 2048, 8, T)
    piece = {"n": 0, "free": [None] * NPIECE}

    def split_piece(raw, q, *w):
        i = piece["n"] % NPIECE
        piece["n"] += 1
        hi, lo = (wp[:, (2 * i + j) * PIECE:(2 * i + j + 1) * PIECE] for j in range(2))
        ta = act(hi, raw, ACT.Copy, w, piece["free"][i])
        if q is not None:
            return i, tt(q, lo, raw, hi, ALU.subtract, ta)
        h = PIECE // 2
        return i, (tt(V, lo[:, 0:h], raw[:, 0:h], hi[:, 0:h], ALU.subtract, ta),
                   tt(G, lo[:, h:], raw[:, h:], hi[:, h:], ALU.subtract, ta))

    def mm3(out, w, x, start, stop, *toks, inc=False):
        mm(out, w[0], x[0], start, False, toks, skip=True)
        mm(out, w[0], x[1], False, False, skip=True)
        return mm(out, w[1], x[0], False, stop, inc=inc, skip=True)

    def weight(i, c, n=128):
        return [wp[:, (2 * i + j) * PIECE + c:(2 * i + j) * PIECE + c + n] for j in range(2)]

    class Products:

        def __init__(self, slots, ph, *specs, ahead=None, share=False):
            self.slots, self.ph, self.share, self.n = list(slots), ph, share, 0
            self.gen, self.specs, self.ahead = self.pieces(specs), list(specs), []
            self.lead = G
            self.more(len(self.slots) if ahead is None else ahead)
            self.lead = None

        def split(self, raw, *w):
            slot = self.slots[self.n % len(self.slots)]
            self.n += 1
            k, n = raw.shape[1], raw.shape[2]
            hi, lo = (wp[:, (2 * slot + j) * PIECE:(2 * slot + j) * PIECE + k * n].rearrange("p (k n) -> p k n", k=k)
                      for j in range(2))
            t = act(hi, raw, ACT.Copy, w, self.ph, piece["free"][slot])
            if self.lead is not None and self.n % 2:
                return hi, lo, tt(G, lo, raw, hi, ALU.subtract, t), slot
            if not self.share:
                return hi, lo, tt(V, lo, raw, hi, ALU.subtract, t), slot
            h = k // 2
            return hi, lo, (tt(V, lo[:, 0:h], raw[:, 0:h], hi[:, 0:h], ALU.subtract, t),
                            tt(G, lo[:, h:], raw[:, h:], hi[:, h:], ALU.subtract, t)), slot

        def pieces(self, specs):
            for N, K, fn in specs:
                KT = K // 128
                if N is None:
                    s, wt, wtok = rg.get(128, KT * 256, lambda I, fn=fn: ktiles(fn(I)))
                    w = wt.rearrange("p (k n) -> p k n", k=KT)
                    used = []
                    for j in range(0, KT, 4):
                        p = self.split(w[:, j:j + 4], wtok)
                        used.append(p[2])
                        if j + 4 == KT:
                            rg.put(s, used)
                        yield (0, 1, j) + p
                    continue
                per = max(1, SLOT // (KT * 128))
                kk, group = min(KT, 8), max(1, 8 // KT)
                for m0 in range(0, N // 128, per):
                    n = min(per, N // 128 - m0)
                    s, wt, wtok = rg.get(128, KT * n * 128,
                                         lambda I, fn=fn, a=m0 * 128, b=(m0 + n) * 128: ktiles(fn(I, a, b)))
                    w = wt.rearrange("p (k n) -> p k n", k=KT)
                    todo = [(j, min(group, n - j), p) for j in range(0, n, group) for p in range(max(1, KT // 8))]
                    used = []
                    for j, g, p in todo:
                        q = self.split(w[:, p * kk:(p + 1) * kk, j * 128:(j + g) * 128], wtok)
                        used.append(q[2])
                        if len(used) == len(todo):
                            rg.put(s, used)
                        yield (m0 + j, g, p) + q

        def more(self, n=1):
            for _ in range(n):
                if any(p[-1] == self.slots[self.n % len(self.slots)] for p in self.ahead):
                    return
                p = next(self.gen, None)
                if p is not None:
                    self.ahead.append(p)

        def take(self, n):
            if len(self.ahead) < n:
                self.more(max(n, len(self.slots)) - len(self.ahead))
            out = self.ahead[:n]
            del self.ahead[:n]
            return out

        def lin(self, x, x_tok, evac):
            N, K, _ = self.specs.pop(0)
            KT, toks = K // 128, []
            kk, parts = min(KT, 8), max(1, KT // 8)
            while len(toks) < N // 128:
                first = self.take(parts)
                m, g = first[0][0:2]
                done = []
                for j in range(g):
                    i, ps, fr = bk.get()
                    for _, _, p, hi, lo, tw, slot in first:
                        for k in range(kk):
                            c = p * kk + k
                            t = mm3(ps[:, 0:T], [a[:, k, j * 128:(j + 1) * 128] for a in (hi, lo)], x(c), c == 0, c == KT - 1,
                                    fr, tw, x_tok[c], inc=(k == kk - 1))
                        piece["free"][slot] = t
                    done.append((m + j, i, ps, t))
                self.more(parts)
                for m_, i, ps, t in done:
                    toks.append(evac(m_, ps[:, 0:T], t))
                    bk.put(i, toks[-1])
            return toks

        def tokmajor(self, x, x_tok, evac):
            _, K, _ = self.specs.pop(0)
            KT, toks = K // 128, []
            ps_ = self.take(KT // 4)
            for tb in range(2):
                i, ps, fr = bk.get()
                for k in range(KT):
                    _, _, _, hi, lo, tw, slot = ps_[k // 4]
                    t = mm3(ps[:, 0:256], [a[:, tb * 128:(tb + 1) * 128] for a in x(k)], (hi[:, k % 4, :], lo[:, k % 4, :]),
                            k == 0, k == KT - 1, fr, tw, x_tok[k], inc=(k % 4 == 3))
                    if tb == 1 and k % 4 == 3:
                        piece["free"][slot] = t
                if tb == 1:
                    self.more(len(ps_))
                toks.append(evac(tb, ps[:, 0:256], t))
                bk.put(i, toks[-1])
            return toks

    def norm_to(hi, lo, gain, tok, ph):
        t_n, t_s = [], []
        for k in range(KD + 1):
            if k < KD:
                t_n.append(stt(H3[:, k, :], X3[:, k, :], gain(k), rsb[:, :], ALU.mult, ALU.mult, tok, ph))
                t_s.append(act(hi[:, k, :], H3[:, k, :], ACT.Copy, t_n[k], ph))
            if k > 0:
                n = k - 1
                t_s[n] = tt(V, lo[:, n, :], H3[:, n, :], hi[:, n, :], ALU.subtract, t_s[n])
        return t_n, t_s

    in_hx = lambda k: (Hh[:, k, :], Hl[:, k, :])
    Zh, Zl = v3(hz, 0, 8, T), v3(hz, 2048, 8, T)
    in_hz = lambda k: (Zh[:, k, :], Zl[:, k, :])

    def to_hx(ph):
        def evac(m, ps, t):
            t = act(Hh[:, m, :], ps, ACT.Copy, t, ph)
            return lambda: tt(V, Hl[:, m, :], ps, Hh[:, m, :], ALU.subtract, t)
        return evac

    class Units:

        def __init__(self, fn):
            self.fn, self.u, self.ph, self.ready = fn, 0, now(), []

        def fetch(self, then=None):
            u = self.u
            self.u += 1
            s, w, wtok = rg.get(128, 3072, lambda I: self.fn(I, u))
            raw = [w[:, j * PIECE:(j + 1) * PIECE] for j in range(3)]
            if then is None:
                ps = [split_piece(raw[j], q, wtok, self.ph) for j, q in enumerate((V, None, G))]
            else:
                i0, i1 = (split_piece(raw[j], G, wtok, self.ph) for j in range(2))
                then()
                ps = [i0, i1, split_piece(raw[2], G, wtok, self.ph)]
            rg.put(s, [t for _, t in ps])
            self.ready.append(ps)

    def squares(tok):
        return [tt(G, Q3[:, k, :], X3[:, k, :], X3[:, k, :], ALU.mult, state["x"][k], tok) for k in range(KD)]

    def late_norm(b, t_sq):
        for k in range(KD):
            t = mm(pb[b][:, 0:T], ones[:, 0:128], Q3[:, k, :], k == 0, k == KD - 1, bk.free[b], t_sq[k], inc=(k == KD - 1))
        return pb[b], t

    def glu(units, src, z_tok, evac, hooks=(lambda: None,), cw=None):
        ph = now()
        bk.use([4, 5, 6, 7])
        Y = [pb[i] for i in range(4)]
        sg = [sq[:, 768 + i * 256:768 + (i + 1) * 256] for i in range(3)]
        eh = [ex[:, i * 512:i * 512 + 256] for i in range(3)]
        el = [ex[:, i * 512 + 256:(i + 1) * 512] for i in range(3)]
        e_free = [ph, ph, ph]
        made, pend = [], []
        first = len(hooks) - 1
        r_tok = None

        def products(u):
            (wa, ta), (wb, tb), (wd, td) = src.ready.pop(0)
            i, ps, fr = bk.get()
            for b, (wi, wtok) in enumerate(((wa, ta), (wb, tb))):
                for k in range(KD):
                    t = mm3(ps[:, b * T:(b + 1) * T], weight(wi, k * 128), (Hh[:, k, :], Hl[:, k, :]), k == 0, k == KD - 1,
                            fr, wtok, z_tok[k], inc=(k == KD - 1))
                piece["free"][wi] = t
            made.append((u, i, t, wd, td))

        def hidden():
            u, i, t, wd, td = made.pop(0)
            n = u % 3
            g_, ps = sg[n], pb[i]
            if cw is None:
                t1 = act(g_, ps[:, 0:T], ACT.Silu, t, e_free[n])
                t2 = tt(V, g_, g_, ps[:, T:2 * T], ALU.mult, t, t1)
                bk.put(i, t2)
            else:
                ic, pcw, frc = bk.get()
                sel = cst[0:32, ccol["ident"][0] + u:ccol["ident"][0] + u + 1].to_broadcast([32, 128])
                tc = mm(pcw[:, 0:T], sel, cw, True, True, frc, r_tok, inc=True)
                t0 = tt(V, g_, ps[:, 0:T], rsb[:, :], ALU.mult, t, r_tok, e_free[n])
                t1 = act(g_, g_, ACT.Silu, t0)
                t2 = tt(V, g_, g_, ps[:, T:2 * T], ALU.mult, t, t1)
                bk.put(i, t2)
                t2 = tt(V, g_, g_, pcw[:, 0:T], ALU.mult, tc, t2)
                bk.put(ic, t2)
            t1 = act(eh[n], g_, ACT.Copy, t2, e_free[n])
            t2 = tt(V, el[n], g_, eh[n], ALU.subtract, t1)
            pend.append((u, wd, td, t2))

        def down(u, wi, wtok, t_hid):
            toks = []
            for m in range(8):
                t = mm3(Y[m // 2][:, (m % 2) * T:(m % 2 + 1) * T], weight(wi, m * 128), (eh[u % 3], el[u % 3]),
                        u == 0 and m % 2 == 0, u == units - 1, t_hid, wtok, bk.free[m // 2], inc=(m % 2 == 1))
                toks.append(t)
            piece["free"][wi] = t
            e_free[u % 3] = t
            return toks

        for u in range(units):
            products(u)
            if u < len(hooks):
                r_tok = hooks[u]()
            late_sum = ada_sum() if u % 2 else None
            early = u != first or first == 0
            if early and src.u == u + 1 < units:
                src.fetch()
            if u % 2 == 0 and u >= first:
                ada_next(ph)
            if u >= first:
                while made:
                    hidden()
                while len(pend) > 1:
                    down(*pend.pop(0))
            if not early and src.u == u + 1 < units:
                src.fetch()
            if late_sum:
                late_sum()
        t_y = down(*pend.pop(0))
        toks = [evac(m, Y[m // 2][:, (m % 2) * T:(m % 2 + 1) * T], t_y[m | 1]) for m in range(8)]
        for i in range(4):
            bk.put(i, toks[2 * i + 1])
        bk.use(range(8))
        return toks

    def attention(units, off, evac):
        ph = now()
        bk.use([2, 3, 4, 5, 6, 7])
        NB = 4
        sbuf = [wk[:, off + i * 384:off + (i + 1) * 384] for i in range(NB)]
        ptb = [wk[:, off + (NB + i) * 384:off + (NB + i + 1) * 384] for i in range(NB)]
        stb = [wk[:, off + 2 * NB * 384 + i * 8:off + 2 * NB * 384 + (i + 1) * 8] for i in range(NB)]
        sfree, pfree = [ph] * NB, [ph] * NB
        st, out, whole = {}, [], []

        def scores(n, u):
            i, ps, fr = bk.get()
            mm(ps[:, 0:128], u["q"][:, 0:128], u["k"][:, 0:128], True, True, fr, u["tok"])
            t = mm(ps[:, 128:384], u["q"][:, 128:256], u["k"][:, 0:256], True, True, inc=True)
            st[n] = (i, ps, t)

        def softmax(n, u):
            i, ps, t = st[n]
            b, s = sbuf[n % NB], stb[n % NB]
            init = u["sink"] if u["sink"] is not None else -3e38
            for qb, (a, z) in enumerate(((0, 128), (128, 384))):
                tm = V(lambda e, qb=qb, a=a, z=z: e.tensor_tensor_reduce(
                    out=b[:, a:z], in0=u["bias"][:, a:z], in1=ps[:, a:z], scale=1.0, scalar=init,
                    op0=ALU.add, op1=ALU.max, accum_out=s[:, qb:qb + 1]), t, sfree[n % NB], u["btok"])
            bk.put(i, tm)
            tm = ts(V, s[:, 2:4], s[:, 0:2], -1.0, None, ALU.mult, None, tm)
            te = None
            for qb, (a, z) in enumerate(((0, 128), (128, 384))):
                te = act(b[:, a:z], b[:, a:z], ACT.Exp, tm, bias=s[:, 2 + qb:3 + qb], accum=s[:, 4 + qb:5 + qb])
            if u["sink"] is not None:
                te = act(s[:, 6:8], s[:, 2:4], ACT.Exp, tm, bias=u["sink"])
            st[n] = te

        def normalise(n, u):
            b, s = sbuf[n % NB], stb[n % NB]
            t = st[n]
            if u["sink"] is not None:
                t = tt(V, s[:, 4:6], s[:, 4:6], s[:, 6:8], ALU.add, t)
            else:
                t = ts(V, s[:, 4:6], s[:, 4:6], 1e-30, None, ALU.max, None, t)
            t = recip(s[:, 4:6], s[:, 4:6], t)
            for qb, (a, z) in enumerate(((0, 128), (128, 384))):
                if u["gate"] is None:
                    tn = ts(V, b[:, a:z], b[:, a:z], s[:, 4 + qb:5 + qb], None, ALU.mult, None, t)
                else:
                    tn = ts(V, b[:, a:z], b[:, a:z], s[:, 4 + qb:5 + qb], u["gate"](qb), ALU.mult, ALU.mult, t, u["tok"])
            i, ps, fr = bk.get()
            for j in range(3):
                t = tp(ps[:, j * 128:(j + 1) * 128], b[:, j * 128:(j + 1) * 128], fr, tn, inc=(j == 2))
            sfree[n % NB] = t
            st[n] = (i, ps, t)

        def transposed(n, u):
            i, ps, t = st[n]
            st[n] = act(ptb[n % NB], ps[:, 0:384], ACT.Copy, t, pfree[n % NB])
            bk.put(i, st[n])

        def values(n, u):
            h = u["h"]
            hp = h % 2
            ob = pb[(h // 2) % 2]
            o = ob[64 * hp:64 * hp + 64, :]
            p = ptb[n % NB]
            fr = bk.free[(h // 2) % 2]
            first = u["first"]
            if first:
                for j, (l, r, et) in enumerate(u["extra"]):
                    mm(o[:, 0:T], l, r, first, False, fr, et, skip=True)
                    first = False
            mm(o[:, 0:T], u["v"](0), p[:, 0:256], first, False, fr, st[n], u["tok"], skip=True)
            t = mm(o[:, 128:256], u["v"](1), p[:, 256:384], False, u["last"], inc=True, skip=True)
            pfree[n % NB] = t
            if u["last"] and hp == 1:
                whole.append((h // 2, ob[:, 0:T], t))

        n = len(units)
        stages = ((scores, 0), (values, 4), (normalise, 3), (softmax, 1), (transposed, 3))
        for i in range(n + 5):
            late = [(m, evac(m, ps, t)) for m, ps, t in whole]
            whole.clear()
            for stage, lag in stages:
                if 0 <= i - lag < n:
                    stage(i - lag, units[i - lag])
            for m, low in late:
                out.append(low())
                bk.put(m % 2, out[-1])
        bk.use(range(8))
        return out

    def residual(m, ps, t):
        return tt(V, X3[:, m, :], X3[:, m, :], ps, ALU.add, t)

    def gated_residual(l, s):
        return lambda m, ps, t: stt(X3[:, m, :], ps, mod(l, s, 2, m), X3[:, m, :], ALU.mult, ALU.add, t)

    def alibi(offs, ph):
        out = [wk[:, o:o + 384] for o in offs]
        for h in range(16):
            t = ts(G, out[h], C("dist"), -SLOPES[HEADS[h]], None, ALU.mult, None, ph, loaded)
        return out, t

    def nsa():
        ph = now()
        W = lambda a, b: (lambda I: np.asarray(I["a_w_in"])[0][:, a:b])
        dup = lambda a: (lambda I, n0, n1: dup_heads(W(a, a + 256)(I))[:, n0:n1])
        cut = lambda a: (lambda I, n0, n1: W(a + n0, a + n1)(I))
        w = Products((5, 6, 7), ph, (512, D, dup(1024)), (512, D, dup(1280)), (256, D, cut(1536)), (256, D, cut(2048)),
                     (D, D, lambda I, n0, n1: head_cols(W(0, 1024)(I))[:, n0:n1]))
        t = dnorm()
        t_n, t_hx = norm_to(Hh, Hl, lambda k: pc("ln_mix0", k), t, ph)
        t_h = t_n[-1]
        o = 0

        def take(n):
            nonlocal o
            o += n
            return o - n

        qT = v3(wk, take(2048), 8, T)
        kT = v3(wk, take(1024), 4, T)
        vS, vW = v3(wk, take(512), 2, T), v3(wk, take(512), 2, T)
        gts = v3(wk, take(96), 2, 48)
        b_off = take(16 * 384)
        kcT = wk[:, take(60):o].rearrange("p (k n) -> p k n", n=60)
        vc = wk[0:15, take(256):o]
        a_off = take(3104)
        pct_off = take(4096)
        bias, t_bias = alibi([b_off + h * 384 for h in range(16)], ph)

        cmpr = {}
        for n, name in enumerate(("ck", "cv")):
            Xc = sq[:, n * 960:(n + 1) * 960].rearrange("p (k n) -> p k n", n=60)
            hid = wk[:, a_off + 1088 + n * 120:a_off + 1088 + (n + 1) * 120].rearrange("p (m n) -> p m n", n=60)
            pos = pc(f"{name}_pos", 0, 16)

            def to_windows(g, ps, t, Xc=Xc, pos=pos):
                pv = ps.rearrange("p (n k two) -> p two k n", k=8, two=2)
                for hf in range(2):
                    r = slice(64 * hf, 64 * hf + 64)
                    for kh in range(2):
                        tl = tt(V, Xc[r, kh * 8:(kh + 1) * 8, g * 15:(g + 1) * 15], pv[r, hf, :, kh:kh + 15],
                                pos[r, kh * 8:(kh + 1) * 8].unsqueeze(2).to_broadcast([64, 8, 15]), ALU.add, t, ph)
                return tl

            t_x = w.lin(in_hx, t_hx, to_windows)
            cmpr[name] = Xc, hid, t_x[-1]

        ksq = v3(wk, a_off, 4, T)
        t_ksq, t_qsq = [], []
        for n in range(2):
            w.lin(in_hx, t_hx, keep_squares(kT, ksq, t_ksq, ph, 2 * n))

        for name in ("ck", "cv"):
            Xc, hid, t_x = cmpr[name]
            for m in range(2):
                s, wt, wtok = rg.get(128, 2048, lambda I, m=m, name=name: ktiles(
                    np.asarray(I[f"a_{name}_w1"])[0][:, m * 128:(m + 1) * 128]))
                w1 = wt.rearrange("p (k n) -> p k n", k=16)
                i, ps, fr = bk.get()
                for k in range(16):
                    t = mm(ps[:, 0:60], w1[:, k, :], Xc[:, k, :], k == 0, k == 15, fr, wtok, t_x, inc=(k == 15))
                rg.put(s, t)
                t_g = act(hid[:, m, :], ps[:, 0:60], ACT.Gelu_apprx_tanh, t, ph)
                bk.put(i, t_g)
            cmpr[name] = hid, t_g

        hid, t_g = cmpr["ck"]
        s, wt, wtok = rg.get(128, 256, lambda I: ktiles(dup_heads(np.asarray(I["a_ck_w2"])[0])))
        w2 = wt.rearrange("p (k n) -> p k n", k=2)
        i, ps, fr = bk.get()
        for m in range(2):
            t = mm(ps[:, 0:60], w2[:, m, :], hid[:, m, :], m == 0, m == 1, fr, wtok, t_g, inc=(m == 1))
        rg.put(s, t)
        csq = wk[:, a_off + 1024:a_off + 1084].rearrange("p (k n) -> p k n", n=60)
        t_csq = []
        bk.put(i, keep_squares(kcT, csq, t_csq, ph)(0, ps[:, 0:60], t))
        kc_done = head_norms([dict(dst=kcT, sq=csq, toks=t_csq, n=60, gain=lambda k: pc("a_k0"), scale=1.0)])
        hid, t_g = cmpr["cv"]
        s, wt, wtok = rg.get(128, 128, lambda I: ktiles(np.asarray(I["a_cv_w2"])[0]))
        w2 = wt.rearrange("p (k n) -> p k n", k=2)
        i, ps, fr = bk.get()
        for g in range(4):
            for m in range(2):
                t = mm(ps[0:15, g * 64:(g + 1) * 64], hid[:, m, g * 15:(g + 1) * 15], w2[:, m, :], m == 0, m == 1,
                       fr, wtok, t_g, inc=(m == 1 and g == 3))
        rg.put(s, t)
        t_vc = cp(V, vc, ps[0:15, 0:256], t)
        bk.put(i, t_vc)

        w.lin(in_hx, t_hx, keep_squares(qT, Q3, t_qsq, ph))
        t_kc = kc_done()[0][0]
        qk_done = head_norms([dict(dst=qT, sq=Q3, toks=t_qsq, n=T, gain=lambda k: pc("a_q"), scale=0.125),
                              dict(dst=kT, sq=ksq, toks=t_ksq, n=T, gain=lambda k: pc(f"a_k{1 + k // 2}"), scale=1.0)])

        def values_of(vv, a):
            s, wt, wtok = rg.get(128, 2048, lambda I: ktiles(W(a, a + 256)(I)))
            t = tokmajor(wt.rearrange("p (k n) -> p k n", k=8), 256, wtok, H3, t_h,
                         lambda tb, ps, t: cp(A, vv[:, tb, :], ps, t, ph))
            rg.put(s, t)
            return A.last

        s, wt, wtok = rg.get(128, 384, lambda I: ktiles(head_cols(W(2560, 2608)(I))))
        t = tokmajor(wt.rearrange("p (k n) -> p k n", k=8), 48, wtok, H3, t_h,
                     lambda tb, ps, t: act(gts[:, tb, :], ps, ACT.Sigmoid, t, ph))
        rg.put(s, t)
        t_vS = values_of(vS, 1792)
        t_qn, t_kn = qk_done()
        t_vW = None
        t_all = now()

        pct = wk[0:15, pct_off:pct_off + 4096].rearrange("p (h t) -> p h t", t=T)
        cs = wk[:, a_off:a_off + 240]
        c3 = cs.rearrange("p (h n) -> p h n", n=15)
        cst1 = wk[:, a_off + 240:a_off + 272]
        for qb in range(2):
            cm = C(f"cmp{qb}").rearrange("p (h two n) -> p two h n", two=2, n=15)
            ch = cs.rearrange("p (h two n) -> p two h n", two=2, n=15)
            ready = now()
            for hp in range(2):
                i, ps, fr = bk.get()
                for n in range(8):
                    h = 2 * n + hp
                    t = mm(ps[:, n * 15:(n + 1) * 15], qT[64 * hp:64 * hp + 64, n, qb * 128:(qb + 1) * 128],
                           kcT[64 * hp:64 * hp + 64, 0, (HEADS[h] // 4) * 15:(HEADS[h] // 4 + 1) * 15], True, True, fr, t_all, inc=(n == 7))
                t = tt(V, ch[:, hp], ps[:, 0:120].rearrange("p (h n) -> p h n", n=15), cm[:, hp], ALU.add, t, ready)
                bk.put(i, t)
            if qb == 0:
                t_vW = values_of(vW, 2304)
            mx, sm = cst1[:, 0:16], cst1[:, 16:32]
            t = red(mx, c3, ALU.max, t)
            t = ts(V, mx, mx, -1e20, None, ALU.max, None, t)
            t = tt(V, c3, c3, mx.unsqueeze(2).to_broadcast([128, 16, 15]), ALU.subtract, t)
            t = act(cs, cs, ACT.Exp, t)
            t = red(sm, c3, ALU.add, t)
            t = ts(V, sm, sm, 1e-30, None, ALU.max, None, t)
            t = recip(sm, sm, t)
            gq = gts[:, qb, :].rearrange("p (h b) -> p b h", b=3)[:, 0, :]
            t = tt(V, sm, sm, gq, ALU.mult, t)
            t = tt(V, c3, c3, sm.unsqueeze(2).to_broadcast([128, 16, 15]), ALU.mult, t)
            for h4 in range(4):
                i, ps, fr = bk.get()
                for j in range(4):
                    tk = tp(ps[0:15, j * 128:(j + 1) * 128], c3[:, h4 * 4 + j, :], fr, t, inc=(j == 3))
                tl = cp(V, pct[:, h4 * 4:h4 * 4 + 4, qb * 128:(qb + 1) * 128],
                        ps[0:15, 0:512].rearrange("p (h t) -> p h t", t=128), tk, t_all)
                bk.put(i, tl)
        t_pc = now()
        units = []
        for h in range(16):
            g, r = HEADS[h] // 4, slice(64 * (h % 2), 64 * (h % 2) + 64)
            for b, (vv, t_vv) in enumerate(((vS, t_vS), (vW, t_vW))):
                units.append(dict(
                    h=h, q=qT[r, h // 2, :], k=kT[r, 2 * b + g // 2, :], bias=bias[h], btok=t_bias,
                    tok=(t_pc, t_qn[h // 2], t_kn[2 * b + g // 2], t_vv), sink=None,
                    v=lambda kb, vv=vv, g=g: vv[:, kb, g * 64:(g + 1) * 64],
                    gate=lambda qb, h=h, b=b: gts[:, qb, h * 3 + 1 + b:h * 3 + 2 + b],
                    first=(b == 0), last=(b == 1),
                    extra=[(vc[:, g * 64:(g + 1) * 64], pct[:, h, :], t_pc)]))
        t_o = attention(units, a_off, to_hx(t_pc))
        w = Products(range(8), now(), (D, D, lambda I, n0, n1: head_rows_of(np.asarray(I["a_w_out"])[0])[:, n0:n1]), ahead=4)
        state["x"] = w.lin(in_hx, t_o, residual)

    def grouped_weights(slots, ph, w_kv, w_q):
        return Products(slots, ph, (256, D, lambda I, n0, n1: w_kv(I)[:, n0:n1]),
                        (D, D, lambda I, n0, n1: head_cols(w_q(I))[:, n0:n1]), (None, D, lambda I: w_kv(I)[:, 256:512]))

    def grouped_attention(w, x_kv, t_kv, x_q, t_q, a_off, w_o, slots, early, gains, bias, t_bias, sinks, ph, evac):
        qT, kT, vv = v3(wk, 0, 8, T), v3(wk, 2048, 2, T), v3(wk, 2560, 2, T)
        ksq = vv
        t_ksq, t_qsq = [], []
        w.lin(x_kv, t_kv, keep_squares(kT, ksq, t_ksq, ph))
        w.lin(x_q, t_q, keep_squares(qT, Q3, t_qsq, ph))
        qk_done = head_norms([dict(dst=qT, sq=Q3, toks=t_qsq, n=T, gain=lambda k: pc(gains[0]), scale=0.125),
                              dict(dst=kT, sq=ksq, toks=t_ksq, n=T, gain=lambda k: pc(gains[1]), scale=1.0)])
        t_v = w.tokmajor(x_kv, t_kv, lambda tb, ps, t: cp(A, vv[:, tb, :], ps, t, ph))[-1]
        t_qn, t_kn = qk_done()
        units = []
        for h in range(16):
            g, r = HEADS[h] // 4, slice(64 * (h % 2), 64 * (h % 2) + 64)
            units.append(dict(h=h, q=qT[r, h // 2, :], k=kT[r, g // 2, :], bias=bias(h), btok=t_bias,
                              tok=(t_qn[h // 2], t_kn[g // 2], t_v), sink=sinks(h) if sinks else None, gate=None,
                              first=True, last=True, extra=[], v=lambda kb, g=g: vv[:, kb, g * 64:(g + 1) * 64]))
        w = Products(slots, now(), (D, D, lambda I, n0, n1: head_rows_of(w_o(I))[:, n0:n1]), ahead=early)
        t_o = attention(units, a_off, to_hx(now()))
        w.ph = now()
        state["x"] = w.lin(in_hx, t_o, evac)

    def moba():
        ph = now()
        w = grouped_weights((6, 7), ph, lambda I: np.asarray(I["w_kv_shared"]), lambda I: np.asarray(I["b_w_q"])[0])
        t = dnorm()
        t_n, t_kv = norm_to(Hh, Hl, lambda k: pc("kv_norm", k), t, ph)
        _, t_q = norm_to(Zh, Zl, lambda k: pc("ln_mix1", k), t_kv[-1], ph)
        bias, t_bias = alibi([3072, 3456] + [8192 + h * 384 for h in range(14)], ph)
        grouped_attention(w, in_hx, t_kv, in_hz, t_q, 8192 + 14 * 384, lambda I: np.asarray(I["b_w_out"])[0],
                          (7, 6, 5, 4, 3, 2), 1, ("b_q", "k_shared"), lambda h: bias[h], t_bias, None, ph, residual)

    def moe(l):
        def unit(I, u):
            a = ktiles(np.asarray(I["moe_w_gate"])[l, u])
            b = ktiles(np.asarray(I["moe_w_up"])[l, u])
            return np.concatenate([a, b, np.asarray(I["moe_w_down"])[l, u]], 1)

        ph = now()
        src = Units(unit)
        t_sq, t_z = [], []

        def scaled():
            t_sq.extend(squares(ph))
            for k in range(KD):
                g = pc(f"ln_ffn{l}", k)
                t0 = ts(V, H3[:, k, :], X3[:, k, :], g, None, ALU.mult, None, state["x"][k], ph)
                t1 = act(Hh[:, k, :], X3[:, k, :], ACT.Copy, state["x"][k], ph, scale=g)
                t_z.append(tt(V, Hl[:, k, :], H3[:, k, :], Hh[:, k, :], ALU.subtract, t0, t1))

        src.fetch(scaled)
        o = 0

        def take(n):
            nonlocal o
            o += n
            return sq[:, o - n:o]

        lg = take(72).rearrange("p (b n) -> p b n", b=2)
        lgT, cwT = sq[0:36, 1536:1792], sq[0:32, 1792:2048]
        wr = pc(f"moe_w{l}", 0, 288).rearrange("p (k n) -> p k n", k=8)
        st = {}

        def norm_and_logits():
            ps, t = late_norm(0, t_sq)
            for k in range(8):
                tr = mm(pb[1][0:36, 0:T], wr[:, k, :], H3[:, k, :], k == 0, k == 7, bk.free[1], t_z[k], loaded, inc=(k == 7))
            src.fetch()
            t0, t_r = rsqrt(rsb[:, :], ps[:, 0:T], 128, T, 1.0 / D, 1e-6, t)
            bk.put(0, t0)
            t = tt(V, lgT, pb[1][0:36, 0:T], rsb[0:36, :], ALU.mult, tr, t_r)
            bk.put(1, t)
            st["lg"] = ts(V, lgT, lgT, pc(f"moe_b{l}", 0, 1, 36), None, ALU.add, None, t)

        def logits_by_token():
            for b in range(2):
                t = tp(pb[2][:, b * 36:(b + 1) * 36], lgT[:, b * 128:(b + 1) * 128], bk.free[2], st["lg"], inc=(b == 1))
            t = cp(V, lg, pb[2][:, 0:72].rearrange("p (b n) -> p b n", b=2), t)
            bk.put(2, t)
            src.fetch()
            choose(t)

        def first_max(src, n, t):
            mx, eq, cum, oh = take(2), take(2 * n), take(2 * n), take(2 * n)
            eq, cum, oh = (a.rearrange("p (b n) -> p b n", b=2) for a in (eq, cum, oh))
            t = red(mx, src, ALU.max, t)
            t = tt(V, eq, src, mx.unsqueeze(2).to_broadcast([128, 2, n]), ALU.is_equal, t)
            for b in range(2):
                tb_ = V(lambda e, b=b: e.tensor_tensor_scan(cum[:, b, :], ones[:, 0:n], eq[:, b, :], 0.0, ALU.mult, ALU.add), t)
            t = stt(oh, cum, 1.0, eq, ALU.is_equal, ALU.mult, tb_)
            return mx, oh, t

        def choose(t):
            gl = lg[:, :, 0:4]
            gm, goh, t = first_max(gl, 4, t)
            ge = take(8).rearrange("p (b n) -> p b n", b=2)
            gw = take(2)
            t = tt(V, ge, gl, gm.unsqueeze(2).to_broadcast([128, 2, 4]), ALU.subtract, t)
            t = act(ge, ge, ACT.Exp, t)
            t = red(gw, ge, ALU.add, t)
            t = recip(gw, gw, t)
            pr = take(64).rearrange("p (b e g) -> p b e g", b=2, g=4)
            el = take(16).rearrange("p (b n) -> p b n", b=2)
            for b in range(2):
                t = tt(V, pr[:, b], lg[:, b, 4:36].rearrange("p (g e) -> p e g", g=4),
                       goh[:, b, :].unsqueeze(1).to_broadcast([128, 8, 4]), ALU.mult, t)
            t = red(el, pr, ALU.add, t)
            m1, oh1, t = first_max(el, 8, t)
            el2 = take(16).rearrange("p (b n) -> p b n", b=2)
            t = stt(el2, oh1, -3e38, el, ALU.mult, ALU.add, t)
            m2, oh2, t = first_max(el2, 8, t)
            e2, den = take(2), take(2)
            t = tt(V, e2, m2, m1, ALU.subtract, t)
            t = act(e2, e2, ACT.Exp, t)
            t = ts(V, den, e2, 1.0, None, ALU.add, None, t)
            t = recip(den, den, t)
            t = tt(V, den, den, gw, ALU.mult, t)
            wgt = take(16).rearrange("p (b n) -> p b n", b=2)
            cw = take(64).rearrange("p (b g e) -> p b g e", b=2, g=4)
            for b in range(2):
                t = stt(wgt[:, b, :], oh2[:, b, :], e2[:, b:b + 1], oh1[:, b, :], ALU.mult, ALU.add, t)
                t = ts(V, wgt[:, b, :], wgt[:, b, :], den[:, b:b + 1], None, ALU.mult, None, t)
                t = tt(V, cw[:, b], goh[:, b, :].unsqueeze(2).to_broadcast([128, 4, 8]),
                       wgt[:, b, :].unsqueeze(1).to_broadcast([128, 4, 8]), ALU.mult, t)
            st["cw"] = cw.rearrange("p b g e -> p b (g e)"), t

        def weights_by_expert():
            cw, t = st["cw"]
            for b in range(2):
                t1 = tp(pb[3][0:32, b * 128:(b + 1) * 128], cw[:, b, :], bk.free[3], t, inc=(b == 1))
            t = tt(V, cwT, pb[3][0:32, 0:T], rsb[0:32, :], ALU.mult, t1)
            bk.put(3, t)
            return t

        state["x"] = glu(32, src, t_z, residual, (norm_and_logits, logits_by_token, weights_by_expert), cwT)

    def ple(l):
        ph = now()
        pT = pc(f"p{l}", 0, 512)
        ph_, pl_ = ex[:, 0:512], ex[:, 512:1024]
        w = Products(range(8), ph, (D, D, lambda I, n0, n1: np.asarray(I["ple_w_gate"])[l][:, n0:n1]),
                     (D, 256, lambda I, n0, n1: np.asarray(I["ple_w_proj"])[l][:, n0:n1]), ahead=4)
        t = dnorm()
        _, t_h = norm_to(Hh, Hl, lambda k: pc(f"ln_ple{l}", k), t, ph)
        t_p = act(ph_, pT, ACT.Copy, loaded, ph)
        t_p = tt(G, pl_, pT, ph_, ALU.subtract, t_p)
        gt = Q3
        t_g = w.lin(in_hx, t_h, lambda m, ps, t: act(gt[:, m, :], ps, ACT.Sigmoid, t))
        t_x = []

        def add(m, ps, t):
            t1 = tt(V, gt[:, m, :], gt[:, m, :], ps, ALU.mult, t, t_g[m])
            t_x.append(tt(V, X3[:, m, :], X3[:, m, :], gt[:, m, :], ALU.add, t1))
            return t1

        w.lin(lambda k: (ph_[:, k * T:(k + 1) * T], pl_[:, k * T:(k + 1) * T]), [t_p] * 2, add)
        state["x"] = t_x

    def gains(l, s, w=()):
        while ada["at"] < 24 * (l + 1):
            ada_next(now())
            ada_sum()()
        tg = ts(V, gs[:, 0:8], mods[:, l * 72 + s * 24 + 8:l * 72 + s * 24 + 16], 1.0, None, ALU.add, None, ada["tok"][l], w)
        return tt(V, gs[:, 0:8], gs[:, 0:8], pc(f"ng{l}{s}", 0, 8), ALU.mult, tg)

    def adaln(l, s, then=None):
        tg = gains(l, s)
        ph = now()
        t = dnorm(then or (lambda: None))
        t_n = []
        for k in range(9 if then else 8):
            if k < 8:
                t1 = stt(H3[:, k, :], X3[:, k, :], gs[:, k:k + 1], rsb[:, :], ALU.mult, ALU.mult, t, tg, ph)
                t_n.append(act((Hh if then else H3)[:, k, :], H3[:, k, :], ACT.Identity, t1, ph, bias=mod(l, s, 0, k)))
            if then and k > 0:
                n = k - 1
                t_n[n] = stt(Hl[:, n, :], H3[:, n, :], mod(l, s, 0, n), Hh[:, n, :], ALU.add, ALU.subtract, t_n[n], ph)
        return t_n

    def ffn(l, s, w):
        def unit(I, u):
            wi, wo = np.asarray(I["ffn_w_in_2"])[l, w], np.asarray(I["ffn_w_out_2"])[l, w]
            return np.concatenate([ktiles(wi[:, u * 128:(u + 1) * 128]),
                                   ktiles(wi[:, 2816 + u * 128:2816 + (u + 1) * 128]), wo[u * 128:(u + 1) * 128]], 1)

        src = Units(unit)
        t_h = adaln(l, s, lambda: src.fetch(lambda: None))
        th = ts(V, gs[:, 8:16], mods[:, l * 72 + s * 24 + 16:l * 72 + s * 24 + 24], 0.5, None, ALU.mult, None, V.last)
        state["x"] = glu(22, src, t_h, lambda m, ps, t: stt(
            X3[:, m, :], ps, gs[:, 8 + m:9 + m], X3[:, m, :], ALU.mult, ALU.add, t, th))

    def swa(l):
        W = lambda a, b: (lambda I: np.asarray(I["sw_w_qkv_2"])[0][:, a:b])
        w = grouped_weights(range(3, 8), now(), W(1024, 1536), W(0, 1024))
        t_h = adaln(l, 1, lambda: None)
        grouped_attention(w, in_hx, t_h, in_hx, t_h, 3072, lambda I: np.asarray(I["sw_w_o_2"])[0], range(3, 8), 3,
                          ("sw_q", "sw_k"), lambda h: C("swa"), loaded, lambda h: pc("sinks", h), now(),
                          gated_residual(l, 1))

    def mamba(l):
        ph = now()
        o = 0

        def take(n):
            nonlocal o
            o += n
            return o - n

        xsT = v3(wk, take(4096), 16, T)
        BT, CT = v3(wk, take(2048), 8, T), v3(wk, take(2048), 8, T)
        zT = v3(wk, 15296, 16, T)
        Xt = [hT, sq]
        xp = [wk[:, take(260):o] for _ in range(3)]
        acc = [wk[:, take(256):o] for _ in range(3)]
        sm = [wk[0:32, take(256):o] for _ in range(5)]
        cbm = [wk[:, 19392 + i * 384:19392 + (i + 1) * 384] for i in range(2)]
        Gb = [wk[:, 19392 + i * 384:19392 + (i + 1) * 384] for i in range(2, 6)]
        dtT, acT = v3(wk, take(64), 2, 32), v3(wk, take(64), 2, 32)
        eA = wk[0:32, take(1):o]
        W = lambda a, b: (lambda I: np.asarray(I["mb_w_in_2"])[0][:, a:b])

        s, wt, wtok = rg.get(128, 256, lambda I: ktiles(W(6144, 6176)(I)))
        t_w = act(ex[:, 0:256], wt, ACT.Copy, wtok, ph)
        t_w = tt(V, ex[:, 256:512], wt, ex[:, 0:256], ALU.subtract, t_w)
        rg.put(s, t_w)
        w = Products([4, 5, 6, 7] * 8 + [4, 5] * 8, ph, (4096, D, lambda I, n0, n1: W(2048 + n0, 2048 + n1)(I)),
                     (2048, D, lambda I, n0, n1: W(n0, n1)(I)), ahead=3, share=True)
        t_h = adaln(l, 1, lambda: None)
        i, ps, fr = bk.get()
        for k in range(8):
            t = mm3(ps[0:32, 0:T], [ex[:, n * 256 + k * 32:n * 256 + (k + 1) * 32] for n in range(2)], in_hx(k),
                    k == 0, k == 7, fr, t_w, t_h[k], inc=(k == 7))
        v, e, r, s2, p = sm
        t = ts(V, v, ps[0:32, 0:T], pc("dt_bias", 0, 1, 32), None, ALU.add, None, t, ph)
        bk.put(i, t)
        def softplus(t):
            t = act(e, v, ACT.Abs, t)
            yield t
            t = act(e, e, ACT.Exp, t, scale=-1.0)
            yield t
            t = ts(V, r, e, 2.0, None, ALU.add, None, t)
            yield t
            t = recip(r, r, t)
            yield t
            t = tt(V, e, e, r, ALU.mult, t)
            yield t
            t = tt(V, s2, e, e, ALU.mult, t)
            yield t
            t = ts(V, p, s2, 1.0 / 19, None, ALU.mult, None, t)
            yield t
            for n in (17, 15, 13, 11, 9, 7, 5, 3):
                t = stt(p, p, 1.0 / n, s2, ALU.add, ALU.mult, t)
                yield t
            t = stt(p, p, 1.0, e, ALU.add, ALU.mult, t)
            yield t
            t = ts(V, p, p, 2.0, None, ALU.mult, None, t)
            yield t
            t = stt(v, v, 0.0, p, ALU.max, ALU.add, t)
            yield t
            ta = act(eA, pc("A_log", 0, 1, 32), ACT.Exp, ph)
            yield t
            t = ts(V, e, v, eA, -1.0, ALU.mult, ALU.mult, t, ta)
            yield t
            t = V(lambda q: q.tensor_tensor_scan(r, ones[0:32, 0:T], e, 0.0, ALU.mult, ALU.add), t)
            yield t

        steps = softplus(t)
        dt, acum = v, r
        for j in range(3):
            V(lambda q, j=j: q.memset(xp[j][:, 0:3], 0.0), ph)
        t_xp = V.last
        cfree = [ph, ph, ph]
        afree = [ph, ph, ph]
        def silu(c):
            dst = xsT[:, c, :] if c < 16 else (BT if c < 24 else CT)[:, c % 8, :]
            afree[c % 3] = act(dst, acc[c % 3], ACT.Silu, cfree[c % 3], ph)

        def conv(c, ps, t):
            j = c % 3
            x, a = xp[j], acc[j]
            t1 = act(x[:, 3:259], ps, ACT.Copy, t, cfree[j], t_xp)
            t2 = act(a, x[:, 0:T], ACT.Identity, t1, afree[j], scale=pc("conv0", c), bias=pc("conv_b", c))
            if c:
                silu(c - 1)
            next(steps, None)
            for k in (1, 2, 3):
                t2 = stt(a, x[:, k:k + T], pc(f"conv{k}", c), a, ALU.mult, ALU.add, t2)
            cfree[j] = t2
            return t1

        w.lin(in_hx, t_h, conv)
        silu(31)
        t_c = A.last
        assert next(steps, None) is None
        t_sp = now()

        for src, dst in ((dt, dtT), (acum, acT)):
            i, ps, fr = bk.get()
            for b in range(2):
                tk = tp(ps[:, b * 32:(b + 1) * 32], src[:, b * 128:(b + 1) * 128], fr, t_sp, inc=(b == 1))
            tl = cp(V, dst, ps[:, 0:64].rearrange("p (b n) -> p b n", b=2), tk)
            bk.put(i, tl)
        t_dt = V.last

        def gate(m, ps, t):
            tz = act(zT[:, m, :], ps, ACT.Silu, t, ph)
            i, ps, fr = bk.get()
            for b in range(2):
                tk = tp(ps[:, b * 128:(b + 1) * 128], xsT[:, m, b * 128:(b + 1) * 128], fr, t_c, inc=(b == 1))
            for b in range(2):
                tl = tt(V, Xt[b][:, m * 128:(m + 1) * 128].rearrange("p (h d) -> p h d", h=2),
                        ps[:, b * 128:(b + 1) * 128].rearrange("p (h d) -> p h d", h=2),
                        dtT[:, b, 2 * m:2 * m + 2].unsqueeze(2).to_broadcast([128, 2, 64]), ALU.mult, tk, t_dt, ph)
            bk.put(i, tl)
            return tz

        t_z = w.lin(in_hx, t_h, gate)[-1]
        t_X = V.last
        w = Products((4, 5, 6, 7), now(), (D, 2048, lambda I, n0, n1: np.asarray(I["mb_w_out_2"])[0][:, n0:n1]), ahead=2)

        bk.use(range(2, 7))
        gfree, mfree = [t_X] * 4, [t_X] * 2
        decays, heads, t_y, t_sq = [], [], [], []

        def group(g):
            i, ps, fr = bk.get()
            mm(ps[:, 0:256], BT[:, g, 0:128], CT[:, g, :], True, True, fr, t_c)
            t = mm(ps[:, 256:384], BT[:, g, 128:256], CT[:, g, 128:256], True, True, inc=True)
            t = tt(V, cbm[g % 2], ps[:, 0:384], C("S384"), ALU.mult, t, mfree[g % 2])
            bk.put(i, t)

        def weights(h):
            i, ps, fr = bk.get()
            sel = cst[0:32, ccol["ident"][0] + h:ccol["ident"][0] + h + 1].to_broadcast([32, 128])
            t = mm(ps[:, 0:T], sel, acum, True, True, fr, t_dt, inc=True)
            b = Gb[h % 4]
            ts(V, b[:, 0:256], ps[:, 0:256], acT[:, 0, h:h + 1], 0.0, ALU.subtract, ALU.min, t, gfree[h % 4])
            t = ts(V, b[:, 256:384], ps[:, 128:256], acT[:, 1, h:h + 1], 0.0, ALU.subtract, ALU.min, t)
            bk.put(i, t)
            decays.append(act(b, b, ACT.Exp, t))

        def masked(h):
            g, b = h // 4, Gb[h % 4]
            mfree[g % 2] = tt(V, b, b, cbm[g % 2], ALU.mult, decays[h])
            heads.append(mfree[g % 2])

        def output(h):
            m, hp = h // 2, h % 2
            ob = pb[m % 2]
            b = Gb[h % 4]
            mm(ob[64 * hp:64 * hp + 64, 0:T], Xt[0][:, h * 64:(h + 1) * 64], b[:, 0:256], True, False,
               bk.free[m % 2], heads[h], t_X, skip=True)
            t = mm(ob[64 * hp:64 * hp + 64, 128:256], Xt[1][:, h * 64:(h + 1) * 64], b[:, 256:384], False, True,
                   inc=True, skip=True)
            gfree[h % 4] = t
            if hp == 1:
                t = stt(xsT[:, m, :], xsT[:, m, :], pc("mb_D", m), ob[:, 0:T], ALU.mult, ALU.add, t)
                bk.put(m % 2, t)
                t_y.append(tt(G, xsT[:, m, :], xsT[:, m, :], zT[:, m, :], ALU.mult, t, t_z))
                t_sq.append(act(zT[:, m, :], xsT[:, m, :], ACT.Square, t_y[m]))

        def sums(m):
            return mm(pb[7][0:8, 0:T], selg[:, m // 2 * 8:(m // 2 + 1) * 8], zT[:, m, :], m == 0, m == 15,
                      bk.free[7], t_sq[m], t_selg, inc=(m == 15))

        for h in range(34):
            if h < 32:
                if h % 4 == 0:
                    group(h // 4)
                weights(h)
            if 1 <= h < 33:
                masked(h - 1)
            if h >= 2:
                output(h - 2)
            if h >= 5 and h % 2:
                t = sums((h - 5) // 2)
        t = sums(15)
        bk.use(range(8))
        w.ph = now()

        t0 = ts(V, nv[0:8, :], pb[7][0:8, 0:T], 1.0 / 256, 1e-6, ALU.mult, ALU.add, t, V.last)
        bk.put(7, t0)
        t = rsqrt_of(hr[0:8, :], nv[0:8, :], nm[0:8, :], nt[0:8, :])
        yh, yl = (lambda m: (Hh, Zh)[m // 8][:, m % 8, :]), (lambda m: (Hl, Zl)[m // 8][:, m % 8, :])
        t_hi, t_n = [], []

        def low(m):
            t_n.append(tt((V, G)[m % 2], yl(m), xsT[:, m, :], yh(m), ALU.subtract, t_hi[m]))

        for g in range(8):
            i, ps, fr = bk.get()
            sel = cst[0:8, ccol["ident"][0] + g:ccol["ident"][0] + g + 1].to_broadcast([8, 128])
            tb = mm(ps[:, 0:T], sel, hr[0:8, :], True, True, fr, t, inc=True)
            for m in (2 * g, 2 * g + 1):
                tl = stt(xsT[:, m, :], xsT[:, m, :], pc("mb_g", m), ps[:, 0:T], ALU.mult, ALU.mult, tb, t_y[m], t_sq[m])
                t_hi.append(act(yh(m), xsT[:, m, :], ACT.Copy, tl, w.ph))
                if m:
                    low(m - 1)
            bk.put(i, tl)
        low(15)
        state["x"] = w.lin(lambda m: (yh(m), yl(m)), t_n, gated_residual(l, 1))

    V(lambda e: e.memset(selg[:, :], 0.0))
    t_selg = V.last
    for k in range(8):
        V(lambda e, k=k: e.memset(selg[:, k * 9:k * 9 + 1], 1.0), t_selg)
    t_selg = V.last

    def rwkv(l, j):
        ph = now()
        o = 0

        def take(n):
            nonlocal o
            o += n
            return o - n

        offs = {n: take(2048) for n in ("r", "k", "v", "kk", "a", "lw", "c")}
        fl = {n: wk[:, a:a + 2048] for n, a in offs.items() if n != "lo"}
        r3, k3, v3_, kk3, a3, lw3, c3 = (v3(wk, offs[n], 8, T) for n in ("r", "k", "v", "kk", "a", "lw", "c"))
        offs["lo"] = take(512)
        lo = wk[:, offs["lo"]:o].rearrange("p (k n) -> p k n", n=T)
        base = o
        dx3 = c3
        KAPPA = float(np.exp(-0.5))
        Ah, Al = v3(ha, 0, 8, T), v3(ha, 2048, 8, T)
        ksq, xg = v3(wk, 19392, 8, T), v3(wk, 21440, 8, T)
        kn = bsum[:, :]
        I_ = lambda name, n=j: (lambda I: np.asarray(I[name])[n])
        w = Products([6, 7, 0, 1] * 2 + [6, 7, 1, 6, 7, 1, 6, 7] + [6, 7] * 4, ph,
                     *[(D, D, lambda I, n0, n1, n=n: np.asarray(I["rw_w_rkv_2"])[j, n][:, n0:n1]) for n in range(3)],
                     ahead=3, share=True)
        t_h = adaln(l, 1)
        t_ad = now()

        t_dx = []
        for k in range(8):
            t0 = ts(V, dx3[:, k, 0:1], H3[:, k, 0:1], -1.0, None, ALU.mult, None, t_h[k], ph)
            t_dx.append((t0, tt(G, dx3[:, k, 1:T], H3[:, k, 0:T - 1], H3[:, k, 1:T], ALU.subtract, t_h[k], ph)))

        def mixed(m, k, dst, *w):
            return stt(dst[:, k, :], dx3[:, k, :], pc(f"mu{j}{m}", k), H3[:, k, :], ALU.mult, ALU.add, t_dx[k], w)

        def split_mix(m, hi, lo, toks, *w):
            for k in range(9):
                if k < 8:
                    toks.append(act(hi[:, k, :], Q3[:, k, :], ACT.Copy, mixed(m, k, Q3, t_ad), w))
                if k:
                    toks[k - 1] = tt(V, lo[:, k - 1, :], Q3[:, k - 1, :], hi[:, k - 1, :], ALU.subtract, toks[k - 1])
                yield

        t_r, t_k, t_v_ = [], [], []
        for _ in split_mix(0, Hh, Hl, t_r, ph):
            pass
        mix_k = split_mix(2, Ah, Al, t_k, ph)

        def to_r(m, ps, t):
            t1 = cp(A, r3[:, m, :], ps, t, ph)
            next(mix_k)
            return t1

        w.lin(in_hx, t_r, to_r)
        next(mix_k)
        mix_v = split_mix(3, Hh, Hl, t_v_, PE.last)

        def to_k(m, ps, t):
            t1 = cp(A, k3[:, m, :], ps, t, ph)
            next(mix_v)
            return t1

        t = w.lin(lambda k: (Ah[:, k, :], Al[:, k, :]), t_k, to_k)
        next(mix_v)
        t_w, t_a, t_kk = [], [], []

        def to_v(m, ps, t1):
            t2 = cp(A, v3_[:, m, :], ps, t1, ph)
            t_kk.append(ts(V, kk3[:, m, :], k3[:, m, :], pc(f"k_k{j}", m), None, ALU.mult, None, t[m], t1))
            t_w.append(mixed(1, m, a3, t1))
            t_a.append(mixed(4, m, lw3, t1))
            return t2

        t_v = w.lin(in_hx, t_v_, to_v)
        t_lin = PE.last
        t_sq = [act(ksq[:, k, :], kk3[:, k, :], ACT.Square, t_kk[k], t_lin) for k in range(8)]
        t_g = [mixed(5, k, xg, t_lin) for k in range(8)]

        def first(I):
            return np.concatenate([ktiles(I_(f"rw_{n}1_2", i)(I)) for n, i in ranks], 1)

        ranks = [("w", j), ("a", j), ("g", j)] + ([("v", 0)] if j else [])
        s1, w1, tok1 = rg.get(128, 8 * (64 + 64 + 160 + (32 if j else 0)), first)

        def second(I):
            out = [I_("rw_w2_2")(I), I_("rw_a2_2")(I)]
            if j:
                v2 = I_("rw_v2_2", 0)(I)
                out.append(np.concatenate([v2, np.zeros_like(v2)], 0))
            return np.concatenate(out, 1)

        s2, w2, tok2 = rg.get(64, 3072 if j else 2048, second)

        def third(I):
            g2 = I_("rw_g2_2")(I)
            return np.concatenate([g2[0:128], np.concatenate([g2[128:160], np.zeros_like(g2[0:96])], 0)], 1)

        s3, w3, tok3 = rg.get(128, 2048, third)

        def lora_in(rank, at, src, tok, func, outs, *w):
            w1_ = w1[:, 8 * at:8 * (at + rank)].rearrange("p (k n) -> p k n", k=8)
            parts = []
            for n, a in enumerate(range(0, rank, 128)):
                z = min(128, rank - a)
                i, ps, fr = bk.get()
                for k in range(8):
                    t = mm(ps[0:z, 0:T], w1_[:, k, a:a + z], src[:, k, :], k == 0, k == 7, fr, tok1, tok[k], inc=(k == 7))
                te = act(outs[n][0:z, :], ps[0:z, 0:T], func, t, w)
                bk.put(i, te)
                parts.append((z, outs[n][0:z, :], te))
            return parts

        def lora_out(parts, ws, wtok, evac):
            toks = []
            for m in range(8):
                i, ps, fr = bk.get()
                for n, (z, h, te) in enumerate(parts):
                    t = mm(ps[:, 0:T], ws[n][0:z, m * 128:(m + 1) * 128], h, n == 0, n == len(parts) - 1,
                           fr, wtok, te, inc=(n == len(parts) - 1))
                toks.append(evac(m, ps[:, 0:T], t))
                bk.put(i, toks[-1])
            return toks

        i, ps, t = head_rows(ksq, 8, T, t_sq)
        t0 = ts(V, nv[0:16, :], ps, 1e-24, None, ALU.max, None, t, V.last)
        bk.put(i, t0)
        t_hr = rsqrt_of(kn, nv[0:16, :], nm[0:16, :], nt[0:16, :])
        lw_ = lora_in(64, 0, a3, t_w, ACT.Tanh, [wk[:, base:base + T]], ph)
        la = lora_in(64, 64, lw3, t_a, ACT.Copy, [rsb], t_lin)
        t_in = PE.last
        if j:
            lv = lora_in(32, 288, Q3, t_v_, ACT.Copy, [hr], ph)
        lg_ = lora_in(160, 128, xg, t_g, ACT.Sigmoid, [lo[:, 0, :], lo[:, 1, :]], ph)
        rg.put(s1, PE.last)
        t_lw = lora_out(lw_, [w2], tok2, lambda m, ps, t: act(lw3[:, m, :], ps, ACT.Sigmoid, t, t_in, bias=pc(f"w0{j}", m)))
        t_c = []
        for k in range(8):
            t_c.append(V(lambda q, k=k: q.tensor_tensor_scan(c3[:, k, :], C("reset"), lw3[:, k, :], 0.0, ALU.mult, ALU.add),
                         t_lw[k], V.last))
        t_a = lora_out(la, [w2[:, 1024:2048]], tok2,
                       lambda m, ps, t: act(a3[:, m, :], ps, ACT.Sigmoid, t, t_in, bias=pc(f"a0{j}", m)))
        if j == 0:
            t_v = cp(A, vfirst[:, :], fl["v"], t_v)
        else:
            sig, diff = v3(wk, 15296, 8, T), v3(wk, 17344, 8, T)
            t_vl, t_v = t_v, []

            def mix_first(m, ps, t):
                t1 = act(sig[:, m, :], ps, ACT.Sigmoid, t, t_lin, bias=pc("v01", m))
                t2 = tt(V, diff[:, m, :], vfirst[:, m * T:(m + 1) * T], v3_[:, m, :], ALU.subtract, t_vl, t_lin)
                t2 = tt(V, diff[:, m, :], diff[:, m, :], sig[:, m, :], ALU.mult, t1, t2)
                t_v.append(tt(G, v3_[:, m, :], v3_[:, m, :], diff[:, m, :], ALU.add, t2))
                return t1

            lora_out(lv, [w2[:, 2048:3072]], tok2, mix_first)
        rg.put(s2, PE.last)
        t_mx = PE.last

        spare = base + 11 * 512 + 5 * 256 + 192
        ex3 = [v3(wk, spare + i * 768, 3, T) for i in range(2)]
        ex_free = [now(), now()]
        ready, bonus = [], []

        def prepare():
            k = len(ready)
            e1, e2, e3 = (ex3[k % 2][:, n, :] for n in range(3))
            ef = ex_free[k % 2]
            t3 = tt(G, lw3[:, k, :], c3[:, k, :], lw3[:, k, :], ALU.subtract, t_c[k])
            te2 = act(e2, c3[:, k, :], ACT.Exp, t_c[k], ef, scale=-KAPPA)
            te3 = act(e3, c3[:, k, :], ACT.Exp, scale=KAPPA)
            te1 = act(e1, lw3[:, k, :], ACT.Exp, t3, scale=-KAPPA)
            i, ps, tb = head_bcast(kn, k, T, t_hr)
            t_kk = tt(V, kk3[:, k, :], kk3[:, k, :], ps, ALU.mult, tb)
            bk.put(i, t_kk)
            t1 = ts(V, Q3[:, k, :], a3[:, k, :], -1.0, pc(f"k_a{j}", k), ALU.add, ALU.mult, t_a[k], t_mx)
            t1 = stt(k3[:, k, :], Q3[:, k, :], 1.0, k3[:, k, :], ALU.add, ALU.mult, t1)
            t4 = tt(V, a3[:, k, :], a3[:, k, :], kk3[:, k, :], ALU.mult, t_kk)
            t2 = stt(Q3[:, k, :], r3[:, k, :], pc(f"r_k{j}", k), k3[:, k, :], ALU.mult, ALU.mult, t1)
            t7 = tt(G, a3[:, k, :], a3[:, k, :], e3, ALU.mult, te3, t4)
            t8 = tt(G, k3[:, k, :], k3[:, k, :], e3, ALU.mult, te3, t2)
            t6 = tt(V, r3[:, k, :], r3[:, k, :], e2, ALU.mult, te2, t2)
            cp(V, dl[:, 4 * k:4 * k + 4], e2.rearrange("p (n c) -> p n c", c=64)[:, :, 63], te2)
            t5 = stt(kk3[:, k, :], kk3[:, k, :], -1.0, e1, ALU.mult, ALU.mult, te1, t4)
            ready.append((t5, t6, t7, t8))
            ex_free[k % 2] = (t5, t8)
            bonus.append(t2)

        def sum_bonus(k):
            mm(pb[1][0:16, 0:T], half_select(k), Q3[:, k, :], k == 0, k == 7, bk.free[1], bonus[k], inc=(k == 7))

        bk.use([0, 2, 3, 4, 5, 6, 7])
        gate3 = H3

        def to_gate(m, ps, t):
            t1 = cp(A, gate3[:, m, :], ps, t, t_g)
            prepare()
            if m > 1:
                sum_bonus(m - 2)
            return t1

        t_gate = lora_out(lg_, [w3, w3[:, 1024:2048]], tok3, to_gate)
        rg.put(s3, PE.last)
        sum_bonus(6)
        sum_bonus(7)
        t_bs = cp(V, hr[0:16, :], pb[1][0:16, 0:T], PE.last)
        bk.put(1, t_bs)

        names = ["M16", "M16T", "Mo32", "Mo64", "ArbT", "ArkT", "AakT", "M2", "M2T", "TI", "TT"]
        y3 = r3
        uns = [(hp, hf) for hp in range(2) for hf in range(2)]
        mask = lambda n: C(n).unsqueeze(1).to_broadcast([128, 2, 128])
        idm = ident.unsqueeze(1).to_broadcast([128, 4, 128])

        def memory(n):
            if n == 0:
                at = [wk[:, base + i * 512:base + (i + 1) * 512] for i in range(11)]
                o = base + 11 * 512
                sm_ = [wk[:, o + i * 256:o + (i + 1) * 256] for i in range(5)]
                o += 5 * 256
            else:
                at = [fl[x][:, i * 512:(i + 1) * 512] for x in ("lw", "c") for i in range(4)]
                at += [sq[:, i * 512:(i + 1) * 512] for i in range(3)]
                sm_ = [wk[:, spare + i * 256:spare + (i + 1) * 256] for i in range(5)]
                o = spare + 5 * 256
            mat = {x: a.rearrange("p (u n) -> p u n", u=4) for x, a in zip(names, at)}
            mat["M4"], mat["M4T"] = mat["M16"], mat["M16T"]
            return mat, [a.rearrange("p (b n) -> p b n", b=2) for a in sm_], wk[:, o:o + 128], wk[:, o + 128:o + 192]

        def tile(m, n, mem, free):
            mat, (Bt, Kt, Vt, W0, Ub), Pb, Pd = mem
            t_in = ready[m]
            t_pb = V(lambda e: e.memset(Pb, 0.0), free)
            t_u0 = V(lambda e: e.memset(Ub, 0.0), free)

            def of(x):
                return lambda u: mat[x][:, u, :]

            def product(l_, r_, *w):
                i, ps, fr = bk.get()
                for u in range(4):
                    t = mm(ps[:, u * 128:(u + 1) * 128], l_(u), r_(u), True, True, fr, w, inc=(u == 3))
                return i, ps[:, :].rearrange("p (u n) -> p u n", u=4), t

            def fm(x3):
                return lambda u: x3[64 * uns[u][0]:64 * uns[u][0] + 64, m, uns[u][1] * 128:(uns[u][1] + 1) * 128]

            at_, bt_, kt_, rt_ = fm(kk3), fm(a3), fm(k3), fm(r3)

            def by_head(l_, r_, outs):
                for hp in range(2):
                    i, ps, fr = bk.get()
                    for hf in range(2):
                        u = 2 * hp + hf
                        t = mm(ps[:, hf * 128:(hf + 1) * 128], l_(u), r_(u), True, True, fr, t_in, inc=(hf == 1))
                    p3 = ps[:, 0:256].rearrange("p (u n) -> p u n", u=2)
                    for x, mk in outs:
                        t1 = tt(V, mat[x][:, 2 * hp:2 * hp + 2, :], p3, mask(mk), ALU.mult, t, free)
                    bk.put(i, t1)
                return t1

            def turned(x, *w):
                i, ps, fr = bk.get()
                for u in range(4):
                    t = tp(ps[:, u * 128:(u + 1) * 128], mat[x][:, u, :], fr, w, inc=(u == 3))
                return i, ps[:, :].rearrange("p (u n) -> p u n", u=4), t

            def turn(x, dst, *w):
                i, ps, t = turned(x, *w)
                t = cp(A, mat[dst], ps, t, free)
                bk.put(i, t)
                return t

            def power(l_, r_, dst, *w):
                i, ps, t = product(of(l_), of(r_), *w)
                t = cp(A, mat[dst], ps, t, free)
                bk.put(i, t)
                return t

            def grow(x, *w):
                i, ps, t = product(of(x), of("TT"), *w)
                t = tt(V, mat["TT"], mat["TT"], ps, ALU.add, t)
                bk.put(i, t)
                return t

            t_m = by_head(at_, bt_, (("M16", "L16"), ("Mo32", "Lo32"), ("Mo64", "Lo64")))
            yield
            i, ps, t = turned("M16", t_m)
            t1 = cp(A, mat["M16T"], ps, t, free)
            tg = tt(V, mat["TT"], ps, idm, ALU.add, t, t1, free)
            bk.put(i, t1, tg)
            yield
            for x3, dst in ((a3, Bt), (k3, Kt), (v3_, Vt)):
                i, ps, fr = bk.get()
                for b in range(2):
                    t = tp(ps[:, b * 128:(b + 1) * 128], x3[:, m, b * 128:(b + 1) * 128], fr, t_in, t_v, inc=(b == 1))
                t_tok = cp(A, dst, ps[:, 0:256].rearrange("p (b n) -> p b n", b=2), t, free)
                bk.put(i, t_tok)
            t2 = power("M16T", "M16", "M2", t_m, t1)
            yield
            by_head(kt_, at_, (("AakT", "U64"),))
            yield
            t2t = turn("M2", "M2T", t2)
            tg = grow("M2", t2, tg)
            yield
            t4 = power("M2T", "M2", "M4", t2t)
            by_head(bt_, rt_, (("ArbT", "Ui64"),))
            yield
            t4t = turn("M4", "M4T", t4)
            tg = grow("M4", t4, tg)
            yield
            t8 = power("M4T", "M4", "M2", t4t)
            t_A = by_head(kt_, rt_, (("ArkT", "Ui64"),))
            yield
            tg = grow("M2", t8, tg)
            yield
            for n_, x in enumerate(("Mo32", "Mo64")):
                t1 = turn("TT", "TI", tg)
                t2 = power(x, "TT", "M4", tg)
                yield
                if n_ == 0:
                    i, ps, fr = bk.get()
                    for u, (hp, hf) in enumerate(uns):
                        t = mm(ps[:, hf * 128 + hp * 64:hf * 128 + hp * 64 + 64], mat["AakT"][:, u, :],
                               Vt[:, hf, 64 * hp:64 * hp + 64], True, True, fr, t_A, t_tok, inc=(u == 3))
                    tw0 = cp(V, W0[:, :, :], ps[:, 0:256].rearrange("p (b n) -> p b n", b=2), t, free)
                    bk.put(i, tw0)
                    yield
                i, ps, t = product(of("TI"), of("M4"), t1, t2)
                tg = tt(V, mat["TT"], mat["TT"], ps, ALU.add, t)
                bk.put(i, tg)
                yield
            py, fry = pb[n], bk.free[n]
            for u, (hp, hf) in enumerate(uns):
                mm(py[64 * hp:64 * hp + 64, hf * 128:(hf + 1) * 128], Vt[:, hf, 64 * hp:64 * hp + 64], mat["ArkT"][:, u, :],
                   hf == 0, False, fry, t_A, t_tok, skip=True)
            t_P = t_Pd = None
            for c in range(4):
                hf, c2 = divmod(c, 2)
                rs_ = slice(64 * c2, 64 * c2 + 64)
                cs_ = slice(c * 64, (c + 1) * 64)
                if c:
                    i, ps, fr = bk.get()
                    t = mm(ps[rs_, 0:128], kk3[:, m, cs_], Pb[:, :], True, True, fr, t_P, inc=True)
                    tw = tt(V, W0[rs_, hf, :], ps[rs_, 0:128], W0[rs_, hf, :], ALU.add, t, tw0)
                    bk.put(i, tw)
                    mm(py[:, cs_], Pb[:, :], r3[:, m, cs_], False, False, fry, t_P, skip=True)
                    yield
                else:
                    tw = tw0
                i, ps, fr = bk.get()
                for hp in range(2):
                    t = mm(ps[rs_, hp * 64:(hp + 1) * 64], mat["TT"][:, hp * 2 + hf, rs_], W0[:, hf, hp * 64:(hp + 1) * 64],
                           True, True, fr, tw, tg, inc=(hp == 1))
                tu = cp(V, Ub[rs_, hf, :], ps[rs_, 0:128], t, free, t_u0)
                bk.put(i, tu)
                yield
                for hp in range(2):
                    hs = slice(64 * hp, 64 * hp + 64)
                    t_y = mm(py[hs, cs_], Ub[:, hf, hs], mat["ArbT"][:, hp * 2 + hf, rs_], False, c == 3, tu, t_A,
                             inc=(hp == 1), skip=True)
                if c < 3:
                    i, ps, fr = bk.get()
                    for hp in range(2):
                        hs = slice(64 * hp, 64 * hp + 64)
                        mm(ps[hs, 0:64], Bt[rs_, hf, hs], Ub[rs_, hf, hs], True, False, fr, tu, t_tok, skip=True)
                        t = mm(ps[hs, 0:64], Kt[rs_, hf, hs], Vt[rs_, hf, hs], False, True, inc=(hp == 1), skip=True)
                    for hp in range(2):
                        hs = slice(64 * hp, 64 * hp + 64)
                        d = dl[hs, m * 4 + c:m * 4 + c + 1]
                        if c == 0:
                            t_P = ts(V, Pb[hs, hs], ps[hs, 0:64], d, None, ALU.mult, None, t, free, t_pb)
                        else:
                            t_P = stt(Pb[hs, hs], ps[hs, 0:64], d, Pd[hs, :], ALU.mult, ALU.add, t, t_y, t_Pd)
                    bk.put(i, t_P)
                    if c < 2:
                        for hp in range(2):
                            hs = slice(64 * hp, 64 * hp + 64)
                            t_Pd = ts(V, Pd[hs, :], Pb[hs, hs], dl[hs, m * 4 + c + 1:m * 4 + c + 2], None, ALU.mult, None, t_P)
                    yield
            t1 = cp(V, y3[:, m, :], py[:, 0:T], t_y)
            bk.put(n, t1)
            frees[n] = t1
            yield
            i, ps, fr = bk.get()
            t = mm(ps[:, 0:T], C("blk64"), y3[:, m, :], True, True, fr, t1, inc=True)
            t1 = stt(y3[:, m, :], ps[:, 0:T], -1.0 / 64, y3[:, m, :], ALU.mult, ALU.add, t)
            bk.put(i, t1)
            t_sq[m] = act(kk3[:, m, :], y3[:, m, :], ACT.Square, t1)
            i, ps, tb = head_bcast(hr[0:16, :], m, T, t_bs)
            t2 = tt(V, v3_[:, m, :], v3_[:, m, :], ps, ALU.mult, tb, t_v)
            bk.put(i, t2)
            t2 = act(v3_[:, m, :], v3_[:, m, :], ACT.Identity, t2, bias=pc(f"ln_b{j}", m))
            tt(G, v3_[:, m, :], v3_[:, m, :], gate3[:, m, :], ALU.mult, t2, t_gate[m])
            t_yg[m] = tt(G, y3[:, m, :], y3[:, m, :], gate3[:, m, :], ALU.mult, t1, t_sq[m])

        t_sq, t_yg = [None] * 8, [None] * 8
        bk.use(range(2, 8))
        mems = [memory(0), memory(1)]
        waiting = list(range(8))
        frees = [now(), now()]
        slots = [None, None]
        starts = [0, 12]
        while waiting or any(slots):
            starts[1] -= 1
            for n in range(2):
                if slots[n] is None and waiting and starts[n] <= 0:
                    slots[n] = tile(waiting.pop(0), n, mems[n], frees[n])
                if slots[n] is not None and next(slots[n], "end") == "end":
                    slots[n] = None
        bk.use(range(8))

        w = Products((7, 6, 5, 4, 3), now(), (D, D, lambda I, n0, n1: np.asarray(I["rw_w_o_2"])[j][:, n0:n1]), ahead=4)
        i, ps, t = head_rows(kk3, 8, T, t_sq)
        t0 = ts(V, nv[0:16, :], ps, 1.0 / 64, 64e-5, ALU.mult, ALU.add, t, V.last)
        bk.put(i, t0)
        t = rsqrt_of(hr[0:16, :], nv[0:16, :], nm[0:16, :], nt[0:16, :])
        t_o = []
        for k in range(9):
            if k < 8:
                i, ps, tb = head_bcast(hr[0:16, :], k, T, t)
                tl = stt(y3[:, k, :], y3[:, k, :], pc(f"ln_w{j}", k), ps, ALU.mult, ALU.mult, tb, t_yg[k])
                bk.put(i, tl)
                tl = tt(G, y3[:, k, :], y3[:, k, :], v3_[:, k, :], ALU.add, tl)
                t_o.append(act(Hh[:, k, :], y3[:, k, :], ACT.Copy, tl, w.ph))
            if k:
                t_o[k - 1] = tt(V, Hl[:, k - 1, :], y3[:, k - 1, :], Hh[:, k - 1, :], ALU.subtract, t_o[k - 1])
        state["x"] = w.lin(in_hx, t_o, gated_residual(l, 1))

    phases = [nsa, lambda: moe(0), lambda: ple(0), moba, lambda: moe(1), lambda: ple(1)]

    def make(l, mixer):
        return [lambda: ffn(l, 0, 0), mixer, lambda: ffn(l, 2, 1)]

    phases += make(0, lambda: rwkv(0, 0)) + make(1, lambda: mamba(1)) + make(2, lambda: swa(2)) + make(3, lambda: rwkv(3, 1))
    for n, phase in enumerate(phases):
        if stop is not None and n not in stop:
            continue
        phase()

    d_x = nc.dram_tensor("xT_in", [128, 2048], F32, kind="ExternalInput").ap()
    d_p = nc.dram_tensor("params", [128, L.cols], F32, kind="ExternalInput").ap()
    d_c = nc.dram_tensor("consts", [128, NC], F32, kind="ExternalInput").ap()
    d_w = nc.dram_tensor("weights", [L.size], F32, kind="ExternalInput").ap()
    d_o = nc.dram_tensor("xT_out", [128, 2048], F32, kind="ExternalOutput").ap()

    def start(e):
        e.dma_start(xT[:, :], d_x).then_inc(s_in, 16)
        e.dma_start(prm[:, :], d_p).then_inc(s_in, 16)
        return e.dma_start(cst[:, :], d_c).then_inc(s_in, 16)

    SP(start, inc=False)
    for off, rows, cols, dst, sm_, fr in loads:
        src = d_w[off:off + rows * cols].rearrange("(p n) -> p n", p=rows)
        SP(lambda e, dst=dst, src=src, sm_=sm_: e.dma_start(dst, src).then_inc(sm_, 16), fr, inc=False)
    SP(lambda e: e.dma_start(d_o, xT[:, :]).then_inc(s_out, 16), state["x"], inc=False)

    with ctx, nc.Block() as block:
        @block.sync
        def _(e):
            SP.emit(e)
            e.wait_ge(s_out, 16)

        @block.tensor
        def _(e):
            e.wait_ge(s_in, 48)
            PE.emit(e)

        @block.vector
        def _(e):
            e.wait_ge(s_in, 48)
            V.emit(e)

        @block.scalar
        def _(e):
            e.wait_ge(s_in, 48)
            A.emit(e)

        @block.gpsimd
        def _(e):
            e.wait_ge(s_in, 48)
            G.emit(e)

    return L, consts


STOP = None


def kernel(**inputs):
    import concourse.bacc as bacc
    from concourse.bass_utils import run_bass_kernel_spmd as run

    nc = bacc.Bacc("TRN2", target_bir_lowering=False, num_devices=1)
    L, consts = build_program(nc, STOP)
    inputs = {k: np.asarray(v) for k, v in inputs.items()}
    small, flat = L.fill(inputs)
    maps = {"xT_in": np.ascontiguousarray(ktiles(inputs["x"][0].T)), "params": small, "consts": consts, "weights": flat}
    r = run(nc, [maps], core_ids=[0])
    o = np.asarray(r.results[0]["xT_out"])
    return np.ascontiguousarray(o.reshape(128, 8, 256).transpose(2, 1, 0).reshape(1, 256, 1024))
```
